# Optimizing a Trainium2 kernel written in Bass

```python
import math
import jax
import jax.numpy as jnp
from jax import lax
import numpy as np

D_MODEL = 1024
BATCH = 1
SEQ = 128
DEPTH = 2
DEC_BATCH = 1
DEC_SEQ = 128
PAST_LEN = 128

GRID_W = 64
N_EVEN = (DEPTH + 1) // 2
N_ODD = DEPTH // 2

HEAD_DIM = 64
NAT_HEADS = 8
NAT_WIN_H = 8
NAT_WIN_W = 16
DIFF_HEADS = 4
NAT_WIDTH = NAT_HEADS * HEAD_DIM
DIFF_WIDTH = DIFF_HEADS * 2 * HEAD_DIM
EVEN_IN = 3 * NAT_WIDTH + 3 * DIFF_WIDTH
EVEN_OUT = NAT_WIDTH + DIFF_WIDTH
ROPE_THETA = 10000.0
Q_BLOCK = 128

DN_HEADS = 8
DN_DK = 128
DN_DV = 128
DN_QK_WIDTH = DN_HEADS * DN_DK
DN_WIDTH = DN_HEADS * DN_DV
DN_CONV_CH = 2 * DN_QK_WIDTH + DN_WIDTH
DN_CONV = 3
DN_CHUNK = 64
ODD_IN = DN_CONV_CH + 4 * DN_HEADS + DN_WIDTH

N_EXPERTS = 16
N_GROUPS = 4
EXPERTS_PER_GROUP = N_EXPERTS // N_GROUPS
TOP_K = 2
EXPERT_FF = 512

ALPHA = (2 * DEPTH) ** 0.25
BETA = (8 * DEPTH) ** -0.25
EPS = 1e-5

kernel_name = 'nat_diffattn_deltanet_moe_diffusion_step'

F32 = jnp.float32

def layer_norm(x, g, b):
    xf = x.astype(F32)
    xc = xf - xf.mean(-1, keepdims=True)
    var = (xc * xc).mean(-1, keepdims=True)
    return (xc * lax.rsqrt(var + EPS) * g + b).astype(x.dtype)

def rms_norm(x, g):
    xf = x.astype(F32)
    return (xf * lax.rsqrt((xf * xf).mean(-1, keepdims=True) + EPS) * g).astype(x.dtype)

def l2_normalize(x):
    return x * lax.rsqrt((x * x).sum(-1, keepdims=True) + 1e-6)

def ada_modulation(cond, w, b):
    mod = jax.nn.silu(cond) @ w + b
    mod = mod.reshape(mod.shape[:-1] + (6, D_MODEL))
    return [mod[..., j, :][..., None, :] for j in range(6)]

def modulate(x, shift, scale):
    return x * (1 + scale) + shift

def axial_rope(x):
    length, dh = x.shape[1], x.shape[-1]
    nf = dh // 4
    t = jnp.arange(length)
    inv = ROPE_THETA ** (-jnp.arange(nf, dtype=F32) / nf)
    ang_r = (t // GRID_W).astype(F32)[:, None] * inv
    ang_c = (t % GRID_W).astype(F32)[:, None] * inv
    bshape = (length,) + (1,) * (x.ndim - 3) + (nf,)
    cr = jnp.cos(ang_r).reshape(bshape).astype(x.dtype)
    sr = jnp.sin(ang_r).reshape(bshape).astype(x.dtype)
    cc = jnp.cos(ang_c).reshape(bshape).astype(x.dtype)
    sc = jnp.sin(ang_c).reshape(bshape).astype(x.dtype)
    x1, x2, x3, x4 = jnp.split(x, 4, axis=-1)
    return jnp.concatenate([x1 * cr - x2 * sr, x2 * cr + x1 * sr,
                            x3 * cc - x4 * sc, x4 * cc + x3 * sc], axis=-1)

def sweep_query_blocks(fn, q):
    b, length = q.shape[:2]
    nb = length // Q_BLOCK
    qb = jnp.moveaxis(q.reshape((b, nb, Q_BLOCK) + q.shape[2:]), 1, 0)
    out = lax.map(fn, qb)
    return jnp.moveaxis(out, 0, 1).reshape((b, length) + out.shape[3:])

def softmax_attend(q, k, v):
    scale = q.shape[-1] ** -0.5

    def block(qb):
        s = jnp.einsum('bqhd,bkhd->bhqk', qb, k).astype(F32) * scale
        p = jax.nn.softmax(s, axis=-1).astype(v.dtype)
        return jnp.einsum('bhqk,bkhd->bqhd', p, v)

    return sweep_query_blocks(block, q)

def diff_attend(q, k, v, lam):
    scale = q.shape[-1] ** -0.5

    def block(qb):
        s = jnp.einsum('bqhjd,bkhjd->bhjqk', qb, k).astype(F32) * scale
        p = jax.nn.softmax(s, axis=-1)
        p = (p[:, :, 0] - lam * p[:, :, 1]).astype(v.dtype)
        return jnp.einsum('bhqk,bkhe->bqhe', p, v)

    return sweep_query_blocks(block, q)

def diff_lambda(lam_p, layer):
    lam_init = 0.8 - 0.6 * math.exp(-0.3 * layer)
    lp = lam_p.astype(F32)
    lam = jnp.exp(jnp.sum(lp[0] * lp[1])) - jnp.exp(jnp.sum(lp[2] * lp[3])) + lam_init
    return lam, lam_init

def nat_latent(q, k, v, ctx_k, ctx_v, rel_bias):
    b, length, heads, dh = q.shape
    rows = length // GRID_W
    kh = min(NAT_WIN_H, rows)
    kw = NAT_WIN_W
    scale = dh ** -0.5
    qg = q.reshape(b, rows, GRID_W, heads, dh)
    kg = k.reshape(b, rows, GRID_W, heads, dh)
    vg = v.reshape(b, rows, GRID_W, heads, dh)
    col = jnp.arange(GRID_W)
    col_start = jnp.clip(col - kw // 2, 0, GRID_W - kw)
    col_ok = (col[None, :] >= col_start[:, None]) & (col[None, :] < col_start[:, None] + kw)
    dc = jnp.clip(col[None, :] - col[:, None], 1 - kw, kw - 1) + (NAT_WIN_W - 1)

    def row_block(r):
        start = jnp.clip(r - kh // 2, 0, rows - kh)
        qr = lax.dynamic_index_in_dim(qg, r, axis=1, keepdims=False)
        kr = lax.dynamic_slice_in_dim(kg, start, kh, axis=1)
        vr = lax.dynamic_slice_in_dim(vg, start, kh, axis=1)
        dr = start + jnp.arange(kh) - r + (NAT_WIN_H - 1)
        bias = rel_bias[:, dr[:, None, None], dc[None, :, :]].astype(F32)
        s_loc = (jnp.einsum('bqhd,bawhd->bhqaw', qr, kr).astype(F32) * scale
                 + jnp.transpose(bias, (0, 2, 1, 3))[None])
        s_loc = jnp.where(col_ok[:, None, :], s_loc, -jnp.inf).reshape(b, heads, GRID_W, kh * GRID_W)
        s_ctx = jnp.einsum('bqhd,bkhd->bhqk', qr, ctx_k).astype(F32) * scale
        p = jax.nn.softmax(jnp.concatenate([s_loc, s_ctx], axis=-1), axis=-1).astype(v.dtype)
        p_loc = p[..., :kh * GRID_W].reshape(b, heads, GRID_W, kh, GRID_W)
        p_ctx = p[..., kh * GRID_W:]
        return (jnp.einsum('bhqaw,bawhd->bqhd', p_loc, vr)
                + jnp.einsum('bhqk,bkhd->bqhd', p_ctx, ctx_v))

    out = lax.map(row_block, jnp.arange(rows))
    return jnp.moveaxis(out, 0, 1).reshape(b, length, heads, dh)

def even_project(h, w_in):
    b, length, _ = h.shape
    splits = [NAT_WIDTH, 2 * NAT_WIDTH, 3 * NAT_WIDTH,
              3 * NAT_WIDTH + DIFF_WIDTH, 3 * NAT_WIDTH + 2 * DIFF_WIDTH]
    nq, nk, nv, dq, dk, dv = jnp.split(h @ w_in, splits, axis=-1)
    nat = tuple(t.reshape(b, length, NAT_HEADS, HEAD_DIM) for t in (nq, nk, nv))
    dq = dq.reshape(b, length, DIFF_HEADS, 2, HEAD_DIM)
    dk = dk.reshape(b, length, DIFF_HEADS, 2, HEAD_DIM)
    dv = dv.reshape(b, length, DIFF_HEADS, 2 * HEAD_DIM)
    return nat, (dq, dk, dv)

def even_merge(nat_o, diff_o, subln_g, lam_init, w_out):
    b, length = nat_o.shape[:2]
    diff_o = rms_norm(diff_o, subln_g) * (1.0 - lam_init)
    o = jnp.concatenate([nat_o.reshape(b, length, NAT_WIDTH),
                         diff_o.reshape(b, length, DIFF_WIDTH)], axis=-1)
    return o @ w_out

def even_mixer_context(h, w_in, w_out, lam_p, subln_g, layer):
    (nq, nk, nv), (dq, dk, dv) = even_project(h, w_in)
    nat_o = softmax_attend(nq, nk, nv)
    lam, lam_init = diff_lambda(lam_p, layer)
    diff_o = diff_attend(dq, dk, dv, lam)
    return even_merge(nat_o, diff_o, subln_g, lam_init, w_out), (nk, nv, dk, dv)

def even_mixer_latent(h, w_in, w_out, lam_p, subln_g, rel_bias, ck_nat, cv_nat, ck_diff, cv_diff, layer):
    (nq, nk, nv), (dq, dk, dv) = even_project(h, w_in)
    nat_o = nat_latent(nq, nk, nv, ck_nat, cv_nat, rel_bias)
    lam, lam_init = diff_lambda(lam_p, layer)
    dq, dk = axial_rope(dq), axial_rope(dk)
    diff_o = diff_attend(dq, jnp.concatenate([ck_diff, dk], axis=1),
                         jnp.concatenate([cv_diff, dv], axis=1), lam)
    return even_merge(nat_o, diff_o, subln_g, lam_init, w_out)

def short_conv(x, w):
    length = x.shape[1]
    left = DN_CONV // 2
    xp = jnp.pad(x, ((0, 0), (left, DN_CONV - 1 - left), (0, 0)))
    return sum(xp[:, j:j + length] * w[j] for j in range(DN_CONV))

def gated_delta_chunked(q, k, v, g, beta, s0):
    b, length, heads, _ = q.shape
    dv = v.shape[-1]
    n = length // DN_CHUNK

    def chunks(t):
        t = jnp.moveaxis(t, 2, 1)
        return t.reshape((b, heads, n, DN_CHUNK) + t.shape[3:])

    q, k, v, g, beta = (chunks(t) for t in (q, k, v, g, beta))
    gc = jnp.cumsum(g, axis=-1)
    kb = k * beta[..., None]
    vb = v * beta[..., None]
    tri = jnp.tril(jnp.ones((DN_CHUNK, DN_CHUNK), dtype=bool))
    strict = jnp.tril(jnp.ones((DN_CHUNK, DN_CHUNK), dtype=bool), -1)
    decay = jnp.exp(jnp.where(tri, gc[..., :, None] - gc[..., None, :], -jnp.inf))
    lower = jnp.where(strict, jnp.einsum('bhncd,bhnsd->bhncs', kb, k) * decay, 0.0)
    eye = jnp.eye(DN_CHUNK, dtype=F32)
    t_inv = lax.linalg.triangular_solve(lower + eye, jnp.broadcast_to(eye, lower.shape),
                                        left_side=True, lower=True)
    u = t_inv @ vb
    w = t_inv @ (kb * jnp.exp(gc)[..., None])
    a_qk = jnp.einsum('bhncd,bhnsd->bhncs', q, k) * decay

    def step(s, xs):
        qi, ki, ui, wi, gi, ai = xs
        v_new = ui - jnp.einsum('bhck,bhkv->bhcv', wi, s)
        o = (jnp.einsum('bhck,bhkv->bhcv', qi * jnp.exp(gi)[..., None], s)
             + jnp.einsum('bhcs,bhsv->bhcv', ai, v_new))
        g_last = gi[..., -1]
        s = (s * jnp.exp(g_last)[..., None, None]
             + jnp.einsum('bhck,bhcv->bhkv', ki * jnp.exp(g_last[..., None] - gi)[..., None], v_new))
        return s, o

    xs = tuple(jnp.moveaxis(t, 2, 0) for t in (q, k, u, w, gc, a_qk))
    s_final, o = lax.scan(step, s0, xs)
    o = jnp.moveaxis(o, 0, 2).reshape(b, heads, length, dv)
    return jnp.moveaxis(o, 1, 2), s_final

def deltanet_mixer(h, w_in, conv_w, a_log, dt_bias, onorm_g, w_out, s0):
    b, length, _ = h.shape
    z = h @ w_in
    qkv, ab, gate = jnp.split(z, [DN_CONV_CH, DN_CONV_CH + 4 * DN_HEADS], axis=-1)
    qkv = jax.nn.silu(short_conv(qkv, conv_w)).astype(F32)
    q, k, v = jnp.split(qkv, [DN_QK_WIDTH, 2 * DN_QK_WIDTH], axis=-1)
    q = l2_normalize(q.reshape(b, length, DN_HEADS, DN_DK)) * (DN_DK ** -0.5)
    k = l2_normalize(k.reshape(b, length, DN_HEADS, DN_DK))
    v = v.reshape(b, length, DN_HEADS, DN_DV)
    ab = ab.astype(F32).reshape(b, length, 2, 2, DN_HEADS)
    g = -jnp.exp(a_log.astype(F32)) * jax.nn.softplus(ab[:, :, 0] + dt_bias.astype(F32))
    beta = jax.nn.sigmoid(ab[:, :, 1])
    s0 = s0.astype(F32)
    o_f, s_f = gated_delta_chunked(q, k, v, g[:, :, 0], beta[:, :, 0], s0[:, 0])
    flip = lambda t: t[:, ::-1]
    o_b, s_b = gated_delta_chunked(flip(q), flip(k), flip(v), flip(g[:, :, 1]), flip(beta[:, :, 1]), s0[:, 1])
    o = o_f + flip(o_b)
    o = rms_norm(o, onorm_g) * jax.nn.silu(gate.astype(F32).reshape(b, length, DN_HEADS, DN_DV))
    out = o.reshape(b, length, DN_WIDTH).astype(h.dtype) @ w_out
    return out, jnp.stack([s_f, s_b], axis=1)

def moe_ffn(h, router_w, router_b, wg, wu, wd):
    b, length, d = h.shape
    x = h.reshape(b * length, d)
    scores = jax.nn.sigmoid((x @ router_w).astype(F32))
    biased = scores + router_b.astype(F32)
    group_score = lax.top_k(biased.reshape(-1, N_GROUPS, EXPERTS_PER_GROUP), TOP_K)[0].sum(-1)
    group_sel = jnp.argmax(group_score, axis=-1)
    in_group = (jnp.arange(N_EXPERTS) // EXPERTS_PER_GROUP)[None, :] == group_sel[:, None]
    _, idx = lax.top_k(jnp.where(in_group, biased, -jnp.inf), TOP_K)
    wts = jnp.take_along_axis(scores, idx, axis=-1)
    wts = wts / wts.sum(-1, keepdims=True)
    gates = jnp.einsum('tk,tke->te', wts, jax.nn.one_hot(idx, N_EXPERTS, dtype=F32)).astype(h.dtype)
    y = jnp.zeros_like(x)
    for e in range(N_EXPERTS):
        he = jax.nn.silu(x @ wg[e]) * (x @ wu[e])
        y = y + gates[:, e:e + 1] * (he @ wd[e])
    return y.reshape(b, length, d)

def setup_inputs(seed: int = 0) -> dict:
    key = jax.random.key(seed)
    ks = jax.random.split(key, 32)
    d = D_MODEL

    def nrm(k, shape, scale):
        return jax.random.normal(k, shape, F32) * scale

    dt = jnp.exp(jax.random.uniform(ks[17], (N_ODD, 2, DN_HEADS), F32, math.log(1e-3), math.log(1e-1)))
    return {
        'x_prompt': nrm(ks[0], (BATCH, SEQ, d), 1.0),
        'x_sample': nrm(ks[1], (DEC_BATCH, DEC_SEQ, d), 1.0),
        'cache_nat_k': nrm(ks[2], (DEC_BATCH, N_EVEN, PAST_LEN, NAT_HEADS, HEAD_DIM), 1.0),
        'cache_nat_v': nrm(ks[3], (DEC_BATCH, N_EVEN, PAST_LEN, NAT_HEADS, HEAD_DIM), 1.0),
        'cache_diff_k': nrm(ks[4], (DEC_BATCH, N_EVEN, PAST_LEN, DIFF_HEADS, 2, HEAD_DIM), 1.0),
        'cache_diff_v': nrm(ks[5], (DEC_BATCH, N_EVEN, PAST_LEN, DIFF_HEADS, 2 * HEAD_DIM), 1.0),
        'state_delta': nrm(ks[6], (DEC_BATCH, N_ODD, 2, DN_HEADS, DN_DK, DN_DV), 0.2),
        'c': nrm(ks[7], (DEC_BATCH, d), 1.0),
        'c_ctx': nrm(ks[8], (d,), 1.0),
        'w_in_even': nrm(ks[9], (N_EVEN, d, EVEN_IN), d ** -0.5),
        'w_out_even': nrm(ks[10], (N_EVEN, EVEN_OUT, d), EVEN_OUT ** -0.5 * BETA),
        'nat_bias': nrm(ks[11], (N_EVEN, NAT_HEADS, 2 * NAT_WIN_H - 1, 2 * NAT_WIN_W - 1), 0.1),
        'diff_lam': nrm(ks[12], (N_EVEN, 4, HEAD_DIM), 0.1),
        'diff_subln': 1.0 + nrm(ks[13], (N_EVEN, 2 * HEAD_DIM), 0.01),
        'w_in_odd': nrm(ks[14], (N_ODD, d, ODD_IN), d ** -0.5),
        'conv_odd': nrm(ks[15], (N_ODD, DN_CONV, DN_CONV_CH), DN_CONV ** -0.5),
        'a_log_odd': jnp.log(jax.random.uniform(ks[16], (N_ODD, 2, DN_HEADS), F32, 1.0, 16.0)),
        'dt_bias_odd': dt + jnp.log(-jnp.expm1(-dt)),
        'onorm_odd': 1.0 + nrm(ks[18], (N_ODD, DN_DV), 0.01),
        'w_out_odd': nrm(ks[19], (N_ODD, DN_WIDTH, d), DN_WIDTH ** -0.5 * BETA),
        'ada_w': nrm(ks[20], (DEPTH, d, 6 * d), 0.5 * d ** -0.5),
        'ada_b': nrm(ks[21], (DEPTH, 6 * d), 0.02),
        'ln_g': 1.0 + nrm(ks[22], (DEPTH, 2, d), 0.01),
        'ln_b': nrm(ks[23], (DEPTH, 2, d), 0.01),
        'router_w': nrm(ks[24], (d, N_EXPERTS), d ** -0.5),
        'router_b': nrm(ks[25], (N_EXPERTS,), 0.01),
        'moe_wg': nrm(ks[26], (DEPTH, N_EXPERTS, d, EXPERT_FF), d ** -0.5),
        'moe_wu': nrm(ks[27], (DEPTH, N_EXPERTS, d, EXPERT_FF), d ** -0.5),
        'moe_wd': nrm(ks[28], (DEPTH, N_EXPERTS, EXPERT_FF, d), EXPERT_FF ** -0.5 * BETA),
    }

def reference(x_prompt, x_sample, cache_nat_k, cache_nat_v, cache_diff_k, cache_diff_v, state_delta,
              c, c_ctx, w_in_even, w_out_even, nat_bias, diff_lam, diff_subln,
              w_in_odd, conv_odd, a_log_odd, dt_bias_odd, onorm_odd, w_out_odd,
              ada_w, ada_b, ln_g, ln_b, router_w, router_b, moe_wg, moe_wu, moe_wd):
    xp, xs = x_prompt, x_sample
    nat_k_list, nat_v_list, diff_k_list, diff_v_list, delta_list = [], [], [], [], []
    for layer in range(DEPTH):
        mp = ada_modulation(c_ctx, ada_w[layer], ada_b[layer])
        ms = ada_modulation(c, ada_w[layer], ada_b[layer])
        hp = modulate(xp, mp[0], mp[1])
        hs = modulate(xs, ms[0], ms[1])
        i = layer // 2
        if layer % 2 == 0:
            op, (nk, nv, dk, dv) = even_mixer_context(hp, w_in_even[i], w_out_even[i], diff_lam[i],
                                                      diff_subln[i], layer)
            os_ = even_mixer_latent(hs, w_in_even[i], w_out_even[i], diff_lam[i], diff_subln[i], nat_bias[i],
                                    cache_nat_k[:, i], cache_nat_v[:, i], cache_diff_k[:, i], cache_diff_v[:, i],
                                    layer)
            nat_k_list.append(nk)
            nat_v_list.append(nv)
            diff_k_list.append(dk)
            diff_v_list.append(dv)
        else:
            s_zero = jnp.zeros((xp.shape[0], 2, DN_HEADS, DN_DK, DN_DV), F32)
            op, st = deltanet_mixer(hp, w_in_odd[i], conv_odd[i], a_log_odd[i], dt_bias_odd[i],
                                    onorm_odd[i], w_out_odd[i], s_zero)
            os_, _ = deltanet_mixer(hs, w_in_odd[i], conv_odd[i], a_log_odd[i], dt_bias_odd[i],
                                    onorm_odd[i], w_out_odd[i], state_delta[:, i])
            delta_list.append(st)
        xp = layer_norm(ALPHA * xp + mp[2] * op, ln_g[layer, 0], ln_b[layer, 0])
        xs = layer_norm(ALPHA * xs + ms[2] * os_, ln_g[layer, 0], ln_b[layer, 0])
        hp = modulate(xp, mp[3], mp[4])
        hs = modulate(xs, ms[3], ms[4])
        fp = moe_ffn(hp, router_w, router_b, moe_wg[layer], moe_wu[layer], moe_wd[layer])
        fs = moe_ffn(hs, router_w, router_b, moe_wg[layer], moe_wu[layer], moe_wd[layer])
        xp = layer_norm(ALPHA * xp + mp[5] * fp, ln_g[layer, 1], ln_b[layer, 1])
        xs = layer_norm(ALPHA * xs + ms[5] * fs, ln_g[layer, 1], ln_b[layer, 1])
    y_prompt = xp
    y_sample = xs
    new_nat_k = jnp.stack(nat_k_list, axis=1)
    new_nat_v = jnp.stack(nat_v_list, axis=1)
    new_diff_k = jnp.stack(diff_k_list, axis=1)
    new_diff_v = jnp.stack(diff_v_list, axis=1)
    new_state_delta = jnp.stack(delta_list, axis=1)
    return (y_prompt, y_sample, new_nat_k, new_nat_v, new_diff_k, new_diff_v, new_state_delta)


_drawn_inputs = setup_inputs


def setup_inputs(seed=0):
    import zlib

    import numpy as np

    out = dict(_drawn_inputs(seed))
    spreads = {}
    factors = {'cache_nat_k': 5.562,
     'cache_nat_v': 4.335,
     'state_delta': 2.871,
     'nat_bias': 64.0,
     'diff_lam': 8.0,
     'diff_subln': 64.0,
     'onorm_odd': 64.0}
    for name, (base, spread) in spreads.items():
        noise = np.random.default_rng([zlib.crc32(name.encode()), seed]).standard_normal(out[name].shape)
        drawn = base * np.exp(spread * noise) if base else spread * noise
        out[name] = jnp.asarray(drawn.astype(out[name].dtype))
    for name, factor in factors.items():
        out[name] = (out[name] * factor).astype(out[name].dtype)
    return out
```

```python
from contextlib import ExitStack
import math

import concourse.bass as bass
from concourse import mybir

P = 128
D = 1024
KC = D // P
T = 256
SLOT = 4096
RING = 6
DEPTH = 2
N_EXP = 16
FF = 512
FC = FF // P
HEADS = 8
ADA0, EIN0, EOUT0, MOE0, OIN0, OOUT0, MOE1, N_SLOTS = 0, 24, 30, 32, 80, 88, 90, 138
ALPHA = (2 * DEPTH) ** 0.25
EPS = 1e-5
LEVELS = 7
BIG = 1e30

F32 = mybir.dt.float32
ALU = mybir.AluOpType
ACT = mybir.ActivationFunctionType
AX = mybir.AxisListType.X

CONST_W = {}
_at = 0
for _n, _w in (("ident", 128), ("mean", 128), ("le", 128), ("gt", 128), ("ge", 128), ("lt", 128),
               ("level", 2 * LEVELS * 128), ("rope_c", 64), ("rope_s", 64), ("window", 128),
               ("rank4", 4), ("rank16", 16)):
    CONST_W[_n] = (_at, _at + _w)
    _at += _w
N_CONST = _at
PARAM_W = {}
_at = 0
for _n, _w in (("cond", KC * 2), ("ada_b", 192), ("ln_g", 4 * 16), ("ln_b", 4 * 16), ("router", KC * 16),
               ("router_b", 16), ("subln", 1), ("onorm", 1), ("conv", 24 * 3), ("a_log", 16),
               ("dt_bias", 16), ("w_ab", KC * 32)):
    PARAM_W[_n] = (_at, _at + _w)
    _at += _w
N_PARAM = _at


def build_program(nc, slots, x_t, consts, params, nat_kc, nat_vc, diff_kc, diff_vc, nat_bias, lam_in, state0,
                  y_out, nk_out, nv_out, dk_out, dv_out, st_out):
    ctx = ExitStack()
    with ctx:
        def sb(name, shape):
            return ctx.enter_context(nc.sbuf_tensor(name, shape, F32))

        ring = sb("ring", [P, RING, SLOT])
        res = sb("res", [P, KC, T])
        act_t = sb("act_t", [P, KC, T])
        cst = sb("cst", [P, N_CONST])
        par = sb("par", [P, N_PARAM])
        mod = sb("mod", [P, 192])
        small = sb("small", [P, 1176])
        arena = sb("arena", [P, 17408])

        bank = [ctx.enter_context(nc.psum_tensor(f"bank{i}", [P, 512], F32)) for i in range(8)]

        def c_(name):
            a, b = CONST_W[name]
            return cst[:, a:b]

        def p_(name):
            a, b = PARAM_W[name]
            return par[:, a:b]

        ident = c_("ident")
        sems = {}

        def S(name):
            if name not in sems:
                sems[name] = ctx.enter_context(nc.semaphore(name))
            return sems[name]

        slot_full = [S(f"slot_full{k}") for k in range(RING)]
        slot_free = [S(f"slot_free{k}") for k in range(RING)]

        mod_v = mod[:, :].rearrange("p (l j c s) -> p l j c s", l=DEPTH, j=6, c=KC)

        def gate_col(l, j, c, s):
            i = ((l * 6 + j) * KC + c) * 2 + s
            return mod[:, i:i + 1]

        s_at = [0]

        def take(n):
            s_at[0] += n
            assert s_at[0] <= 1176
            return small[:, s_at[0] - n:s_at[0]]

        cond_t = take(16)
        mod_g = take(64)
        mod_b = take(64)
        lam_w = take(8)
        sub_g = take(1)
        mx = take(32)
        sums = take(32)
        rsum = take(32)
        nlr = take(32)
        rms = take(24)
        scores = take(32)
        biased = take(32)
        r_a = take(32)
        r_b = take(32)
        r_c = take(32)
        masked = take(32)
        oh1 = take(32)
        oh2 = take(32)
        gates = take(32)
        g8a = take(16)
        g8b = take(16)
        g8c = take(16)
        g2 = take(8)
        w2 = take(8)
        sp_x = take(32)
        sp_a = take(32)
        sp_b = take(32)
        g_tok = take(32)
        beta = take(32)
        egc = take(32)
        kdec = take(32)
        negA = take(16)
        qk_ss = take(32)
        o_ss = take(16)
        ab_raw = take(64)

        ln_scaled = take(128)
        nbeta = take(32)
        rstd = arena[:, 0:T]
        o_d = sb("o_delta", [P, 2, 1024])

        a_at = [0]

        def ar(n, reset=False):
            if reset:
                a_at[0] = 0
            a_at[0] += n
            assert a_at[0] <= 17408, a_at[0]
            return arena[:, a_at[0] - n:a_at[0]]

        qkv = ar(6144, True).rearrange("p (s n) -> p s n", s=2)
        heads_t = ar(4096).rearrange("p (w s c n) -> p w s c n", w=4, s=2, c=4)
        nkc = ar(512).rearrange("p (c n) -> p c n", c=4)
        nvc = ar(512)
        dkc = ar(512).rearrange("p (c n) -> p c n", c=4)
        dvc = ar(512)
        bias = ar(1024).rearrange("p (h n) -> p h n", h=8)
        probs = ar(1024).rearrange("p (b j n) -> p b j n", b=2, j=2)
        probs_t = ar(1024).rearrange("p (b j n) -> p b j n", b=2, j=2)
        o_tok = ar(2048).rearrange("p (s n) -> p s n", s=2)
        lam_p = o_tok[:, 0, 0:256]
        rope_1 = probs.rearrange("p b j n -> p (b j n)")[:, 0:512]
        rope_2 = probs.rearrange("p b j n -> p (b j n)")[:, 512:1024]
        o_sq = qkv[:, 0, 0:1024]

        yacc = ar(2048, True).rearrange("p (c n) -> p c n", c=KC)
        gate_bc = ar(4096).rearrange("p (e n) -> p e n", e=N_EXP)
        silu_b = ar(1024).rearrange("p (h f n) -> p h f n", h=2, f=2)
        he = ar(2048).rearrange("p (b f n) -> p b f n", b=2, f=FC)
        y_tok = arena[:, 0:2048].rearrange("p (s n) -> p s n", s=2)

        dqkv = ar(6144, True).rearrange("p (s n) -> p s n", s=2)
        dgate = ar(2048).rearrange("p (s n) -> p s n", s=2)
        qk_t = ar(4096).rearrange("p (w s h n) -> p w s h n", w=2, s=2, h=HEADS)
        work_at = a_at[0]
        zpad = ar(3 * 260).rearrange("p (b s n) -> p b s n", b=3, s=2)
        conv_o = ar(3 * 256).rearrange("p (b s n) -> p b s n", b=3, s=2)
        a_at[0] = work_at
        dsq = ar(2048)
        a_at[0] = work_at
        sets = []
        for _ in range(2):
            sets.append({n: None for n in ("X", "XT", "LT", "LM", "Y", "AT", "DT")})
        for n in ("X", "XT", "LT", "LM", "Y"):
            for w in sets:
                w[n] = ar(512).rearrange("p (h n) -> p h n", h=4)
        free_q = [dqkv[:, 0, 0:1024], dqkv[:, 1, 0:1024]]
        for w, f in zip(sets, free_q):
            w["AT"] = f[:, 0:512].rearrange("p (h n) -> p h n", h=4)
            w["DT"] = f[:, 512:1024].rearrange("p (h n) -> p h n", h=4)
        st_stage = dqkv[:, 1, 1024:2048].rearrange("p (b h n) -> p b h n", b=2, h=4)
        s0 = act_t[:, :, :].rearrange("p c n -> p (c n)").rearrange("p (d h n) -> p d h n", d=2, h=HEADS)

        def bcast(ap, n):
            return ap.unsqueeze(2).to_broadcast([ap.shape[0], ap.shape[1], n])

        block = ctx.enter_context(nc.Block())

        class Chain:

            def __init__(self, eng, name):
                self.eng, self.sem, self.n, self.off = eng, S(name), 0, None

            def link(self, ins):
                ins.then_inc(self.sem, 1)
                self.n += 1
                self.eng.wait_ge(self.sem, self.n if self.off is None else self.off + self.n)

            def enter(self, i, per):
                self.off = i * per
                self.mark = self.n
                self.per = per

            def leave(self, times):
                assert self.n - self.mark == self.per, self.n - self.mark
                self.off = None
                self.n = self.mark + times * self.per

        meet_n = {}

        def meet(eng, name):
            meet_n[name] = meet_n.get(name, 0) + 1
            eng.drain().then_inc(S("phase_done"), 1)
            eng.wait_ge(S("phase_done"), 4 * meet_n[name])

        def at_ring(n0, off=0):
            return (n0 + off) % RING, (n0 + off) // RING

        def wait_slot(eng, n0, off=0, turns=None):
            k, t = at_ring(n0, off)
            if turns is None:
                eng.wait_ge(slot_full[k], 16 * (t + 1))
            else:
                eng.wait_ge(slot_full[k], turns * 16 + 16 * (t + 1))
            return k

        def ln_pe(pe, site):
            for half, (name, src) in enumerate((("ln_mean", res), ("ln_var", act_t))):
                if half == 1:
                    pe.wait_ge(S("ln_sq"), site + 1)
                for c in range(KC):
                    last = pe.matmul(bank[6 + half][:, 0:T], c_("mean"), src[:, c, :], start=(c == 0), stop=(c == KC - 1))
                last.then_inc(S(name), 1)

        def ln_act(act, ch, site):
            act.wait_ge(S("ln_centred"), site + 1)
            act.activation(act_t[:, :, :], res[:, :, :], ACT.Square).then_inc(S("ln_sq"), 1)
            act.wait_ge(S("ln_eps"), site + 1)
            t = rstd[:, 0:T]
            ch.link(act.activation(t, t, ACT.Ln))
            act.activation(t, t, ACT.Exp, scale=-0.5).then_inc(S("ln_rstd"), 1)

        def ln_dve(dve, ch, site):
            dve.wait_ge(S("ln_mean"), site + 1)
            mean = bank[6][:, 0:T].unsqueeze(1).to_broadcast([P, KC, T])
            dve.tensor_tensor(res[:, :, :], res[:, :, :], mean, ALU.subtract).then_inc(S("ln_centred"), 1)
            dve.wait_ge(S("ln_var"), site + 1)
            t = rstd[:, 0:T]
            dve.tensor_scalar(t, bank[7][:, 0:T], EPS, None, ALU.add).then_inc(S("ln_eps"), 1)
            dve.wait_ge(S("ln_rstd"), site + 1)
            dve.wait_ge(S("ln_centred"), site + 1)
            dve.tensor_tensor(res[:, :, :], res[:, :, :], t.unsqueeze(1).to_broadcast([P, KC, T]),
                              ALU.mult).then_inc(S("ln_norm"), 1)
            if site < 3:
                dve.wait_ge(S("ln_norm"), site + 1)
                rv = res[:, :, :].rearrange("p c (s n) -> p (c s) n", s=2)
                av = act_t[:, :, :].rearrange("p c (s n) -> p (c s) n", s=2)
                gm = mod_g[:, site * 16:site * 16 + 16]
                bm = mod_b[:, site * 16:site * 16 + 16]
                ch.link(dve.tensor_tensor(av, rv, bcast(gm, P), ALU.mult))
                dve.tensor_tensor(av, av, bcast(bm, P), ALU.add).then_inc(S("ln_h"), 1)

        def ln_pool(pool, ch, site):
            pool.wait_ge(S("ln_norm"), site + 1)
            if site < 3:
                pool.wait_ge(S("ln_h"), site + 1)
            for c in range(KC):
                i = site * 16 + 2 * c
                last = pool.tensor_scalar(res[:, c, :], res[:, c, :], ln_scaled[:, 0 + i:i + 1],
                                          ln_scaled[:, 64 + i:65 + i], ALU.mult, ALU.add)
            ch.link(last)


        def moe_pool(pool, ch):
            pass

        def moe_pe(pe, layer, n0):
            L = layer
            for s in range(2):
                for c in range(KC):
                    last = pe.matmul(bank[0][:, s * 16:s * 16 + 16], act_t[:, c, s * P:(s + 1) * P],
                                     p_("router")[:, c * 16:c * 16 + 16], start=(c == 0), stop=(c == KC - 1))
            last.then_inc(S("logits"), 1)
            pe.wait_ge(S("gates_ready"), L + 1)
            for q in range(8):
                for j in range(2):
                    for s in range(2):
                        e = 2 * q + j
                        col = gates[:, s * 16 + e:s * 16 + e + 1]
                        last = pe.matmul(bank[q][:, j * T + s * P:j * T + (s + 1) * P], col.to_broadcast([P, P]), ident,
                                         start=True, stop=True)
                last.then_inc(S("gate_rows"), 1)
            pe.wait_ge(S("gate_copied"), 8 * (L + 1))

            def gate_up(i, e):
                ks = [wait_slot(pe, n0, 3 * e + m, i) for m in range(2)]
                for hf in range(2):
                    val = 4 * i + 2 * e + hf + 1 if i is not None else 2 * e + hf + 1
                    pe.wait_ge(S("gu_free"), val + 34 * L)
                    for m in range(2):
                        w = ring[:, ks[m], :].rearrange("p (c n) -> p c n", c=KC)
                        for f in range(2):
                            fc = 2 * hf + f
                            for c in range(KC):
                                last = pe.matmul(bank[2 * m + hf][:, f * T:(f + 1) * T], w[:, c, fc * P:(fc + 1) * P],
                                                 act_t[:, c, :], start=(c == 0), stop=(c == KC - 1))
                    last.then_inc(S("gu_done"), 1)

            def down(i, e):
                k = wait_slot(pe, n0, 3 * e + 2, i)
                w = ring[:, k, :].rearrange("p (f n) -> p f n", f=FC)
                pe.wait_ge(S("he_ready"), (4 * i + 2 * e + 2 if i is not None else 2 * e + 2) + 32 * L)
                for b in range(4):
                    pe.wait_ge(S("y_free"), (8 * i + 4 * e + b + 1 if i is not None else 4 * e + b + 1) + 68 * L)
                    for o in range(2):
                        oc = 2 * b + o
                        for f in range(FC):
                            last = pe.matmul(bank[4 + b][:, o * T:(o + 1) * T], w[:, f, oc * P:(oc + 1) * P],
                                             he[:, e % 2, f, :], start=(f == 0), stop=(f == FC - 1))
                    last.then_inc(S("y_done"), 1)

            gate_up(None, 0)
            with pe.Fori(0, 7) as i:
                gate_up(i, 1)
                down(i, 0)
                gate_up(i, 2)
                down(i, 1)
            gate_up(None, 15)
            down(None, 14)
            down(None, 15)

        def moe_act(act, ch, layer, n0):
            L = layer
            act.wait_ge(S("logits"), L + 1)
            ch.link(act.activation(scores, bank[0][:, 0:32], ACT.Exp, scale=-1.0))
            act.sem_inc(S("sig_exp"), 1)
            for q in range(8):
                act.wait_ge(S("gate_rows"), 8 * L + q + 1)
                act.activation(gate_bc[:, 2 * q:2 * q + 2, :], bank[q][:, :].rearrange("p (e n) -> p e n", e=2),
                               ACT.Copy).then_inc(S("gate_copied"), 1)

            def silu(i, e, hf):
                val = (4 * i + 2 * e + hf + 1 if i is not None else 2 * e + hf + 1) + 32 * L
                act.wait_ge(S("gu_done"), val)
                act.wait_ge(S("gu_free"), (4 * i + 2 * e + hf + 1 if i is not None else 2 * e + hf + 1) + 34 * L)
                act.activation(silu_b[:, hf], bank[hf][:, :].rearrange("p (f n) -> p f n", f=2),
                               ACT.Silu).then_inc(S("silu_done"), 1)
                if hf == 1:
                    for m in range(2):
                        act.sem_inc(slot_free[at_ring(n0, 3 * e + m)[0]], 1)

            with act.Fori(0, 8) as i:
                for e in range(2):
                    for hf in range(2):
                        silu(i, e, hf)

        def moe_dve(dve, ch, layer, n0):
            L = layer
            j0 = 3
            dve.memset(yacc, 0.0).then_inc(S("yacc_zero"), 1)
            dve.wait_ge(S("sig_exp"), L + 1)
            ch.link(dve.tensor_scalar(scores, scores, 1.0, None, ALU.add))
            ch.link(dve.reciprocal(scores, scores))
            sv = scores.rearrange("p (s e) -> p s e", s=2)
            ch.link(dve.tensor_tensor(biased.rearrange("p (s e) -> p s e", s=2), sv,
                                      p_("router_b").unsqueeze(1).to_broadcast([P, 2, 16]), ALU.add))
            bv = biased.rearrange("p (g k) -> p g k", k=4)
            a8 = g8a.rearrange("p (g k) -> p g k", k=2)
            b8 = g8b.rearrange("p (g k) -> p g k", k=2)
            dve.tensor_tensor(a8, bv[:, :, 0:2], bv[:, :, 2:4], ALU.max).then_inc(S("dve_par"), 1)
            dve.tensor_tensor(b8, bv[:, :, 0:2], bv[:, :, 2:4], ALU.min).then_inc(S("dve_par"), 1)
            dve.wait_ge(S("dve_par"), 2 * L + 2)
            c8 = g8c.rearrange("p (g k) -> p g k", k=2)
            ch.link(dve.tensor_tensor(c8[:, :, 0], a8[:, :, 0], a8[:, :, 1], ALU.max))
            ch.link(dve.tensor_tensor(c8[:, :, 1], a8[:, :, 0], a8[:, :, 1], ALU.min))
            ch.link(dve.tensor_tensor(a8[:, :, 0], b8[:, :, 0], b8[:, :, 1], ALU.max))
            ch.link(dve.tensor_tensor(a8[:, :, 1], a8[:, :, 0], c8[:, :, 1], ALU.max))
            ch.link(dve.tensor_tensor(b8[:, :, 0], a8[:, :, 1], c8[:, :, 0], ALU.add))

            def first_best(dst, src, n, rank, top, tmp):
                sv_ = src.rearrange("p (s n) -> p s n", s=2)
                tv, dv_ = tmp.rearrange("p (s n) -> p s n", s=2), dst.rearrange("p (s n) -> p s n", s=2)
                ch.link(dve.tensor_reduce(top, sv_, AX, ALU.max))
                ch.link(dve.tensor_tensor(tv, sv_, bcast(top, n), ALU.is_equal))
                ch.link(dve.tensor_tensor(tv, tv, rank.unsqueeze(1).to_broadcast([P, 2, n]), ALU.mult))
                ch.link(dve.tensor_reduce(top, tv, AX, ALU.max))
                ch.link(dve.tensor_tensor(dv_, tv, bcast(top, n), ALU.is_equal))

            gsc = g8c[:, 8:16]
            ch.link(dve.tensor_copy(gsc, b8[:, :, 0]))
            first_best(g2, gsc, 4, c_("rank4"), w2[:, 0:2], g8a[:, 0:8])
            gsel = g2.unsqueeze(2).to_broadcast([P, 8, 4])
            rv = r_a.rearrange("p (g k) -> p g k", k=4)
            ch.link(dve.tensor_tensor(rv, bv, gsel, ALU.mult))
            ch.link(dve.tensor_scalar(g8b[:, 0:8], g2, BIG, -BIG, ALU.mult, ALU.add))
            ch.link(dve.tensor_tensor(masked.rearrange("p (g k) -> p g k", k=4), rv,
                                      bcast(g8b[:, 0:8], 4), ALU.add))
            first_best(oh1, masked, 16, c_("rank16"), w2[:, 0:2], r_b)
            ch.link(dve.scalar_tensor_tensor(masked, oh1, -3.0 * BIG, masked, ALU.mult, ALU.add))
            first_best(oh2, masked, 16, c_("rank16"), w2[:, 0:2], r_b)
            ch.link(dve.tensor_tensor(oh1, oh1, oh2, ALU.add))
            ch.link(dve.tensor_tensor(r_a, oh1, scores, ALU.mult))
            ch.link(dve.tensor_reduce(w2[:, 2:4], r_a.rearrange("p (s e) -> p s e", s=2), AX, ALU.add))
            ch.link(dve.reciprocal(w2[:, 4:6], w2[:, 2:4]))
            dve.tensor_tensor(gates.rearrange("p (s e) -> p s e", s=2), r_a.rearrange("p (s e) -> p s e", s=2),
                              bcast(w2[:, 4:6], 16), ALU.mult).then_inc(S("gates_ready"), 1)
            dve.wait_ge(S("gate_copied"), 8 * (L + 1))
            dve.sem_inc(S("gu_free"), 2)
            dve.sem_inc(S("y_free"), 4)
            dve.wait_ge(S("yacc_zero"), L + 1)

            def act_half(i, e, hf, e_dyn):
                val = (4 * i + 2 * e + hf + 1 if i is not None else 2 * e + hf + 1) + 32 * L
                dve.wait_ge(S("silu_done"), val)
                g = gate_bc[:, e_dyn, :]
                g = g if len(g.shape) == 3 else g.unsqueeze(1)
                ch.link(dve.tensor_tensor(silu_b[:, hf], silu_b[:, hf], g.to_broadcast([P, 2, T]), ALU.mult))
                dve.tensor_tensor(he[:, e % 2, 2 * hf:2 * hf + 2, :], silu_b[:, hf],
                                  bank[2 + hf][:, :].rearrange("p (f n) -> p f n", f=2),
                                  ALU.mult).then_inc(S("he_ready"), 1)
                dve.wait_ge(S("he_ready"), val)
                dve.sem_inc(S("gu_free"), 1)

            def add_y(i, e):
                k = at_ring(n0, 3 * e + 2)[0]
                for b in range(4):
                    base = 8 * i + 4 * e + b if i is not None else 4 * e + b
                    dve.wait_ge(S("y_done"), base + 1 + 64 * L)
                    dve.wait_ge(S("y_free"), base + 1 + 68 * L)
                    yv = yacc[:, 2 * b:2 * b + 2, :]
                    dve.tensor_tensor(yv, yv, bank[4 + b][:, :].rearrange("p (o n) -> p o n", o=2),
                                      ALU.add).then_inc(S("y_free"), 1)
                dve.sem_inc(slot_free[k], 1)

            n_half = 4
            for hf in range(2):
                act_half(None, 0, hf, 0)
            with dve.Fori(0, 7) as i:
                ch.enter(i, n_half)
                for e in range(2):
                    for hf in range(2):
                        act_half(i, e + 1, hf, bass.ds(2 * i + (e + 1), 1))
                    add_y(i, e)
                ch.leave(7)
            for hf in range(2):
                act_half(None, 15, hf, 15)
            add_y(None, 14)
            add_y(None, 15)
            dve.wait_ge(S("y_free"), 68 * (L + 1))
            gv = mod_v[:, layer, 5].rearrange("p c s -> p (c s)")
            yv = yacc.rearrange("p c (s n) -> p (c s) n", s=2)
            rv = res[:, :, :].rearrange("p c (s n) -> p (c s) n", s=2)
            ch.link(dve.tensor_tensor(yv, yv, bcast(gv, P), ALU.mult))
            ch.link(dve.tensor_tensor(rv, rv, yv, ALU.add))

        def out_pe(pe, layer, n0):
            for q in range(2):
                k = wait_slot(pe, n0, q)
                w = ring[:, k, :].rearrange("p (c n) -> p c n", c=KC)
                for b in range(2):
                    for o in range(2):
                        m = 2 * b + o
                        for c in range(KC):
                            last = pe.matmul(bank[2 * q + b][:, o * T:(o + 1) * T], w[:, c, m * P:(m + 1) * P],
                                             act_t[:, c, :], start=(c == 0), stop=(c == KC - 1))
                    last.then_inc(S("mix_done"), 1)

        def out_dve(dve, ch, layer, n0):
            for q in range(2):
                for b in range(2):
                    dve.wait_ge(S("mix_done"), 4 * layer + 2 * q + b + 1)
                    for o in range(2):
                        for s in range(2):
                            c = 4 * q + 2 * b + o
                            r = res[:, c, s * P:(s + 1) * P]
                            last = dve.scalar_tensor_tensor(r, bank[2 * q + b][:, o * T + s * P:o * T + (s + 1) * P],
                                                            gate_col(layer, 2, c, s), r, ALU.mult, ALU.add)
                dve.sem_inc(slot_free[at_ring(n0, q)[0]], 1)
            ch.link(last)

        BATCHES = [(s, d, hq) for s in range(2) for hq in range(2) for d in range(2)]

        def lev(b2, lv, u):
            return b2 * 2 * (LEVELS - 1) + 2 * (lv - 1) + u + 1

        def delta_pe(pe):
            def tr(i):
                pe.wait_ge(S("conv_done"), i + 1)
                if i >= 2:
                    pe.wait_ge(S("tok_copied"), i - 1)
                for s in range(2):
                    last = pe.transpose(bank[4 + i % 2][:, s * P:(s + 1) * P], conv_o[:, i % 3, s, :], ident)
                last.then_inc(S("tok_done"), 1)

            for i in range(24):
                k = wait_slot(pe, OIN0, i // 4)
                if i >= 3:
                    pe.wait_ge(S("z_copied"), i - 2)
                w = ring[:, k, :].rearrange("p (c n) -> p c n", c=KC)
                for c in range(KC):
                    last = pe.matmul(bank[i % 3][:, 0:T], w[:, c, (i % 4) * P:(i % 4 + 1) * P], act_t[:, c, :],
                                     start=(c == 0), stop=(c == KC - 1))
                last.then_inc(S("z_done"), 1)
                if i >= 2:
                    tr(i - 2)
            tr(22)
            tr(23)
            pe.wait_ge(S("z_copied"), 24)
            for q in range(2):
                k = wait_slot(pe, OIN0, 6 + q)
                w = ring[:, k, :].rearrange("p (c n) -> p c n", c=KC)
                for s in range(2):
                    for c in range(KC):
                        last = pe.matmul(bank[2 * q + s][:, :], act_t[:, c, s * P:(s + 1) * P], w[:, c, :],
                                         start=(c == 0), stop=(c == KC - 1))
                    last.then_inc(S("dg_done"), 1)
            for s in range(2):
                for c in range(KC):
                    last = pe.matmul(bank[6][:, s * 32:s * 32 + 32], act_t[:, c, s * P:(s + 1) * P],
                                     p_("w_ab")[:, c * 32:c * 32 + 32], start=(c == 0), stop=(c == KC - 1))
            last.then_inc(S("ab_done"), 1)
            pe.wait_ge(S("g_ready"), 1)
            gv = g_tok.rearrange("p (s d h) -> p s d h", s=2, d=2)
            for i, (m, d) in enumerate((("le", 0), ("ge", 1), ("gt", 0), ("lt", 1))):
                last = pe.matmul(bank[7][:, i * 16:i * 16 + 16], c_(m), gv[:, :, d, :], start=True, stop=True)
            last.then_inc(S("gsum_done"), 1)
            pe.wait_ge(S("qk_ready"), 1)
            pe.wait_ge(S("dg_copied"), 4)
            for n in range(8):
                w, s, hq = n // 4, (n // 2) % 2, n % 2
                if n >= 4:
                    pe.wait_ge(S("qkt_copied"), n - 3)
                for j in range(4):
                    h = 4 * hq + j
                    last = pe.transpose(bank[n % 4][:, j * P:(j + 1) * P],
                                        dqkv[:, s, w * 1024 + h * P:w * 1024 + (h + 1) * P], ident)
                last.then_inc(S("qkt_done"), 1)
            pe.wait_ge(S("qkt_copied"), 8)
            pe.wait_ge(S("gsum_copied"), 1)
            for b2 in range(4):
                for u in range(2):
                    b = 2 * b2 + u
                    s, d, hq = BATCHES[b]
                    w = sets[u]
                    pe.wait_ge(S("gm_ready"), b + 1)
                    if b >= 2:
                        pe.wait_ge(S("batch_end"), b - 1)
                    pe.matmul(bank[3 * u][:, :], c_("gt") if d == 0 else c_("lt"),
                              w["LM"].rearrange("p h n -> p (h n)"), start=True, stop=True).then_inc(S("diff_done"), 1)
                    for j in range(4):
                        kt = qk_t[:, 1, s, 4 * hq + j, :]
                        pe.matmul(bank[3 * u + 1][:, j * P:(j + 1) * P], kt, kt, start=True, stop=True)
                        last = pe.matmul(bank[3 * u + 2][:, j * P:(j + 1) * P], kt, qk_t[:, 0, s, 4 * hq + j, :],
                                         start=True, stop=True)
                    last.then_inc(S("kk_done"), 1)
                for u in range(2):
                    b = 2 * b2 + u
                    w = sets[u]
                    pe.wait_ge(S("xt0_ready"), b + 1)
                    for j in range(4):
                        last = pe.transpose(bank[3 * u][:, j * P:(j + 1) * P], w["XT"][:, j, :], ident)
                    last.then_inc(S("x0_done"), 1)
                for lv in range(1, LEVELS):
                    for u in range(2):
                        w = sets[u]
                        pe.wait_ge(S("lm_ready"), lev(b2, lv, u))
                        if lv == 1:
                            pe.wait_ge(S("x0_copied"), 2 * b2 + u + 1)
                        else:
                            pe.wait_ge(S("x_summed"), lev(b2, lv - 1, u))
                        for j in range(4):
                            last = pe.matmul(bank[3 * u][:, j * P:(j + 1) * P], w["LM"][:, j, :], w["X"][:, j, :],
                                             start=True, stop=True)
                        last.then_inc(S("ly_done"), 1)
                    for u in range(2):
                        w = sets[u]
                        pe.wait_ge(S("ly_copied"), lev(b2, lv, u))
                        if lv == 1:
                            pe.wait_ge(S("at_ready"), 2 * b2 + u + 1)
                        for j in range(4):
                            last = pe.matmul(bank[3 * u + 1][:, j * P:(j + 1) * P], w["Y"][:, j, :], w["XT"][:, j, :],
                                             start=True, stop=True)
                        if lv < LEVELS - 1:
                            for j in range(4):
                                last = pe.matmul(bank[3 * u + 2][:, j * P:(j + 1) * P], w["XT"][:, j, :], w["Y"][:, j, :],
                                                 start=True, stop=True)
                        last.then_inc(S("dx_done"), 1)
                for u in range(2):
                    b = 2 * b2 + u
                    s, d, hq = BATCHES[b]
                    w = sets[u]
                    if s == 1:
                        pe.wait_ge(S("s0_in"), 16)
                        pe.wait_ge(S("x_summed"), lev(b2, LEVELS - 2, u))
                        for j in range(4):
                            h = 4 * hq + j
                            pe.matmul(bank[3 * u][:, j * P:(j + 1) * P], qk_t[:, 1, s, h, :], s0[:, d, h, :],
                                      start=True, stop=True)
                            last = pe.matmul(bank[3 * u + 2][:, j * P:(j + 1) * P], qk_t[:, 0, s, h, :], s0[:, d, h, :],
                                             start=True, stop=True)
                        last.then_inc(S("ks_done"), 1)
                for u in range(2):
                    b = 2 * b2 + u
                    s, d, hq = BATCHES[b]
                    w = sets[u]
                    pe.wait_ge(S("xt_final"), b + 1)
                    for j in range(4):
                        h = 4 * hq + j
                        r = w["Y"][:, j, :] if s == 1 else dqkv[:, s, 2048 + h * P:2048 + (h + 1) * P]
                        last = pe.matmul(bank[3 * u + 1][:, j * P:(j + 1) * P], w["XT"][:, j, :], r, start=True, stop=True)
                    last.then_inc(S("vn_done"), 1)
                for u in range(2):
                    b = 2 * b2 + u
                    s, d, hq = BATCHES[b]
                    w = sets[u]
                    pe.wait_ge(S("vn_ready"), b + 1)
                    for j in range(4):
                        last = pe.matmul(bank[3 * u][:, j * P:(j + 1) * P], w["AT"][:, j, :], w["X"][:, j, :],
                                         start=True, stop=True)
                    last.then_inc(S("o_done"), 1)
                    if s == 0:
                        pe.wait_ge(S("kd_ready"), b + 1)
                        for j in range(4):
                            h = 4 * hq + j
                            last = pe.matmul(bank[3 * u + 1][:, j * P:(j + 1) * P],
                                             dqkv[:, s, 1024 + h * P:1024 + (h + 1) * P], w["LM"][:, j, :],
                                             start=True, stop=True)
                        last.then_inc(S("st_done"), 1)
            for s in range(2):
                pe.wait_ge(S("do_ready"), s + 1)
                for q in range(2):
                    for j in range(4):
                        c = 4 * q + j
                        last = pe.transpose(bank[2 * s + q][:, j * P:(j + 1) * P],
                                            o_d[:, s, c * P:(c + 1) * P], ident)
                    last.then_inc(S("dot_done"), 1)
            pe.wait_ge(S("dot_copied"), 4)
            pe.wait_ge(S("dot_banks_free"), 1)
            out_pe(pe, 1, OOUT0)


        def delta_act(act, ch):
            ab = ab_raw.rearrange("p (s n) -> p s n", s=2)
            for i in range(24):
                act.wait_ge(S("z_done"), i + 1)
                if i == 0:
                    act.wait_ge(S("pad_zero"), 1)
                if i >= 3:
                    act.wait_ge(S("conv_sum"), i - 2)
                act.activation(zpad[:, i % 3, :, 1:129], bank[i % 3][:, 0:T].rearrange("p (s n) -> p s n", s=2),
                               ACT.Copy).then_inc(S("z_copied"), 1)
                if i % 4 == 3:
                    act.sem_inc(slot_free[at_ring(OIN0, i // 4)[0]], 1)
                if i >= 1:
                    act.wait_ge(S("conv_sum"), i)
                    act.activation(conv_o[:, (i - 1) % 3], conv_o[:, (i - 1) % 3], ACT.Silu).then_inc(S("conv_done"), 1)
            act.wait_ge(S("conv_sum"), 24)
            act.activation(conv_o[:, 23 % 3], conv_o[:, 23 % 3], ACT.Silu).then_inc(S("conv_done"), 1)
            for q in range(2):
                for s in range(2):
                    act.wait_ge(S("dg_done"), 2 * q + s + 1)
                    act.activation(dgate[:, s, q * 512:(q + 1) * 512], bank[2 * q + s][:, :], ACT.Silu)\
                       .then_inc(S("dg_copied"), 1)
                act.sem_inc(slot_free[at_ring(OIN0, 6 + q)[0]], 1)
            act.wait_ge(S("sp_abs"), 1)
            ch.link(act.activation(sp_b, sp_b, ACT.Exp, scale=-1.0))
            act.activation(sp_b, sp_b, ACT.Ln, bias=1.0).then_inc(S("sp_ln"), 1)
            act.activation(beta.rearrange("p (s n) -> p s n", s=2), ab[:, :, 16:32], ACT.Exp, scale=-1.0)\
               .then_inc(S("beta_exp"), 1)
            act.activation(negA, p_("a_log"), ACT.Exp).then_inc(S("a_exp"), 1)
            act.wait_ge(S("qk_ss"), 1)
            ch.link(act.activation(qk_ss, qk_ss, ACT.Ln))
            act.activation(qk_ss, qk_ss, ACT.Exp, scale=-0.5).then_inc(S("qk_rs"), 1)
            act.wait_ge(S("gsum_done"), 1)
            gs = bank[7][:, 0:64].rearrange("p (i s h) -> p i s h", i=4, s=2)
            ev, kv = (x.rearrange("p (s d h) -> p s d h", s=2, d=2) for x in (egc, kdec))
            for i, (dst, d) in enumerate(((ev, 0), (ev, 1), (kv, 0), (kv, 1))):
                last = act.activation(dst[:, :, d, :], gs[:, i], ACT.Exp)
            last.then_inc(S("gsum_copied"), 1)
            act.wait_ge(S("gsum_copied"), 1)
            for n in range(8):
                w, s, hq = n // 4, (n // 2) % 2, n % 2
                act.wait_ge(S("qkt_done"), n + 1)
                act.activation(qk_t[:, w, s, 4 * hq:4 * hq + 4, :], bank[n % 4][:, :].rearrange("p (h n) -> p h n", h=4),
                               ACT.Copy).then_inc(S("qkt_copied"), 1)
            for b2 in range(4):
                for u in range(2):
                    b = 2 * b2 + u
                    w = sets[u]
                    act.wait_ge(S("diff_done"), b + 1)
                    act.activation(w["DT"], bank[3 * u][:, :].rearrange("p (h n) -> p h n", h=4), ACT.Exp)\
                       .then_inc(S("dt_ready"), 1)
                for u in range(2):
                    b = 2 * b2 + u
                    w = sets[u]
                    act.wait_ge(S("x0_done"), b + 1)
                    act.activation(w["X"], bank[3 * u][:, :].rearrange("p (h n) -> p h n", h=4), ACT.Copy)\
                       .then_inc(S("x0_copied"), 1)
                for lv in range(1, LEVELS):
                    for u in range(2):
                        w = sets[u]
                        act.wait_ge(S("ly_done"), lev(b2, lv, u))
                        act.activation(w["Y"], bank[3 * u][:, :].rearrange("p (h n) -> p h n", h=4), ACT.Copy)\
                           .then_inc(S("ly_copied"), 1)
                for u in range(2):
                    b = 2 * b2 + u
                    s, d, hq = BATCHES[b]
                    if s == 0:
                        act.wait_ge(S("st_done"), b + 1)
                        if b >= 2:
                            act.wait_ge(S(f"state_out{u}"), 16)
                        act.activation(st_stage[:, u], bank[3 * u + 1][:, :].rearrange("p (h n) -> p h n", h=4), ACT.Copy)\
                           .then_inc(S("st_ready"), 1)
            act.wait_ge(S("o_ss"), 1)
            ch.link(act.activation(o_ss, o_ss, ACT.Ln))
            act.activation(o_ss, o_ss, ACT.Exp, scale=-0.5).then_inc(S("o_rs"), 1)
            for s in range(2):
                for q in range(2):
                    act.wait_ge(S("dot_done"), 2 * s + q + 1)
                    act.activation(act_t[:, 4 * q:4 * q + 4, s * P:(s + 1) * P],
                                   bank[2 * s + q][:, :].rearrange("p (h n) -> p h n", h=4), ACT.Copy,
                                   scale=p_("onorm")).then_inc(S("dot_copied"), 1)
            act.wait_ge(S("dot_copied"), 4)
            act.sem_inc(S("dot_banks_free"), 1)

        def delta_pool(pool, ch):
            pool.memset(zpad, 0.0).then_inc(S("pad_zero"), 1)
            pool.wait_ge(S("ab_done"), 1)
            pool.dma_start(s0, state0).then_inc(S("s0_in"), 16)
            pool.wait_ge(S("qkt_done"), 8)
            lvl = c_("level").rearrange("p (d l n) -> p d l n", d=2, l=LEVELS)

            def mask4(ap):
                return ap.unsqueeze(1).to_broadcast([P, 4, P])

            def gcol(x, s, d, hq):
                i = (s * 2 + d) * 8 + 4 * hq
                return bcast(x[:, i:i + 4], P)

            def st_out_dma(b):
                s, d, hq = BATCHES[b]
                pool.wait_ge(S("st_ready"), b + 1)
                pool.dma_start(st_out[d, :, 4 * hq:4 * hq + 4, :], st_stage[:, b % 2]).then_inc(S(f"state_out{b % 2}"), 16)

            for b2 in range(4):
                for u in range(2):
                    b = 2 * b2 + u
                    s, d, hq = BATCHES[b]
                    w = sets[u]
                    if b >= 2:
                        pool.wait_ge(S("batch_end"), b - 1)
                    pool.tensor_tensor(w["LM"], mask4(c_("le") if d == 0 else c_("ge")), gcol(g_tok, s, d, hq), ALU.mult)\
                        .then_inc(S("gm_ready"), 1)
                for u in range(2):
                    b = 2 * b2 + u
                    s, d, hq = BATCHES[b]
                    w = sets[u]
                    pool.wait_ge(S("dt_ready"), b + 1)
                    pool.tensor_tensor(w["LT"], w["DT"], gcol(nbeta, s, d, hq), ALU.mult).then_inc(S("dtb_ready"), 1)
                    pool.tensor_tensor(w["DT"], w["DT"], mask4(c_("le") if d == 0 else c_("ge")), ALU.mult)\
                        .then_inc(S("dtm_ready"), 1)
                for lv in range(LEVELS):
                    for u in range(2):
                        b = 2 * b2 + u
                        s, d, hq = BATCHES[b]
                        w = sets[u]
                        if lv == 0:
                            pool.wait_ge(S("lt_ready"), b + 1)
                            ch.link(pool.tensor_tensor(w["XT"], w["LT"], mask4(lvl[:, d, 0]), ALU.mult))
                            pool.tensor_tensor(w["XT"], w["XT"], mask4(ident), ALU.add).then_inc(S("xt0_ready"), 1)
                        else:
                            if lv >= 2:
                                pool.wait_ge(S("ly_done"), lev(b2, lv - 1, u))
                            pool.tensor_tensor(w["LM"], w["LT"], mask4(lvl[:, d, lv]), ALU.mult).then_inc(S("lm_ready"), 1)
                for u in range(2):
                    b = 2 * b2 + u
                    s, d, hq = BATCHES[b]
                    w = sets[u]
                    if s == 0:
                        pool.wait_ge(S("vn_ready"), b + 1)
                        pool.tensor_tensor(w["LM"], w["X"], gcol(kdec, s, d, hq), ALU.mult).then_inc(S("kd_ready"), 1)
                if b2 < 2:
                    for u in range(2):
                        st_out_dma(2 * b2 + u)
            pool.wait_ge(S("state_out0"), 32)
            pool.wait_ge(S("state_out1"), 32)


        def delta_dve(dve, ch):
            ab = ab_raw.rearrange("p (s n) -> p s n", s=2)
            cw = p_("conv").rearrange("p (i j) -> p i j", j=3)

            def to_tok(i):
                dve.wait_ge(S("tok_done"), i + 1)
                dve.tensor_copy(dqkv[:, :, i * P:(i + 1) * P], bank[4 + i % 2][:, 0:T].rearrange("p (s n) -> p s n", s=2))\
                   .then_inc(S("tok_copied"), 1)

            for i in range(24):
                dve.wait_ge(S("z_copied"), i + 1)
                if i >= 3:
                    dve.wait_ge(S("tok_done"), i - 2)
                z, y = zpad[:, i % 3], conv_o[:, i % 3]
                ch.link(dve.tensor_scalar(y, z[:, :, 0:128], cw[:, i, 0:1], None, ALU.mult))
                ch.link(dve.scalar_tensor_tensor(y, z[:, :, 1:129], cw[:, i, 1:2], y, ALU.mult, ALU.add))
                dve.scalar_tensor_tensor(y, z[:, :, 2:130], cw[:, i, 2:3], y, ALU.mult, ALU.add).then_inc(S("conv_sum"), 1)
                if i >= 3:
                    to_tok(i - 3)
            for i in range(21, 24):
                to_tok(i)
            dve.wait_ge(S("ab_done"), 1)
            ch.link(dve.tensor_copy(ab, bank[6][:, 0:64].rearrange("p (s n) -> p s n", s=2)))
            xv = sp_x.rearrange("p (s n) -> p s n", s=2)
            ch.link(dve.tensor_tensor(xv, ab[:, :, 0:16], p_("dt_bias").unsqueeze(1).to_broadcast([P, 2, 16]), ALU.add))
            ch.link(dve.tensor_scalar(sp_a, sp_x, -1.0, None, ALU.mult))
            dve.tensor_tensor(sp_b, sp_a, sp_x, ALU.max).then_inc(S("sp_abs"), 1)
            dve.wait_ge(S("sp_ln"), 1)
            ch.link(dve.scalar_tensor_tensor(sp_a, sp_x, 0.0, sp_b, ALU.max, ALU.add))
            dve.wait_ge(S("a_exp"), 1)
            dve.wait_ge(S("beta_exp"), 1)
            ch.link(dve.tensor_scalar(sp_a, sp_a, -1.0, None, ALU.mult))
            dve.tensor_tensor(g_tok.rearrange("p (s n) -> p s n", s=2), sp_a.rearrange("p (s n) -> p s n", s=2),
                              negA.unsqueeze(1).to_broadcast([P, 2, 16]), ALU.mult).then_inc(S("g_ready"), 1)
            ch.link(dve.tensor_scalar(beta, beta, 1.0, None, ALU.add))
            ch.link(dve.reciprocal(beta, beta))
            ch.link(dve.tensor_scalar(nbeta, beta, -1.0, None, ALU.mult))
            dve.wait_ge(S("tok_copied"), 24)
            for s in range(2):
                qk = dqkv[:, s, 0:2048]
                ch.link(dve.tensor_tensor(dsq, qk, qk, ALU.mult))
                ch.link(dve.tensor_reduce(qk_ss[:, s * 16:s * 16 + 16], dsq.rearrange("p (h n) -> p h n", h=16), AX, ALU.add))
            dve.tensor_scalar(qk_ss, qk_ss, 1e-6, None, ALU.add).then_inc(S("qk_ss"), 1)
            dve.wait_ge(S("qk_rs"), 1)
            rv = qk_ss.rearrange("p (s w h) -> p s w h", s=2, w=2)
            ch.link(dve.tensor_scalar(rv[:, :, 0, :], rv[:, :, 0, :], float(P) ** -0.5, None, ALU.mult))
            for s in range(2):
                qk = dqkv[:, s, 0:2048].rearrange("p (h n) -> p h n", h=16)
                last = dve.tensor_tensor(qk, qk, bcast(qk_ss[:, s * 16:s * 16 + 16], P), ALU.mult)
            last.then_inc(S("qk_ready"), 1)

            def b4(x, s, d, hq):
                i = (s * 2 + d) * 8 + 4 * hq
                return bcast(x[:, i:i + 4], P)

            def ps(i):
                return bank[i][:, :].rearrange("p (h n) -> p h n", h=4)

            for b2 in range(4):
                for u in range(2):
                    b = 2 * b2 + u
                    w = sets[u]
                    dve.wait_ge(S("kk_done"), b + 1)
                    dve.wait_ge(S("dtb_ready"), b + 1)
                    dve.tensor_tensor(w["LT"], w["LT"], ps(3 * u + 1), ALU.mult).then_inc(S("lt_ready"), 1)
                    dve.wait_ge(S("dtm_ready"), b + 1)
                    dve.tensor_tensor(w["AT"], w["DT"], ps(3 * u + 2), ALU.mult).then_inc(S("at_ready"), 1)
                for u in range(2):
                    dve.wait_ge(S("x0_copied"), 2 * b2 + u + 1)
                for lv in range(1, LEVELS):
                    for u in range(2):
                        w = sets[u]
                        dve.wait_ge(S("dx_done"), lev(b2, lv, u))
                        if lv < LEVELS - 1:
                            ch.link(dve.tensor_tensor(w["X"], w["X"], ps(3 * u + 2), ALU.add))
                        dve.tensor_tensor(w["XT"], w["XT"], ps(3 * u + 1), ALU.add).then_inc(S("x_summed"), 1)
                        dve.wait_ge(S("x_summed"), lev(b2, lv, u))
                for u in range(2):
                    b = 2 * b2 + u
                    s, d, hq = BATCHES[b]
                    w = sets[u]
                    if s == 1:
                        dve.wait_ge(S("ks_done"), b - 3)
                        ch.link(dve.tensor_tensor(w["Y"], ps(3 * u), b4(egc, s, d, hq), ALU.mult))
                        vv = dqkv[:, s, 2048 + 512 * hq:2048 + 512 * hq + 512].rearrange("p (h n) -> p h n", h=4)
                        ch.link(dve.tensor_tensor(w["Y"], vv, w["Y"], ALU.subtract))
                        oo = o_d[:, s, 512 * hq:512 * hq + 512].rearrange("p (h n) -> p h n", h=4)
                        ch.link(dve.tensor_tensor(w["LT"], ps(3 * u + 2), b4(egc, s, d, hq), ALU.mult))
                        if d == 0:
                            ch.link(dve.tensor_copy(oo, w["LT"]))
                        else:
                            ch.link(dve.tensor_tensor(oo, oo, w["LT"], ALU.add))
                    dve.sem_inc(S("xt_final"), 1)
                for u in range(2):
                    b = 2 * b2 + u
                    s, d, hq = BATCHES[b]
                    w = sets[u]
                    dve.wait_ge(S("vn_done"), b + 1)
                    dve.tensor_tensor(w["X"], ps(3 * u + 1), b4(beta, s, d, hq), ALU.mult).then_inc(S("vn_ready"), 1)
                for u in range(2):
                    b = 2 * b2 + u
                    s, d, hq = BATCHES[b]
                    w = sets[u]
                    dve.wait_ge(S("o_done"), b + 1)
                    oo = o_d[:, s, 512 * hq:512 * hq + 512].rearrange("p (h n) -> p h n", h=4)
                    if s == 0 and d == 0:
                        ch.link(dve.tensor_copy(oo, ps(3 * u)))
                    else:
                        ch.link(dve.tensor_tensor(oo, oo, ps(3 * u), ALU.add))
                    if s == 0:
                        dve.wait_ge(S("st_ready"), b + 1)
                    dve.sem_inc(S("batch_end"), 1)
            for s in range(2):
                ch.link(dve.tensor_tensor(dsq[:, s * 1024:(s + 1) * 1024], o_d[:, s, :], o_d[:, s, :], ALU.mult))
            ch.link(dve.tensor_reduce(o_ss, dsq.rearrange("p (h n) -> p h n", h=16), AX, ALU.add))
            dve.tensor_scalar(o_ss, o_ss, 1.0 / P, EPS, ALU.mult, ALU.add).then_inc(S("o_ss"), 1)
            dve.wait_ge(S("o_rs"), 1)
            for s in range(2):
                oo = o_d[:, s, :].rearrange("p (h n) -> p h n", h=8)
                ch.link(dve.tensor_tensor(oo, oo, bcast(o_ss[:, s * 8:s * 8 + 8], P), ALU.mult))
                dve.tensor_tensor(o_d[:, s, :], o_d[:, s, :], dgate[:, s, :], ALU.mult).then_inc(S("do_ready"), 1)
            out_dve(dve, ch, 1, OOUT0)

        PAIRS = [(kind, s, c) for kind in range(2) for s in range(2) for c in range(4)]

        @block.tensor
        def _(pe):
            pe.wait_ge(S("params_in"), 16)
            pe.wait_ge(S("consts_in"), 16)
            pe.wait_ge(S("cond_ready"), 1)
            with pe.Fori(0, 4) as t:
                for k in range(RING):
                    pe.wait_ge(slot_full[k], t * 16 + 16)
                    pe.wait_ge(S("ada_free"), t * RING + (k + 1))
                    w = ring[:, k, :].rearrange("p (c n) -> p c n", c=KC)
                    for m in range(4):
                        for c in range(KC):
                            last = pe.matmul(bank[k][:, 2 * m:2 * m + 2], w[:, c, m * P:(m + 1) * P],
                                             cond_t[:, 2 * c:2 * c + 2], start=(c == 0), stop=(c == KC - 1))
                    last.then_inc(S("ada_done"), 1)
            meet(pe, "pe")
            for n in range(12):
                q, s = n // 2, n % 2
                k = wait_slot(pe, EIN0, q)
                w = ring[:, k, :].rearrange("p (c n) -> p c n", c=KC)
                if n >= 4:
                    pe.wait_ge(S("proj_copied"), n - 3)
                for c in range(KC):
                    last = pe.matmul(bank[n % 4][:, :], act_t[:, c, s * P:(s + 1) * P], w[:, c, :],
                                     start=(c == 0), stop=(c == KC - 1))
                last.then_inc(S("proj_done"), 1)
            pe.wait_ge(S("proj_copied"), 12)
            for n in range(8):
                wi, s = n // 2, n % 2
                col = (0, 512, 1536, 2048)[wi]
                if n >= 2:
                    pe.wait_ge(S("ht_copied"), n - 1)
                for j in range(4):
                    last = pe.transpose(bank[4 + n % 2][:, j * P:(j + 1) * P], qkv[:, s, col + j * P:col + (j + 1) * P], ident)
                last.then_inc(S("ht_done"), 1)
            pe.wait_ge(S("ht_copied"), 8)
            pe.wait_ge(S("even_in"), 96)

            def sc(p):
                kind, s, c = PAIRS[p]
                if p >= 2:
                    pe.wait_ge(S("exp_done"), 2 * (p - 1))
                for j in range(2):
                    bk = bank[p % 2 + 6 * j]
                    r = slice(64 * j, 64 * j + 64)
                    q = heads_t[r, 2 * kind, s, c, :]
                    biased_ = kind == 0 and s == 1
                    last = pe.matmul(bk[:, 0:P], q, heads_t[r, 2 * kind + 1, s, c, :], start=True, stop=not biased_)
                    if biased_:
                        last = pe.matmul(bk[:, 0:P], ident, bias[:, 2 * c + j, :], start=False, stop=True)
                    if s == 1:
                        cache = nkc if kind == 0 else dkc
                        last = pe.matmul(bk[:, P:2 * P], q, cache[r, c, :], start=True, stop=True)
                last.then_inc(S("score_done"), 1)

            def pt(p):
                kind, s, c = PAIRS[p]
                pe.wait_ge(S("p_ready"), p + 1)
                if p >= 2:
                    pe.wait_ge(S("pt_copied"), p - 1)
                nk2 = 1 if s == 0 else 2
                for j in range(2 if kind == 0 else 1):
                    for t in range(nk2):
                        i = j * nk2 + t
                        last = pe.transpose(bank[2 + p % 2][:, i * P:(i + 1) * P], probs[:, p % 2, j, t * P:(t + 1) * P], ident)
                last.then_inc(S("pt_done"), 1)

            def pv(p):
                kind, s, c = PAIRS[p]
                g = p // 4
                pe.wait_ge(S("pt_copied"), p + 1)
                if p % 4 == 0 and g >= 2:
                    pe.wait_ge(S("o_copied"), g - 1)
                nk2 = 1 if s == 0 else 2
                pflat = probs_t[:, p % 2].rearrange("p j n -> p (j n)")
                for j in range(2 if kind == 0 else 1):
                    if kind == 0:
                        h = 2 * c + j
                        vs = [qkv[:, s, 1024 + h * 64:1024 + h * 64 + 64], nvc[:, h * 64:h * 64 + 64]]
                        out = bank[4 + g % 2][:, h * 64:h * 64 + 64]
                    else:
                        vs = [qkv[:, s, 2560 + c * P:2560 + (c + 1) * P], dvc[:, c * P:(c + 1) * P]]
                        out = bank[4 + g % 2][:, c * P:(c + 1) * P]
                    for t in range(nk2):
                        i = j * nk2 + t
                        last = pe.matmul(out, pflat[:, i * P:(i + 1) * P], vs[t], start=(t == 0), stop=(t == nk2 - 1))
                last.then_inc(S("pv_done"), 1)

            for p in range(18):
                if p < 16:
                    sc(p)
                if 1 <= p < 17:
                    pt(p - 1)
                if p >= 2:
                    pv(p - 2)
            for g in range(4):
                kind, s = g // 2, g % 2
                pe.wait_ge(S("o_copied"), 4)
                if kind == 1:
                    pe.wait_ge(S("o_normed"), 1)
                for j in range(4):
                    last = pe.transpose(bank[g][:, j * P:(j + 1) * P], o_tok[:, s, kind * 512 + j * P:kind * 512 + (j + 1) * P], ident)
                last.then_inc(S("ot_done"), 1)
            pe.wait_ge(S("ot_copied"), 4)
            out_pe(pe, 0, EOUT0)
            meet(pe, "pe")
            ln_pe(pe, 0)
            meet(pe, "pe")
            moe_pe(pe, 0, MOE0)
            meet(pe, "pe")
            ln_pe(pe, 1)
            meet(pe, "pe")
            delta_pe(pe)
            meet(pe, "pe")
            ln_pe(pe, 2)
            meet(pe, "pe")
            moe_pe(pe, 1, MOE1)
            meet(pe, "pe")
            ln_pe(pe, 3)
            meet(pe, "pe")
            for s in range(2):
                for q in range(2):
                    for j in range(4):
                        last = pe.transpose(bank[2 * s + q][:, j * P:(j + 1) * P], res[:, 4 * q + j, s * P:(s + 1) * P], ident)
                    last.then_inc(S("yt_done"), 1)

        @block.scalar
        def _(act):
            ch = Chain(act, "act_step")
            act.wait_ge(S("params_in"), 16)
            act.activation(cond_t, p_("cond"), ACT.Silu).then_inc(S("cond_ready"), 1)
            meet(act, "act")
            act.activation(lam_w[:, 0:2], lam_w[:, 0:2], ACT.Exp).then_inc(S("lam_exp"), 1)
            for n in range(12):
                q, s = n // 2, n % 2
                if q in (3, 4) and s == 1:
                    continue
                act.wait_ge(S("proj_done"), n + 1)
                dst = qkv[:, s, q * 512:(q + 1) * 512]
                act.activation(dst, bank[n % 4][:, :], ACT.Copy, scale=(0.125 if q in (0, 3) else 1.0))\
                   .then_inc(S("proj_act"), 1)
                act.wait_ge(S("proj_act"), 1 + len([m for m in range(n) if not (m // 2 in (3, 4) and m % 2 == 1)]))
                act.wait_ge(S("proj_copied"), n) if n else None
                act.sem_inc(S("proj_copied"), 1)
                if s == 1:
                    act.sem_inc(slot_free[at_ring(EIN0, q)[0]], 1)
                if s == 0 and q in (1, 2, 4, 5):
                    act.sem_inc(S("kv_out_ready"), 1)
            for n in range(8):
                wi, s = n // 2, n % 2
                act.wait_ge(S("ht_done"), n + 1)
                act.activation(heads_t[:, wi, s], bank[4 + n % 2][:, :].rearrange("p (c n) -> p c n", c=4), ACT.Copy)\
                   .then_inc(S("ht_copied"), 1)
            def ptc(p):
                kind, s, c = PAIRS[p]
                n = (1 if s == 0 else 2) * (2 if kind == 0 else 1) * P
                act.wait_ge(S("pt_done"), p + 1)
                if p >= 2:
                    act.wait_ge(S("pv_done"), p - 1)
                act.activation(probs_t[:, p % 2].rearrange("p j n -> p (j n)")[:, 0:n], bank[2 + p % 2][:, 0:n], ACT.Copy)\
                   .then_inc(S("pt_copied"), 1)

            def oc(g):
                kind, s = g // 2, g % 2
                act.wait_ge(S("pv_done"), 4 * g + 4)
                act.activation(o_tok[:, s, kind * 512:(kind + 1) * 512], bank[4 + g % 2][:, :], ACT.Copy)\
                   .then_inc(S("o_copied"), 1)

            for p in range(18):
                if p < 16:
                    kind, s, c = PAIRS[p]
                    nk = 128 if s == 0 else 256
                    if p >= 2:
                        act.wait_ge(S("pt_done"), p - 1)
                    for j in range(2):
                        act.wait_ge(S("max_done"), 2 * p + j + 1)
                        act.activation(probs[:, p % 2, j, 0:nk], bank[p % 2 + 6 * j][:, 0:nk], ACT.Exp,
                                       bias=mx[:, 2 * p + j:2 * p + j + 1],
                                       accum_out=sums[:, 2 * p + j:2 * p + j + 1]).then_inc(S("exp_done"), 1)
                if 1 <= p < 17:
                    ptc(p - 1)
                if p >= 2 and (p - 2) % 4 == 3:
                    oc((p - 2) // 4)
            act.wait_ge(S("o_ms"), 1)
            ch.link(act.activation(rms[:, 0:8], rms[:, 0:8], ACT.Ln))
            act.activation(rms[:, 0:8], rms[:, 0:8], ACT.Exp, scale=-0.5).then_inc(S("o_rms"), 1)
            for g in range(2):
                act.wait_ge(S("ot_done"), g + 1)
                act.activation(act_t[:, 0:4, g * P:(g + 1) * P], bank[g][:, :].rearrange("p (c n) -> p c n", c=4), ACT.Copy)\
                   .then_inc(S("ot_copied"), 1)
            for g in range(2):
                act.wait_ge(S("ot_done"), g + 3)
                act.activation(act_t[:, 4:8, g * P:(g + 1) * P], bank[2 + g][:, :].rearrange("p (c n) -> p c n", c=4),
                               ACT.Copy, scale=sub_g).then_inc(S("ot_copied"), 1)
            meet(act, "act")
            ln_act(act, ch, 0)
            meet(act, "act")
            moe_act(act, ch, 0, MOE0)
            meet(act, "act")
            ln_act(act, ch, 1)
            meet(act, "act")
            delta_act(act, ch)
            meet(act, "act")
            ln_act(act, ch, 2)
            meet(act, "act")
            moe_act(act, ch, 1, MOE1)
            meet(act, "act")
            ln_act(act, ch, 3)
            meet(act, "act")
            for g in range(4):
                s, q = g // 2, g % 2
                act.wait_ge(S("yt_done"), g + 1)
                act.activation(y_tok[:, s, q * 512:(q + 1) * 512], bank[g][:, :], ACT.Copy).then_inc(S("y_ready"), 1)

        @block.vector
        def _(dve):
            ch = Chain(dve, "dve_step")
            dve.wait_ge(S("params_in"), 16)
            dve.sem_inc(S("ada_free"), RING)
            with dve.Fori(0, 4) as t:
                for k in range(RING):
                    dve.wait_ge(S("ada_done"), t * RING + (k + 1))
                    col = bass.ds(t * 48 + 8 * k, 8)
                    a, b = PARAM_W["ada_b"]
                    dve.tensor_tensor(mod[:, col], bank[k][:, 0:8], par[:, bass.ds(t * 48 + (a + 8 * k), 8)], ALU.add)\
                       .then_inc(S("ada_free"), 1)
                    dve.sem_inc(slot_free[k], 1)
            dve.wait_ge(S("ada_free"), RING + 24)
            for l in range(DEPTH):
                for j in (1, 4):
                    m = mod_v[:, l, j]
                    ch.link(dve.tensor_scalar(m, m, 1.0, None, ALU.add))
            for site, (l, j) in enumerate(((0, 3), (1, 0), (1, 3))):
                sl = slice(site * 16, site * 16 + 16)
                shift, scale = (mod_v[:, l, j + i].rearrange("p c s -> p (c s)") for i in range(2))
                ch.link(dve.tensor_tensor(mod_g[:, sl], p_("ln_g")[:, sl], scale, ALU.mult))
                ch.link(dve.tensor_tensor(mod_b[:, sl], p_("ln_b")[:, sl], scale, ALU.mult))
                ch.link(dve.tensor_tensor(mod_b[:, sl], mod_b[:, sl], shift, ALU.add))
            for i, name in enumerate(("ln_g", "ln_b")):
                ch.link(dve.tensor_scalar(ln_scaled[:, 64 * i:64 * i + 48], p_(name)[:, 0:48], ALPHA, None, ALU.mult))
                ch.link(dve.tensor_copy(ln_scaled[:, 64 * i + 48:64 * i + 64], p_(name)[:, 48:64]))
            ch.link(dve.tensor_scalar(sub_g, p_("subln"), 1.0 - (0.8 - 0.6 * math.exp(0.0)), None, ALU.mult))
            dve.wait_ge(S("even_in"), 96)
            lamp = lam_p.rearrange("p (a b n) -> p a b n", a=2, b=2)
            ch.link(dve.tensor_tensor(rope_1[:, 0:128].rearrange("p (a n) -> p a n", a=2), lamp[:, :, 0], lamp[:, :, 1], ALU.mult))
            ch.link(dve.tensor_reduce(lam_w[:, 0:2], rope_1[:, 0:128].rearrange("p (a n) -> p a n", a=2), AX, ALU.add))
            dve.wait_ge(S("x_in"), 16)
            dve.wait_ge(S("pool_step"), 1)
            av = act_t[:, :, :].rearrange("p c (s n) -> p (c s) n", s=2)
            ch.link(dve.tensor_tensor(av, av, bcast(mod_v[:, 0, 1].rearrange("p c s -> p (c s)"), P), ALU.mult))
            ch.link(dve.tensor_tensor(av, av, bcast(mod_v[:, 0, 0].rearrange("p c s -> p (c s)"), P), ALU.add))
            meet(dve, "dve")
            for q in (3, 4):
                n = 2 * q + 1
                dve.wait_ge(S("proj_done"), n + 1)
                src = bank[n % 4][:, :].rearrange("p (h a b n) -> p h a b n", h=8, a=2, b=2)
                t1 = rope_1.rearrange("p (h n) -> p h n", h=8)
                t2 = rope_2.rearrange("p (h a b n) -> p h a b n", h=8, a=2, b=2)
                sn = c_("rope_s").rearrange("p (a b n) -> p a b n", a=2, b=2)
                ch.link(dve.tensor_tensor(t1, bank[n % 4][:, :].rearrange("p (h n) -> p h n", h=8),
                                          c_("rope_c").unsqueeze(1).to_broadcast([P, 8, 64]), ALU.mult))
                for b in range(2):
                    for a in range(2):
                        ch.link(dve.tensor_tensor(t2[:, :, a, b, :], src[:, :, a, 1 - b, :],
                                                  sn[:, a, b, :].unsqueeze(1).to_broadcast([P, 8, 16]), ALU.mult))
                dst = qkv[:, 1, q * 512:(q + 1) * 512]
                ch.link(dve.tensor_tensor(dst, rope_1, rope_2, ALU.add))
                if q == 3:
                    ch.link(dve.tensor_scalar(dst, dst, 0.125, None, ALU.mult))
                dve.wait_ge(S("proj_copied"), n)
                dve.sem_inc(S("proj_copied"), 1)
                dve.sem_inc(slot_free[at_ring(EIN0, q)[0]], 1)
            dve.wait_ge(S("lam_exp"), 1)
            ch.link(dve.tensor_tensor(lam_w[:, 2:3], lam_w[:, 1:2], lam_w[:, 0:1], ALU.subtract))
            ch.link(dve.tensor_scalar(lam_w[:, 3:4], lam_w[:, 2:3], -(0.8 - 0.6 * math.exp(0.0)), None, ALU.add))

            def mxp(p):
                kind, s, c = PAIRS[p]
                nk = 128 if s == 0 else 256
                dve.wait_ge(S("score_done"), p + 1)
                for j in range(2):
                    dve.tensor_reduce(mx[:, 2 * p + j:2 * p + j + 1], bank[p % 2 + 6 * j][:, 0:nk],
                                      AX, ALU.max, negate=True).then_inc(S("max_done"), 1)

            for p in range(17):
                if p < 16:
                    mxp(p)
                if p < 1:
                    continue
                q = p - 1
                kind, s, c = PAIRS[q]
                nk = 128 if s == 0 else 256
                dve.wait_ge(S("exp_done"), 2 * (q + 1))
                rs = rsum[:, 2 * q:2 * q + 2]
                ch.link(dve.reciprocal(rs, sums[:, 2 * q:2 * q + 2]))
                pb = probs[:, q % 2]
                if kind == 0:
                    dve.tensor_tensor(pb[:, :, 0:nk], pb[:, :, 0:nk], bcast(rs, nk), ALU.mult).then_inc(S("p_ready"), 1)
                else:
                    ch.link(dve.tensor_tensor(nlr[:, 0:1], rs[:, 1:2], lam_w[:, 3:4], ALU.mult))
                    ch.link(dve.tensor_scalar(pb[:, 0, 0:nk], pb[:, 0, 0:nk], rs[:, 0:1], None, ALU.mult))
                    dve.scalar_tensor_tensor(pb[:, 0, 0:nk], pb[:, 1, 0:nk], nlr[:, 0:1], pb[:, 0, 0:nk],
                                             ALU.mult, ALU.add).then_inc(S("p_ready"), 1)
            dve.wait_ge(S("o_copied"), 4)
            ov = o_tok[:, :, 512:1024]
            dve.wait_ge(S("pv_done"), 16)
            dve.wait_ge(S("out_done"), 64)
            ch.link(dve.tensor_tensor(o_sq.rearrange("p (s n) -> p s n", s=2), ov, ov, ALU.mult))
            ch.link(dve.tensor_reduce(rms[:, 0:8], o_sq.rearrange("p (h n) -> p h n", h=8), AX, ALU.add))
            dve.tensor_scalar(rms[:, 0:8], rms[:, 0:8], 1.0 / P, EPS, ALU.mult, ALU.add).then_inc(S("o_ms"), 1)
            dve.wait_ge(S("o_rms"), 1)
            for s in range(2):
                oh = o_tok[:, s, 512:1024].rearrange("p (h n) -> p h n", h=4)
                ch.link(dve.tensor_tensor(oh, oh, bcast(rms[:, 4 * s:4 * s + 4], P), ALU.mult))
            dve.sem_inc(S("o_normed"), 1)
            out_dve(dve, ch, 0, EOUT0)
            meet(dve, "dve")
            ln_dve(dve, ch, 0)
            meet(dve, "dve")
            moe_dve(dve, ch, 0, MOE0)
            meet(dve, "dve")
            ln_dve(dve, ch, 1)
            meet(dve, "dve")
            delta_dve(dve, ch)
            meet(dve, "dve")
            ln_dve(dve, ch, 2)
            meet(dve, "dve")
            moe_dve(dve, ch, 1, MOE1)
            meet(dve, "dve")
            ln_dve(dve, ch, 3)
            meet(dve, "dve")

        @block.sync
        def _(sp):
            sp.dma_start(par[:, :], params).then_inc(S("params_in"), 16)
            sp.dma_start(cst[:, :], consts).then_inc(S("consts_in"), 16)
            for k in range(RING):
                sp.dma_start(ring[:, k, :], slots[k]).then_inc(slot_full[k], 16)
            with sp.Fori(0, N_SLOTS // RING - 1) as turn:
                for k in range(RING):
                    sp.wait_ge(slot_free[k], turn + 1)
                    sp.dma_start(ring[:, k, :], slots[bass.ds(turn * RING + (RING + k), 1)].rearrange("a p n -> (a p) n")).then_inc(slot_full[k], 16)

        @block.gpsimd
        def _(pool):
            ch = Chain(pool, "pool_step")
            pool.dma_start(act_t[:, :, :], x_t).then_inc(S("x_in"), 16)
            for dst, src in ((nkc, nat_kc), (nvc, nat_vc), (dkc, diff_kc), (dvc, diff_vc), (bias, nat_bias), (lam_p, lam_in)):
                pool.dma_start(dst, src).then_inc(S("even_in"), 16)
            pool.wait_ge(S("x_in"), 16)
            ch.link(pool.tensor_scalar(res[:, :, :], act_t[:, :, :], ALPHA, None, ALU.mult))
            pool.wait_ge(S("even_in"), 96)
            pool.wait_ge(S("consts_in"), 16)
            ch.link(pool.tensor_tensor(bias, bias, c_("window").unsqueeze(1).to_broadcast([P, 8, P]), ALU.add))
            meet(pool, "pool")
            pool.wait_ge(S("kv_out_ready"), 4)
            for w, out in ((1, nk_out), (2, nv_out), (4, dk_out), (5, dv_out)):
                pool.dma_start(out, qkv[:, 0, w * 512:(w + 1) * 512]).then_inc(S("out_done"), 16)
            pool.wait_ge(S("out_done"), 64)
            meet(pool, "pool")
            ln_pool(pool, ch, 0)
            meet(pool, "pool")
            moe_pool(pool, ch)
            meet(pool, "pool")
            ln_pool(pool, ch, 1)
            meet(pool, "pool")
            delta_pool(pool, ch)
            meet(pool, "pool")
            ln_pool(pool, ch, 2)
            meet(pool, "pool")
            moe_pool(pool, ch)
            meet(pool, "pool")
            ln_pool(pool, ch, 3)
            meet(pool, "pool")
            pool.wait_ge(S("y_ready"), 4)
            for s in range(2):
                pool.dma_start(y_out[s], y_tok[:, s, :]).then_inc(S("out_done"), 16)
            pool.wait_ge(S("out_done"), 64 + 32)


def shape_constants():
    import numpy as np
    f = np.float32
    i = np.arange(P)
    r, c = i[:, None], i[None, :]
    out = {"ident": r == c, "mean": np.full((P, P), 1.0 / D), "le": r <= c, "gt": r > c, "ge": r >= c, "lt": r < c}
    lv = []
    for d in range(2):
        for k in range(LEVELS):
            same = (r >> (k + 1)) == (c >> (k + 1))
            hi_r, hi_c = ((r >> k) & 1) == 1, ((c >> k) & 1) == 1
            lv.append(same & ((~hi_r & hi_c) if d == 0 else (hi_r & ~hi_c)))
    out["level"] = np.concatenate(lv, 1)
    inv = (f(10000.0) ** (-np.arange(16, dtype=f) / f(16))).astype(f)
    ar = (i // 64).astype(f)[:, None] * inv
    ac = (i % 64).astype(f)[:, None] * inv
    out["rope_c"] = np.concatenate([np.cos(ar), np.cos(ar), np.cos(ac), np.cos(ac)], 1)
    out["rope_s"] = np.concatenate([-np.sin(ar), np.sin(ar), -np.sin(ac), np.sin(ac)], 1)
    start = np.clip(i % 64 - 8, 0, 48)[:, None]
    ok = ((c % 64) >= start) & ((c % 64) < start + 16)
    out["window"] = np.where(ok, 0.0, -BIG)
    out["rank4"] = np.broadcast_to(4.0 - np.arange(4), (P, 4))
    out["rank16"] = np.broadcast_to(16.0 - np.arange(16), (P, 16))
    return np.ascontiguousarray(np.concatenate([np.asarray(out[n], f) for n in CONST_W], 1))


def kernel(**inputs):
    import numpy as np
    import concourse.bacc as bacc
    from concourse.bass_utils import run_bass_kernel_spmd as run

    a = {k: np.asarray(v) for k, v in inputs.items()}

    def rows(w, n):
        k, m = w.shape
        return w.reshape(k // P, P, m // n, n).transpose(2, 1, 0, 3).reshape(m // n, P, (k // P) * n)

    def feat(v):
        v = v.reshape(v.shape[:-1] + (-1, P))
        return np.moveaxis(v, -1, 0)

    def moe_slots(l):
        g = np.stack([np.stack([rows(a["moe_wg"][l, e], FF)[0], rows(a["moe_wu"][l, e], FF)[0],
                                rows(a["moe_wd"][l, e], D)[0]]) for e in range(N_EXP)])
        return g.reshape(3 * N_EXP, P, SLOT)

    w_odd = a["w_in_odd"][0]
    slots = np.concatenate([rows(a["ada_w"][0], 512), rows(a["ada_w"][1], 512), rows(a["w_in_even"][0], 512),
                            rows(a["w_out_even"][0], 512), moe_slots(0),
                            rows(np.concatenate([w_odd[:, :3072], w_odd[:, 3104:]], 1), 512),
                            rows(a["w_out_odd"][0], 512), moe_slots(1)], 0)
    x = np.stack([a["x_prompt"][0], a["x_sample"][0]])
    x_t = np.ascontiguousarray(x.reshape(2, P, KC, P).transpose(3, 2, 0, 1).reshape(P, KC, T))

    def rep(v):
        return np.broadcast_to(v.reshape(1, -1), (P, v.size))

    par = {
        "cond": feat(np.stack([a["c_ctx"], a["c"][0]])).transpose(0, 2, 1).reshape(P, -1),
        "ada_b": np.repeat(feat(a["ada_b"]).reshape(P, 96), 2, axis=1),
        "ln_g": np.repeat(feat(a["ln_g"]).reshape(P, 32), 2, axis=1),
        "ln_b": np.repeat(feat(a["ln_b"]).reshape(P, 32), 2, axis=1),
        "router": rows(a["router_w"], 16)[0],
        "router_b": rep(a["router_b"]),
        "subln": a["diff_subln"][0].reshape(P, 1),
        "onorm": a["onorm_odd"][0].reshape(P, 1),
        "conv": a["conv_odd"][0].reshape(3, 24, P).transpose(2, 1, 0).reshape(P, 72),
        "a_log": rep(a["a_log_odd"][0]),
        "dt_bias": rep(a["dt_bias_odd"][0]),
        "w_ab": rows(np.ascontiguousarray(w_odd[:, 3072:3104]), 32)[0],
    }
    params = np.ascontiguousarray(np.concatenate([par[n] for n in PARAM_W], 1))
    i = np.arange(P)
    dr = i[None, :] // 64 - i[:, None] // 64 + 7
    dc = np.clip(i[None, :] % 64 - i[:, None] % 64, -15, 15) + 15
    nat_bias = np.ascontiguousarray(a["nat_bias"][0][:, dr, dc].transpose(1, 0, 2))
    arrays = {
        "slots": slots, "x_t": x_t, "consts": shape_constants(), "params": params,
        "nat_kc": np.ascontiguousarray(a["cache_nat_k"][0, 0].reshape(P, 4, P).transpose(2, 1, 0)),
        "nat_vc": np.ascontiguousarray(a["cache_nat_v"][0, 0].reshape(P, 512)),
        "diff_kc": np.ascontiguousarray(a["cache_diff_k"][0, 0].reshape(P, 4, P).transpose(2, 1, 0)),
        "diff_vc": np.ascontiguousarray(a["cache_diff_v"][0, 0].reshape(P, 512)),
        "nat_bias": nat_bias, "lam": np.ascontiguousarray(rep(a["diff_lam"][0])),
        "state0": np.ascontiguousarray(a["state_delta"][0, 0].transpose(2, 0, 1, 3)),
    }
    nc = bacc.Bacc("TRN2", target_bir_lowering=False, num_devices=1)
    args = [nc.dram_tensor(n, v.shape, F32, kind="ExternalInput").ap() for n, v in arrays.items()]
    outs = {"y": (2, P, D), "nk": (P, 512), "nv": (P, 512), "dk": (P, 512), "dv": (P, 512), "st": (2, P, HEADS, P)}
    args += [nc.dram_tensor("out_" + n, s, F32, kind="ExternalOutput").ap() for n, s in outs.items()]
    build_program(nc, *args)
    r = run(nc, [arrays], core_ids=[0]).results[0]
    y = r["out_y"]
    return (y[0:1], y[1:2], r["out_nk"].reshape(1, 1, 128, 8, 64), r["out_nv"].reshape(1, 1, 128, 8, 64),
            r["out_dk"].reshape(1, 1, 128, 4, 2, 64), r["out_dv"].reshape(1, 1, 128, 4, 128),
            r["out_st"].transpose(0, 2, 1, 3).reshape(1, 1, 2, 8, 128, 128))
```

```python
from contextlib import ExitStack
import math

import concourse.bass as bass
from concourse import mybir

P = 128
D = 1024
KC = D // P
T = 256
SLOT = 4096
RING = 6
DEPTH = 2
N_EXP = 16
FF = 512
FC = FF // P
HEADS = 8
ADA_A, EIN0, ADA_B, EOUT0, MOE0, OIN0, ADA_C, OOUT0, MOE1, N_SLOTS = 0, 4, 10, 22, 24, 72, 80, 88, 90, 138
SLOTS_FIRST, SLOTS_EVEN, SLOTS_ODD = 4, 12, 8
CAP = 128
ALPHA = (2 * DEPTH) ** 0.25
EPS = 1e-5
LEVELS = 7
BIG = 1e30

F32 = mybir.dt.float32
ALU = mybir.AluOpType
ACT = mybir.ActivationFunctionType
AX = mybir.AxisListType.X

CONST_W = {}
_at = 0
for _n, _w in (("ident", 128), ("mean", 128), ("le", 128), ("gt", 128), ("ge", 128), ("lt", 128),
               ("level", 2 * LEVELS * 128), ("iota", 128), ("rank4", 4), ("rank16", 16)):
    CONST_W[_n] = (_at, _at + _w)
    _at += _w
N_CONST = _at
EVEN_W = {"rope_c": (0, 64), "rope_s": (64, 128), "window": (128, 256)}
PARAM_W = {}
_at = 0
for _n, _w in (("cond", KC * 2), ("ada_b", 192), ("ln_g", 4 * 16), ("ln_b", 4 * 16), ("router", KC * 16),
               ("router_b", 16), ("subln", 1), ("onorm", 1), ("conv", 24 * 3), ("a_log", 16),
               ("dt_bias", 16), ("w_ab", KC * 32)):
    PARAM_W[_n] = (_at, _at + _w)
    _at += _w
N_PARAM = _at


def build_program(nc, slots, x_t, consts, even_consts, params, nat_kc, nat_vc, diff_kc, diff_vc, nat_bias, lam_in, state0,
                  y_out, nk_out, nv_out, dk_out, dv_out, st_out):
    ctx = ExitStack()
    with ctx:
        def sb(name, shape):
            return ctx.enter_context(nc.sbuf_tensor(name, shape, F32))

        ring = sb("ring", [P, RING, SLOT])
        res = sb("res", [P, KC, T])
        act_t = sb("act_t", [P, KC, T])
        cst = sb("cst", [P, N_CONST])
        par = sb("par", [P, N_PARAM])
        mod = sb("mod", [P, 192])
        small = sb("small", [P, 680])
        arena = sb("arena", [P, 17408])

        flags = ctx.enter_context(nc.sbuf_tensor("flags", [P, N_EXP], mybir.dt.int32))
        ada_row = sb("ada_row", [2, 512])
        bank = [ctx.enter_context(nc.psum_tensor(f"bank{i}", [P, 512], F32)) for i in range(8)]

        def c_(name):
            a, b = CONST_W[name]
            return cst[:, a:b]

        def ec_(name):
            a, b = EVEN_W[name]
            return even_c[:, a:b]

        def p_(name):
            a, b = PARAM_W[name]
            return par[:, a:b]

        ident = c_("ident")
        sems = {}

        def S(name):
            if name not in sems:
                sems[name] = ctx.enter_context(nc.semaphore(name))
            return sems[name]

        slot_full = [S(f"slot_full{k}") for k in range(RING)]
        slot_free = [S(f"slot_free{k}") for k in range(RING)]

        mod_v = mod[:, :].rearrange("p (l j c s) -> p l j c s", l=DEPTH, j=6, c=KC)

        def gate_col(l, j, c, s):
            i = ((l * 6 + j) * KC + c) * 2 + s
            return mod[:, i:i + 1]

        s_at = [0]

        def take(n):
            s_at[0] += n
            assert s_at[0] <= 680
            return small[:, s_at[0] - n:s_at[0]]

        cond_t = take(16)
        mod_g = take(48)
        mod_b = take(48)
        ln_scaled = take(128)
        lam_w = take(8)
        sub_g = take(1)
        phases_at = s_at[0]
        mx = take(32)
        sums = take(32)
        rsum = take(32)
        nlr = take(1)
        rms = take(8)
        s_at[0] = phases_at
        scores, biased, r_a, r_b = take(32), take(32), take(32), take(32)
        posm = take(32)
        posm2 = take(32)
        gate_es = take(32)
        masked, oh1, oh2, gates = take(32), take(32), take(32), take(32)
        g8a, g8b, g8c = take(16), take(16), take(16)
        g2, w2 = take(8), take(8)
        s_at[0] = phases_at
        sp_x, sp_a, sp_b, g_tok, beta, nbeta, egc, kdec = (take(32) for _ in range(8))
        negA = take(16)
        qk_ss = take(32)
        o_ss = take(16)
        ab_raw = take(64)
        rstd = arena[:, 0:T]
        o_d = sb("o_delta", [P, 2, 1024])

        a_at = [0]

        def ar(n, reset=False):
            if reset:
                a_at[0] = 0
            a_at[0] += n
            assert a_at[0] <= 17408, a_at[0]
            return arena[:, a_at[0] - n:a_at[0]]

        qkv = ar(6144, True).rearrange("p (s n) -> p s n", s=2)
        heads_t = ar(4096).rearrange("p (w s c n) -> p w s c n", w=4, s=2, c=4)
        nkc = ar(512).rearrange("p (c n) -> p c n", c=4)
        nvc = ar(512)
        dkc = ar(512).rearrange("p (c n) -> p c n", c=4)
        dvc = ar(512)
        bias = ar(1024).rearrange("p (h n) -> p h n", h=8)
        probs = ar(1024).rearrange("p (b j n) -> p b j n", b=2, j=2)
        probs_t = ar(1024).rearrange("p (b j n) -> p b j n", b=2, j=2)
        o_tok = ar(2048).rearrange("p (s n) -> p s n", s=2)
        lam_p = o_tok[:, 0, 0:256]
        even_c = o_tok[:, 0, 256:512]
        rope_1 = probs.rearrange("p b j n -> p (b j n)")[:, 0:512]
        rope_2 = probs.rearrange("p b j n -> p (b j n)")[:, 512:1024]
        o_sq = qkv[:, 0, 0:1024]

        yacc = ar(2048, True).rearrange("p (c n) -> p c n", c=KC)
        h_tok = ar(2048).rearrange("p (s n) -> p s n", s=2)
        xg = ar(2048).rearrange("p (c n) -> p c n", c=KC)
        sel = ar(512).rearrange("p (q n) -> p q n", q=4)
        gsel = ar(512).rearrange("p (q n) -> p q n", q=4)
        gate_t = ar(512)
        sg = ar(512)
        he = ar(512)
        he_t = ar(512)
        y_e = ar(1024)
        sel1 = ar(256).rearrange("p (s n) -> p s n", s=2)
        gsel1 = ar(256).rearrange("p (s n) -> p s n", s=2)
        xg1 = ar(1024).rearrange("p (c n) -> p c n", c=KC)
        gate_t1 = ar(256)
        y_e1 = ar(1024)
        y_tok = arena[:, 0:2048].rearrange("p (s n) -> p s n", s=2)

        dqkv = ar(6144, True).rearrange("p (s n) -> p s n", s=2)
        dgate = ar(2048).rearrange("p (s n) -> p s n", s=2)
        qk_t = ar(4096).rearrange("p (w s h n) -> p w s h n", w=2, s=2, h=HEADS)
        work_at = a_at[0]
        zpad = ar(3 * 260).rearrange("p (b s n) -> p b s n", b=3, s=2)
        conv_o = ar(3 * 256).rearrange("p (b s n) -> p b s n", b=3, s=2)
        a_at[0] = work_at
        dsq = ar(2048)
        a_at[0] = work_at
        sets = []
        for _ in range(2):
            sets.append({n: None for n in ("X", "XT", "LT", "LM", "Y", "AT", "DT")})
        for n in ("X", "XT", "LT", "LM", "Y"):
            for w in sets:
                w[n] = ar(512).rearrange("p (h n) -> p h n", h=4)
        free_q = [dqkv[:, 0, 0:1024], dqkv[:, 1, 0:1024]]
        for w, f in zip(sets, free_q):
            w["AT"] = f[:, 0:512].rearrange("p (h n) -> p h n", h=4)
            w["DT"] = f[:, 512:1024].rearrange("p (h n) -> p h n", h=4)
        st_stage = dqkv[:, 1, 1024:2048].rearrange("p (b h n) -> p b h n", b=2, h=4)
        s0 = act_t[:, :, :].rearrange("p c n -> p (c n)").rearrange("p (d h n) -> p d h n", d=2, h=HEADS)

        def bcast(ap, n):
            return ap.unsqueeze(2).to_broadcast([ap.shape[0], ap.shape[1], n])

        block = ctx.enter_context(nc.Block())

        class Chain:

            def __init__(self, eng, name):
                self.eng, self.sem, self.n, self.off = eng, S(name), 0, None

            def link(self, ins):
                ins.then_inc(self.sem, 1)
                self.n += 1
                self.eng.wait_ge(self.sem, self.n if self.off is None else self.off + self.n)

            def enter(self, i, per):
                self.off = i * per
                self.mark = self.n
                self.per = per

            def leave(self, times):
                assert self.n - self.mark == self.per, self.n - self.mark
                self.off = None
                self.n = self.mark + times * self.per

        meet_n = {}

        def meet(eng, name):
            meet_n[name] = meet_n.get(name, 0) + 1
            eng.drain().then_inc(S("phase_done"), 1)
            eng.wait_ge(S("phase_done"), 4 * meet_n[name])

        def at_ring(n0, off=0):
            return (n0 + off) % RING, (n0 + off) // RING

        def wait_slot(eng, n0, off=0, turns=None):
            k, t = at_ring(n0, off)
            if turns is None:
                eng.wait_ge(slot_full[k], 16 * (t + 1))
            else:
                eng.wait_ge(slot_full[k], turns * 16 + 16 * (t + 1))
            return k

        def ada_rows(pe, n0, q, job, bk):
            k = wait_slot(pe, n0, q)
            w = ring[:, k, :].rearrange("p (c n) -> p c n", c=KC)
            if job >= 1:
                pe.wait_ge(S("ada_stored"), job)
            for c in range(KC):
                last = pe.matmul(bk[0:2, :], cond_t[:, 2 * c:2 * c + 2], w[:, c, :], start=(c == 0), stop=(c == KC - 1))
            last.then_inc(S("ada_rows"), 1)

        def ada_columns(pe, job, bk):
            pe.wait_ge(S("ada_copied"), job + 1)
            for m in range(4):
                last = pe.transpose(bk[:, 2 * m:2 * m + 2], ada_row[0:2, m * P:(m + 1) * P], ident[0:2, 0:2])
            last.then_inc(S("ada_columns"), 1)

        def ada_copy(act, n0, q, job, bk):
            act.wait_ge(S("ada_rows"), job + 1)
            act.activation(ada_row[:, :], bk[0:2, :], ACT.Copy).then_inc(S("ada_copied"), 1)
            act.sem_inc(slot_free[at_ring(n0, q)[0]], 1)

        def ada_store(dve, job, bk):
            dve.wait_ge(S("ada_columns"), job + 1)
            sl = slice(8 * job, 8 * job + 8)
            dve.tensor_tensor(mod[:, sl], bk[:, 0:8], p_("ada_b")[:, sl], ALU.add).then_inc(S("ada_stored"), 1)

        def fold_norm(dve, ch, site, l, j):
            sl = slice(site * 16, site * 16 + 16)
            shift, scale = (mod_v[:, l, j + i].rearrange("p c s -> p (c s)") for i in range(2))
            ch.link(dve.tensor_scalar(scale, scale, 1.0, None, ALU.add))
            ch.link(dve.tensor_tensor(mod_g[:, sl], p_("ln_g")[:, sl], scale, ALU.mult))
            ch.link(dve.tensor_tensor(mod_b[:, sl], p_("ln_b")[:, sl], scale, ALU.mult))
            ch.link(dve.tensor_tensor(mod_b[:, sl], mod_b[:, sl], shift, ALU.add))

        def ln_pe(pe, site):
            for half, (name, src) in enumerate((("ln_mean", res), ("ln_var", act_t))):
                if half == 1:
                    pe.wait_ge(S("ln_sq"), site + 1)
                for c in range(KC):
                    last = pe.matmul(bank[6 + half][:, 0:T], c_("mean"), src[:, c, :], start=(c == 0), stop=(c == KC - 1))
                last.then_inc(S(name), 1)

        def ln_act(act, ch, site):
            act.wait_ge(S("ln_centred"), site + 1)
            act.activation(act_t[:, :, :], res[:, :, :], ACT.Square).then_inc(S("ln_sq"), 1)
            act.wait_ge(S("ln_eps"), site + 1)
            t = rstd[:, 0:T]
            ch.link(act.activation(t, t, ACT.Ln))
            act.activation(t, t, ACT.Exp, scale=-0.5).then_inc(S("ln_rstd"), 1)

        def ln_dve(dve, ch, site):
            dve.wait_ge(S("ln_mean"), site + 1)
            mean = bank[6][:, 0:T].unsqueeze(1).to_broadcast([P, KC, T])
            dve.tensor_tensor(res[:, :, :], res[:, :, :], mean, ALU.subtract).then_inc(S("ln_centred"), 1)
            dve.wait_ge(S("ln_var"), site + 1)
            t = rstd[:, 0:T]
            dve.tensor_scalar(t, bank[7][:, 0:T], EPS, None, ALU.add).then_inc(S("ln_eps"), 1)
            dve.wait_ge(S("ln_rstd"), site + 1)
            dve.wait_ge(S("ln_centred"), site + 1)
            dve.tensor_tensor(res[:, :, :], res[:, :, :], t.unsqueeze(1).to_broadcast([P, KC, T]),
                              ALU.mult).then_inc(S("ln_norm"), 1)
            if site < 3:
                dve.wait_ge(S("ln_norm"), site + 1)
                rv = res[:, :, :].rearrange("p c (s n) -> p (c s) n", s=2)
                av = act_t[:, :, :].rearrange("p c (s n) -> p (c s) n", s=2)
                gm = mod_g[:, site * 16:site * 16 + 16]
                bm = mod_b[:, site * 16:site * 16 + 16]
                ch.link(dve.tensor_tensor(av, rv, bcast(gm, P), ALU.mult))
                dve.tensor_tensor(av, av, bcast(bm, P), ALU.add).then_inc(S("ln_h"), 1)

        def ln_pool(pool, ch, site):
            pool.wait_ge(S("ln_norm"), site + 1)
            if site < 3:
                pool.wait_ge(S("ln_h"), site + 1)
            for c in range(KC):
                i = site * 16 + 2 * c
                last = pool.tensor_scalar(res[:, c, :], res[:, c, :], ln_scaled[:, 0 + i:i + 1],
                                          ln_scaled[:, 64 + i:65 + i], ALU.mult, ALU.add)
            ch.link(last)


        N_R2 = 19

        def nth(i, n):
            return n if i is None else 2 * i + n

        def second_round(eng, i, n, layer, body, skipped=None):
            e = slice(n, n + 1) if i is None else bass.ds(2 * i + n, 1)
            count = eng.value_load(flags[0:1, e], min_val=0, max_val=T)
            with eng.If(count > CAP):
                body(nth(i, n) * N_R2 + 16 * N_R2 * layer)
            if skipped is not None:
                with eng.Else():
                    skipped()

        def transposes(pe, bk, srcs):
            for j, src in enumerate(srcs):
                last = pe.transpose(bk[:, j * P:(j + 1) * P], src, ident)
            return last

        def copied(x, k, layer):
            return 7 * x + (4 + k + 1 + 56 * layer)

        def moe_pe(pe, layer, n0):
            L = layer
            for s in range(2):
                for c in range(KC):
                    last = pe.matmul(bank[0][:, s * 16:s * 16 + 16], act_t[:, c, s * P:(s + 1) * P],
                                     p_("router")[:, c * 16:c * 16 + 16], start=(c == 0), stop=(c == KC - 1))
            last.then_inc(S("logits"), 1)
            for n in range(4):
                s, q = n // 2, n % 2
                transposes(pe, bank[2 + n], [act_t[:, 4 * q + j, s * P:(s + 1) * P] for j in range(4)])\
                    .then_inc(S("htok_done"), 1)
            pe.wait_ge(S("gates_ready"), L + 1)
            pe.matmul(bank[0][:, 0:16], c_("lt"), oh1[:, 0:16], start=True, stop=True)
            pe.matmul(bank[0][:, 16:32], c_("lt"), oh1[:, 16:32], start=True, stop=False)
            for m in ("le", "gt"):
                pe.matmul(bank[0][:, 16:32], c_(m), oh1[:, 0:16], start=False, stop=(m == "gt"))
            for k, (m, s) in enumerate((("le", 0), ("gt", 0), ("le", 1), ("gt", 1))):
                last = pe.matmul(bank[0][:, 32:48], c_(m), oh1[:, s * 16:s * 16 + 16], start=(k == 0), stop=(k == 3))
            last.then_inc(S("rank_done"), 1)
            pe.wait_ge(S("htok_copied"), 4 * (L + 1))
            pe.wait_ge(S("flags_ready"), L + 1)

            def gather(x, b, wait):
                if wait is not None:
                    pe.wait_ge(S("misc_copied"), wait)
                for o in range(2):
                    for s in range(2):
                        last = pe.matmul(bank[5 - b % 2][:, o * T:(o + 1) * T], h_tok[:, s, (2 * b + o) * P:(2 * b + o + 1) * P],
                                         sel.rearrange("p (e s) n -> p e s n", s=2)[:, :, s, :], start=(s == 0), stop=(s == 1))
                last.then_inc(S("misc_done"), 1)

            def gate_up(i, n):
                for m in range(2):
                    k = wait_slot(pe, n0, 3 * n + m, i)
                    w = ring[:, k, :].rearrange("p (c n) -> p c n", c=KC)
                    for c in range(KC):
                        last = pe.matmul(bank[m][:, :], xg[:, c, (n % 2) * P:(n % 2 + 1) * P], w[:, c, :],
                                         start=(c == 0), stop=(c == KC - 1))
                last.then_inc(S("gu_done"), 1)

            def he_transpose(i, n, x, k):
                pe.wait_ge(S("he_ready"), nth(i, n) + (1 + 16 * L))
                pe.wait_ge(S("misc_copied"), copied(x, k - 2 if k else -1, L))
                transposes(pe, bank[4], [he[:, f * P:(f + 1) * P] for f in range(FC)]).then_inc(S("misc_done"), 1)

            def down(i, n, x, k):
                slot = wait_slot(pe, n0, 3 * n + 2, i)
                w = ring[:, slot, :].rearrange("p (f n) -> p f n", f=FC)
                pe.wait_ge(S("misc_copied"), copied(x, k, L))
                for h in range(2):
                    for f in range(FC):
                        last = pe.matmul(bank[2 + h][:, :], he_t[:, f * P:(f + 1) * P], w[:, f, h * 512:(h + 1) * 512],
                                         start=(f == 0), stop=(f == FC - 1))
                    last.then_inc(S("y_done"), 1)

            def scatter(i, n, x):
                pe.wait_ge(S("y_copied"), 2 * nth(i, n) + (2 + 32 * L))
                if n % 2 == 0:
                    pe.wait_ge(S("misc_copied"), copied(x, 1, L))
                for b in range(4):
                    pe.wait_ge(S("sc_free"), 4 * nth(i, n) + (b + 1 + 66 * L))
                    for o in range(2):
                        oc = 2 * b + o
                        last = pe.matmul(bank[6 + b % 2][:, o * T:(o + 1) * T], y_e[:, oc * P:(oc + 1) * P],
                                         gate_t[:, (n % 2) * T:(n % 2 + 1) * T], start=True, stop=True)
                    last.then_inc(S("sc_done"), 1)

            def round2(i, n, x, k):
                def body(base):
                    pe.wait_ge(S("y_copied"), 2 * nth(i, n) + (2 + 32 * L))
                    pe.wait_ge(S("sc_free"), 4 * nth(i, n) + (2 + 66 * L))
                    pe.wait_ge(S("misc_copied"), copied(x, k, L))
                    pe.wait_ge(S("round2"), base + 2)
                    for b in range(2):
                        for o in range(4):
                            for s in range(2):
                                c = 4 * b + o
                                pe.matmul(bank[4 + b][:, o * P:(o + 1) * P], h_tok[:, s, c * P:(c + 1) * P],
                                          sel1[:, s, :], start=(s == 0), stop=(s == 1))
                    transposes(pe, bank[0], [gsel1[:, s, :] for s in range(2)]).then_inc(S("round2"), 1)
                    pe.wait_ge(S("round2"), base + 6)
                    for m in range(2):
                        w = ring[:, (3 * n + m + n0) % RING, :].rearrange("p (c n) -> p c n", c=KC)
                        for c in range(KC):
                            last = pe.matmul(bank[m][:, :], xg1[:, c, :], w[:, c, :], start=(c == 0), stop=(c == KC - 1))
                    last.then_inc(S("round2"), 1)
                    pe.wait_ge(S("round2"), base + 9)
                    transposes(pe, bank[4], [he[:, f * P:(f + 1) * P] for f in range(FC)]).then_inc(S("round2"), 1)
                    pe.wait_ge(S("round2"), base + 11)
                    w = ring[:, (3 * n + 2 + n0) % RING, :].rearrange("p (f n) -> p f n", f=FC)
                    for h in range(2):
                        for f in range(FC):
                            last = pe.matmul(bank[2 + h][:, :], he_t[:, f * P:(f + 1) * P], w[:, f, h * 512:(h + 1) * 512],
                                             start=(f == 0), stop=(f == FC - 1))
                    last.then_inc(S("round2"), 1)
                    pe.wait_ge(S("round2"), base + 14)
                    for b in range(4):
                        for o in range(2):
                            oc = 2 * b + o
                            last = pe.matmul(bank[4 + b][:, o * T:(o + 1) * T], y_e1[:, oc * P:(oc + 1) * P], gate_t1,
                                             start=True, stop=True)
                    last.then_inc(S("round2"), 1)
                second_round(pe, i, n, L, body)
                pe.wait_ge(S("round2"), nth(i, n) * N_R2 + (N_R2 + 16 * N_R2 * L))

            pe.wait_ge(S("sel_ready"), 1 + 8 * L)
            for b in range(4):
                gather(0, b, None if b < 2 else b - 1 + 56 * L)
            pe.wait_ge(S("misc_copied"), copied(0, -1, L))
            gate_up(None, 0)

            def pair(i, x, n, last_pair):
                he_transpose(i, n, x, 0)
                pe.wait_ge(S("gsel_ready"), x + (1 + 8 * L))
                pe.wait_ge(S("misc_copied"), copied(x, -2, L))
                transposes(pe, bank[5], [gsel[:, q, :] for q in range(4)]).then_inc(S("misc_done"), 1)
                down(i, n, x, 0)
                round2(i, n, x, 1)
                pe.wait_ge(S("he_ready"), nth(i, n) + (1 + 16 * L))
                gate_up(i, n + 1)
                scatter(i, n, x)
                he_transpose(i, n + 1, x, 2)
                if not last_pair:
                    pe.wait_ge(S("sel_ready"), x + (2 + 8 * L))
                    for b in range(4):
                        gather(x + 1, b, copied(x, 1 + b, L))
                down(i, n + 1, x, 2)
                round2(i, n + 1, x, 2 if last_pair else 6)
                if not last_pair:
                    pe.wait_ge(S("he_ready"), nth(i, n) + (2 + 16 * L))
                    pe.wait_ge(S("misc_copied"), copied(x, 6, L))
                    gate_up(i, n + 2)
                scatter(i, n + 1, x)

            with pe.Fori(0, 7) as i:
                pair(i, i, 0, False)
            pair(None, 7, 14, True)

        def moe_act(act, ch, layer, n0):
            L = layer
            act.wait_ge(S("logits"), L + 1)
            act.activation(scores, bank[0][:, 0:32], ACT.Exp, scale=-1.0).then_inc(S("sig_exp"), 1)
            for n in range(4):
                s, q = n // 2, n % 2
                act.wait_ge(S("htok_done"), 4 * L + n + 1)
                act.activation(h_tok[:, s, q * 512:(q + 1) * 512], bank[2 + n][:, :], ACT.Copy).then_inc(S("htok_copied"), 1)
            act.wait_ge(S("flags_ready"), L + 1)

            def misc(x, k, dst, src):
                act.wait_ge(S("misc_done"), copied(x, k, L))
                act.activation(dst, src, ACT.Copy).then_inc(S("misc_copied"), 1)

            def xg_part(b):
                return xg[:, 2 * b:2 * b + 2, :], bank[5 - b % 2][:, :].rearrange("p (c n) -> p c n", c=2)

            def silu(i, n):
                act.wait_ge(S("gu_done"), nth(i, n) + (1 + 16 * L))
                act.activation(sg, bank[0][:, :], ACT.Silu).then_inc(S("silu_done"), 1)

            def y_copy(i, n):
                for h in range(2):
                    act.wait_ge(S("y_done"), 2 * nth(i, n) + (h + 1 + 32 * L))
                    act.activation(y_e[:, h * 512:(h + 1) * 512], bank[2 + h][:, :], ACT.Copy).then_inc(S("y_copied"), 1)

            def round2(i, n):
                def body(base):
                    act.wait_ge(S("round2"), base + 3)
                    for b in range(2):
                        act.activation(xg1[:, 4 * b:4 * b + 4, :], bank[4 + b][:, :].rearrange("p (c n) -> p c n", c=4),
                                       ACT.Copy).then_inc(S("round2"), 1)
                    act.activation(gate_t1, bank[0][:, 0:T], ACT.Copy).then_inc(S("round2"), 1)
                    act.wait_ge(S("round2"), base + 7)
                    act.activation(sg, bank[0][:, :], ACT.Silu).then_inc(S("round2"), 1)
                    act.wait_ge(S("round2"), base + 10)
                    act.activation(he_t, bank[4][:, :], ACT.Copy).then_inc(S("round2"), 1)
                    act.wait_ge(S("round2"), base + 12)
                    for h in range(2):
                        act.activation(y_e1[:, h * 512:(h + 1) * 512], bank[2 + h][:, :], ACT.Copy)\
                            .then_inc(S("round2"), 1)
                second_round(act, i, n, L, body)
                for m in range(3):
                    act.sem_inc(slot_free[at_ring(n0, 3 * n + m)[0]], 1)

            for b in range(4):
                misc(0, b - 4, *xg_part(b))
            silu(None, 0)

            def pair(i, x, n, last_pair):
                misc(x, 0, he_t, bank[4][:, :])
                misc(x, 1, gate_t, bank[5][:, :])
                y_copy(i, n)
                round2(i, n)
                silu(i, n + 1)
                misc(x, 2, he_t, bank[4][:, :])
                if not last_pair:
                    for b in range(4):
                        misc(x, 3 + b, *xg_part(b))
                y_copy(i, n + 1)
                round2(i, n + 1)
                if not last_pair:
                    silu(i, n + 2)

            with act.Fori(0, 7) as i:
                pair(i, i, 0, False)
            pair(None, 7, 14, True)

        def moe_dve(dve, ch, layer, n0):
            L = layer
            j0 = 3
            dve.memset(yacc, 0.0).then_inc(S("yacc_zero"), 1)
            dve.wait_ge(S("sig_exp"), L + 1)
            ch.link(dve.tensor_scalar(scores, scores, 1.0, None, ALU.add))
            ch.link(dve.reciprocal(scores, scores))
            sv = scores.rearrange("p (s e) -> p s e", s=2)
            ch.link(dve.tensor_tensor(biased.rearrange("p (s e) -> p s e", s=2), sv,
                                      p_("router_b").unsqueeze(1).to_broadcast([P, 2, 16]), ALU.add))
            bv = biased.rearrange("p (g k) -> p g k", k=4)
            a8 = g8a.rearrange("p (g k) -> p g k", k=2)
            b8 = g8b.rearrange("p (g k) -> p g k", k=2)
            dve.tensor_tensor(a8, bv[:, :, 0:2], bv[:, :, 2:4], ALU.max).then_inc(S("dve_par"), 1)
            dve.tensor_tensor(b8, bv[:, :, 0:2], bv[:, :, 2:4], ALU.min).then_inc(S("dve_par"), 1)
            dve.wait_ge(S("dve_par"), 2 * L + 2)
            c8 = g8c.rearrange("p (g k) -> p g k", k=2)
            ch.link(dve.tensor_tensor(c8[:, :, 0], a8[:, :, 0], a8[:, :, 1], ALU.max))
            ch.link(dve.tensor_tensor(c8[:, :, 1], a8[:, :, 0], a8[:, :, 1], ALU.min))
            ch.link(dve.tensor_tensor(a8[:, :, 0], b8[:, :, 0], b8[:, :, 1], ALU.max))
            ch.link(dve.tensor_tensor(a8[:, :, 1], a8[:, :, 0], c8[:, :, 1], ALU.max))
            ch.link(dve.tensor_tensor(b8[:, :, 0], a8[:, :, 1], c8[:, :, 0], ALU.add))

            def first_best(dst, src, n, rank, top, tmp):
                sv_ = src.rearrange("p (s n) -> p s n", s=2)
                tv, dv_ = tmp.rearrange("p (s n) -> p s n", s=2), dst.rearrange("p (s n) -> p s n", s=2)
                ch.link(dve.tensor_reduce(top, sv_, AX, ALU.max))
                ch.link(dve.tensor_tensor(tv, sv_, bcast(top, n), ALU.is_equal))
                ch.link(dve.tensor_tensor(tv, tv, rank.unsqueeze(1).to_broadcast([P, 2, n]), ALU.mult))
                ch.link(dve.tensor_reduce(top, tv, AX, ALU.max))
                ch.link(dve.tensor_tensor(dv_, tv, bcast(top, n), ALU.is_equal))

            gsc = g8c[:, 8:16]
            ch.link(dve.tensor_copy(gsc, b8[:, :, 0]))
            first_best(g2, gsc, 4, c_("rank4"), w2[:, 0:2], g8a[:, 0:8])
            in_group = g2.unsqueeze(2).to_broadcast([P, 8, 4])
            rv = r_a.rearrange("p (g k) -> p g k", k=4)
            ch.link(dve.tensor_tensor(rv, bv, in_group, ALU.mult))
            ch.link(dve.tensor_scalar(g8b[:, 0:8], g2, BIG, -BIG, ALU.mult, ALU.add))
            ch.link(dve.tensor_tensor(masked.rearrange("p (g k) -> p g k", k=4), rv,
                                      bcast(g8b[:, 0:8], 4), ALU.add))
            first_best(oh1, masked, 16, c_("rank16"), w2[:, 0:2], r_b)
            ch.link(dve.scalar_tensor_tensor(masked, oh1, -3.0 * BIG, masked, ALU.mult, ALU.add))
            first_best(oh2, masked, 16, c_("rank16"), w2[:, 0:2], r_b)
            ch.link(dve.tensor_tensor(oh1, oh1, oh2, ALU.add))
            ch.link(dve.tensor_tensor(r_a, oh1, scores, ALU.mult))
            ch.link(dve.tensor_reduce(w2[:, 2:4], r_a.rearrange("p (s e) -> p s e", s=2), AX, ALU.add))
            ch.link(dve.reciprocal(w2[:, 4:6], w2[:, 2:4]))
            dve.tensor_tensor(gates.rearrange("p (s e) -> p s e", s=2), r_a.rearrange("p (s e) -> p s e", s=2),
                              bcast(w2[:, 4:6], 16), ALU.mult).then_inc(S("gates_ready"), 1)
            dve.wait_ge(S("rank_done"), L + 1)
            pv_ = posm.rearrange("p (e s) -> p s e", s=2)
            ch.link(dve.scalar_tensor_tensor(pv_, bank[0][:, 0:32].rearrange("p (s e) -> p s e", s=2), 1.0,
                                             oh1.rearrange("p (s e) -> p s e", s=2), ALU.add, ALU.mult))
            ch.link(dve.tensor_scalar(posm, posm, -1.0, None, ALU.add))
            ch.link(dve.tensor_scalar(posm2, posm, -float(CAP), None, ALU.add))
            ch.link(dve.tensor_copy(gate_es.rearrange("p (e s) -> p s e", s=2), gates.rearrange("p (s e) -> p s e", s=2)))
            dve.tensor_copy(flags[:, :], bank[0][:, 32:48]).then_inc(S("flags_ready"), 1)
            dve.wait_ge(S("flags_ready"), L + 1)
            dve.wait_ge(S("yacc_zero"), L + 1)
            dve.sem_inc(S("sc_free"), 2)

            def quad(x):
                return slice(4 * x, 4 * x + 4) if isinstance(x, int) else bass.ds(4 * x, 4)

            def take_slots(x):
                dve.tensor_tensor(sel, c_("iota").unsqueeze(1).to_broadcast([P, 4, P]), bcast(posm[:, quad(x)], P),
                                  ALU.is_equal).then_inc(S("sel_ready"), 1)

            def take_gates(x, own):
                dve.wait_ge(S("sel_ready"), own + 8 * L)
                dve.tensor_tensor(gsel, sel, bcast(gate_es[:, quad(x)], P), ALU.mult).then_inc(S("gsel_ready"), 1)

            def he_product(i, n):
                dve.wait_ge(S("silu_done"), nth(i, n) + (1 + 16 * L))
                dve.tensor_tensor(he, sg, bank[1][:, :], ALU.mult).then_inc(S("he_ready"), 1)

            def add_y(i, n):
                for b in range(4):
                    base = 4 * nth(i, n)
                    dve.wait_ge(S("sc_done"), base + (b + 1 + 64 * L))
                    dve.wait_ge(S("sc_free"), base + (b + 1 + 66 * L))
                    yv = yacc[:, 2 * b:2 * b + 2, :]
                    dve.tensor_tensor(yv, yv, bank[6 + b % 2][:, :].rearrange("p (o n) -> p o n", o=2),
                                      ALU.add).then_inc(S("sc_free"), 1)

            def round2(i, n):
                def body(base):
                    two = slice(2 * n, 2 * n + 2) if i is None else bass.ds(4 * i + 2 * n, 2)
                    dve.tensor_tensor(sel1, c_("iota").unsqueeze(1).to_broadcast([P, 2, P]), bcast(posm2[:, two], P),
                                      ALU.is_equal).then_inc(S("round2"), 1)
                    dve.wait_ge(S("round2"), base + 1)
                    dve.tensor_tensor(gsel1, sel1, bcast(gate_es[:, two], P), ALU.mult).then_inc(S("round2"), 1)
                    dve.wait_ge(S("round2"), base + 8)
                    dve.tensor_tensor(he, sg, bank[1][:, :], ALU.mult).then_inc(S("round2"), 1)
                    dve.wait_ge(S("sc_free"), 4 * nth(i, n) + (2 + 66 * L))
                    for b in range(4):
                        dve.wait_ge(S("round2"), base + 15)
                        yv = yacc[:, 2 * b:2 * b + 2, :]
                        dve.tensor_tensor(yv, yv, bank[4 + b][:, :].rearrange("p (o n) -> p o n", o=2),
                                          ALU.add).then_inc(S("round2"), 1)
                second_round(dve, i, n, L, body, lambda: dve.sem_inc(S("round2"), N_R2))
                dve.wait_ge(S("round2"), nth(i, n) * N_R2 + (N_R2 + 16 * N_R2 * L))

            take_slots(0)
            take_gates(0, 1)
            he_product(None, 0)

            def pair(i, x, n, last_pair):
                round2(i, n)
                if not last_pair:
                    dve.wait_ge(S("gsel_ready"), x + (1 + 8 * L))
                    take_slots(x + 1)
                he_product(i, n + 1)
                add_y(i, n)
                if not last_pair:
                    take_gates(x + 1, x + 2)
                round2(i, n + 1)
                if not last_pair:
                    he_product(i, n + 2)
                add_y(i, n + 1)

            with dve.Fori(0, 7) as i:
                pair(i, i, 0, False)
            pair(None, 7, 14, True)
            dve.wait_ge(S("sc_free"), 66 * (L + 1))
            gv = mod_v[:, layer, 5].rearrange("p c s -> p (c s)")
            yv = yacc.rearrange("p c (s n) -> p (c s) n", s=2)
            rv = res[:, :, :].rearrange("p c (s n) -> p (c s) n", s=2)
            ch.link(dve.tensor_tensor(yv, yv, bcast(gv, P), ALU.mult))
            ch.link(dve.tensor_tensor(rv, rv, yv, ALU.add))

        def out_pe(pe, layer, n0):
            for q in range(2):
                k = wait_slot(pe, n0, q)
                w = ring[:, k, :].rearrange("p (c n) -> p c n", c=KC)
                for b in range(2):
                    for o in range(2):
                        m = 2 * b + o
                        for c in range(KC):
                            last = pe.matmul(bank[2 * q + b][:, o * T:(o + 1) * T], w[:, c, m * P:(m + 1) * P],
                                             act_t[:, c, :], start=(c == 0), stop=(c == KC - 1))
                    last.then_inc(S("mix_done"), 1)

        def out_dve(dve, ch, layer, n0):
            for q in range(2):
                for b in range(2):
                    dve.wait_ge(S("mix_done"), 4 * layer + 2 * q + b + 1)
                    for o in range(2):
                        for s in range(2):
                            c = 4 * q + 2 * b + o
                            r = res[:, c, s * P:(s + 1) * P]
                            last = dve.scalar_tensor_tensor(r, bank[2 * q + b][:, o * T + s * P:o * T + (s + 1) * P],
                                                            gate_col(layer, 2, c, s), r, ALU.mult, ALU.add)
                dve.sem_inc(slot_free[at_ring(n0, q)[0]], 1)
            ch.link(last)

        BATCHES = [(s, d, hq) for s in range(2) for hq in range(2) for d in range(2)]

        def lev(b2, lv, u):
            return b2 * 2 * (LEVELS - 1) + 2 * (lv - 1) + u + 1

        def delta_pe(pe):
            def tr(i):
                pe.wait_ge(S("conv_done"), i + 1)
                if i >= 2:
                    pe.wait_ge(S("tok_copied"), i - 1)
                for s in range(2):
                    last = pe.transpose(bank[4 + i % 2][:, s * P:(s + 1) * P], conv_o[:, i % 3, s, :], ident)
                last.then_inc(S("tok_done"), 1)

            for i in range(24):
                k = wait_slot(pe, OIN0, i // 4)
                if i >= 3:
                    pe.wait_ge(S("z_copied"), i - 2)
                w = ring[:, k, :].rearrange("p (c n) -> p c n", c=KC)
                for c in range(KC):
                    last = pe.matmul(bank[i % 3][:, 0:T], w[:, c, (i % 4) * P:(i % 4 + 1) * P], act_t[:, c, :],
                                     start=(c == 0), stop=(c == KC - 1))
                last.then_inc(S("z_done"), 1)
                if i >= 2:
                    tr(i - 2)
            tr(22)
            tr(23)
            pe.wait_ge(S("z_copied"), 24)
            for q in range(2):
                k = wait_slot(pe, OIN0, 6 + q)
                w = ring[:, k, :].rearrange("p (c n) -> p c n", c=KC)
                for s in range(2):
                    for c in range(KC):
                        last = pe.matmul(bank[2 * q + s][:, :], act_t[:, c, s * P:(s + 1) * P], w[:, c, :],
                                         start=(c == 0), stop=(c == KC - 1))
                    last.then_inc(S("dg_done"), 1)
            for s in range(2):
                for c in range(KC):
                    last = pe.matmul(bank[6][:, s * 32:s * 32 + 32], act_t[:, c, s * P:(s + 1) * P],
                                     p_("w_ab")[:, c * 32:c * 32 + 32], start=(c == 0), stop=(c == KC - 1))
            last.then_inc(S("ab_done"), 1)
            pe.wait_ge(S("g_ready"), 1)
            gv = g_tok.rearrange("p (s d h) -> p s d h", s=2, d=2)
            for i, (m, d) in enumerate((("le", 0), ("ge", 1), ("gt", 0), ("lt", 1))):
                last = pe.matmul(bank[7][:, i * 16:i * 16 + 16], c_(m), gv[:, :, d, :], start=True, stop=True)
            last.then_inc(S("gsum_done"), 1)
            pe.wait_ge(S("qk_ready"), 1)
            pe.wait_ge(S("dg_copied"), 4)
            for n in range(8):
                w, s, hq = n // 4, (n // 2) % 2, n % 2
                if n >= 4:
                    pe.wait_ge(S("qkt_copied"), n - 3)
                for j in range(4):
                    h = 4 * hq + j
                    last = pe.transpose(bank[n % 4][:, j * P:(j + 1) * P],
                                        dqkv[:, s, w * 1024 + h * P:w * 1024 + (h + 1) * P], ident)
                last.then_inc(S("qkt_done"), 1)
            pe.wait_ge(S("qkt_copied"), 8)
            pe.wait_ge(S("gsum_copied"), 1)
            for b2 in range(4):
                for u in range(2):
                    b = 2 * b2 + u
                    s, d, hq = BATCHES[b]
                    w = sets[u]
                    pe.wait_ge(S("gm_ready"), b + 1)
                    if b >= 2:
                        pe.wait_ge(S("batch_end"), b - 1)
                    pe.matmul(bank[3 * u][:, :], c_("gt") if d == 0 else c_("lt"),
                              w["LM"].rearrange("p h n -> p (h n)"), start=True, stop=True).then_inc(S("diff_done"), 1)
                    for j in range(4):
                        kt = qk_t[:, 1, s, 4 * hq + j, :]
                        pe.matmul(bank[3 * u + 1][:, j * P:(j + 1) * P], kt, kt, start=True, stop=True)
                        last = pe.matmul(bank[3 * u + 2][:, j * P:(j + 1) * P], kt, qk_t[:, 0, s, 4 * hq + j, :],
                                         start=True, stop=True)
                    last.then_inc(S("kk_done"), 1)
                for u in range(2):
                    b = 2 * b2 + u
                    w = sets[u]
                    pe.wait_ge(S("xt0_ready"), b + 1)
                    for j in range(4):
                        last = pe.transpose(bank[3 * u][:, j * P:(j + 1) * P], w["XT"][:, j, :], ident)
                    last.then_inc(S("x0_done"), 1)
                for lv in range(1, LEVELS):
                    if lv in (2, 4):
                        q = 2 * b2 + lv // 2 - 1
                        ada_rows(pe, ADA_C, q, SLOTS_FIRST + SLOTS_EVEN + q, bank[6])
                    if lv in (3, 5):
                        ada_columns(pe, SLOTS_FIRST + SLOTS_EVEN + 2 * b2 + (lv - 1) // 2 - 1, bank[7])
                    for u in range(2):
                        w = sets[u]
                        pe.wait_ge(S("lm_ready"), lev(b2, lv, u))
                        if lv == 1:
                            pe.wait_ge(S("x0_copied"), 2 * b2 + u + 1)
                        else:
                            pe.wait_ge(S("x_summed"), lev(b2, lv - 1, u))
                        for j in range(4):
                            last = pe.matmul(bank[3 * u][:, j * P:(j + 1) * P], w["LM"][:, j, :], w["X"][:, j, :],
                                             start=True, stop=True)
                        last.then_inc(S("ly_done"), 1)
                    for u in range(2):
                        w = sets[u]
                        pe.wait_ge(S("ly_copied"), lev(b2, lv, u))
                        if lv == 1:
                            pe.wait_ge(S("at_ready"), 2 * b2 + u + 1)
                        for j in range(4):
                            last = pe.matmul(bank[3 * u + 1][:, j * P:(j + 1) * P], w["Y"][:, j, :], w["XT"][:, j, :],
                                             start=True, stop=True)
                        if lv < LEVELS - 1:
                            for j in range(4):
                                last = pe.matmul(bank[3 * u + 2][:, j * P:(j + 1) * P], w["XT"][:, j, :], w["Y"][:, j, :],
                                                 start=True, stop=True)
                        last.then_inc(S("dx_done"), 1)
                for u in range(2):
                    b = 2 * b2 + u
                    s, d, hq = BATCHES[b]
                    w = sets[u]
                    if s == 1:
                        pe.wait_ge(S("s0_in"), 16)
                        pe.wait_ge(S("x_summed"), lev(b2, LEVELS - 2, u))
                        for j in range(4):
                            h = 4 * hq + j
                            pe.matmul(bank[3 * u][:, j * P:(j + 1) * P], qk_t[:, 1, s, h, :], s0[:, d, h, :],
                                      start=True, stop=True)
                            last = pe.matmul(bank[3 * u + 2][:, j * P:(j + 1) * P], qk_t[:, 0, s, h, :], s0[:, d, h, :],
                                             start=True, stop=True)
                        last.then_inc(S("ks_done"), 1)
                for u in range(2):
                    b = 2 * b2 + u
                    s, d, hq = BATCHES[b]
                    w = sets[u]
                    pe.wait_ge(S("xt_final"), b + 1)
                    for j in range(4):
                        h = 4 * hq + j
                        r = w["Y"][:, j, :] if s == 1 else dqkv[:, s, 2048 + h * P:2048 + (h + 1) * P]
                        last = pe.matmul(bank[3 * u + 1][:, j * P:(j + 1) * P], w["XT"][:, j, :], r, start=True, stop=True)
                    last.then_inc(S("vn_done"), 1)
                for u in range(2):
                    b = 2 * b2 + u
                    s, d, hq = BATCHES[b]
                    w = sets[u]
                    pe.wait_ge(S("vn_ready"), b + 1)
                    for j in range(4):
                        last = pe.matmul(bank[3 * u][:, j * P:(j + 1) * P], w["AT"][:, j, :], w["X"][:, j, :],
                                         start=True, stop=True)
                    last.then_inc(S("o_done"), 1)
                    if s == 0:
                        pe.wait_ge(S("kd_ready"), b + 1)
                        for j in range(4):
                            h = 4 * hq + j
                            last = pe.matmul(bank[3 * u + 1][:, j * P:(j + 1) * P],
                                             dqkv[:, s, 1024 + h * P:1024 + (h + 1) * P], w["LM"][:, j, :],
                                             start=True, stop=True)
                        last.then_inc(S("st_done"), 1)
            for s in range(2):
                pe.wait_ge(S("do_ready"), s + 1)
                for q in range(2):
                    for j in range(4):
                        c = 4 * q + j
                        last = pe.transpose(bank[2 * s + q][:, j * P:(j + 1) * P],
                                            o_d[:, s, c * P:(c + 1) * P], ident)
                    last.then_inc(S("dot_done"), 1)
            pe.wait_ge(S("dot_copied"), 4)
            pe.wait_ge(S("dot_banks_free"), 1)
            out_pe(pe, 1, OOUT0)


        def delta_act(act, ch):
            ab = ab_raw.rearrange("p (s n) -> p s n", s=2)
            for i in range(24):
                act.wait_ge(S("z_done"), i + 1)
                if i == 0:
                    act.wait_ge(S("pad_zero"), 1)
                if i >= 3:
                    act.wait_ge(S("conv_sum"), i - 2)
                act.activation(zpad[:, i % 3, :, 1:129], bank[i % 3][:, 0:T].rearrange("p (s n) -> p s n", s=2),
                               ACT.Copy).then_inc(S("z_copied"), 1)
                if i % 4 == 3:
                    act.sem_inc(slot_free[at_ring(OIN0, i // 4)[0]], 1)
                if i >= 1:
                    act.wait_ge(S("conv_sum"), i)
                    act.activation(conv_o[:, (i - 1) % 3], conv_o[:, (i - 1) % 3], ACT.Silu).then_inc(S("conv_done"), 1)
            act.wait_ge(S("conv_sum"), 24)
            act.activation(conv_o[:, 23 % 3], conv_o[:, 23 % 3], ACT.Silu).then_inc(S("conv_done"), 1)
            for q in range(2):
                for s in range(2):
                    act.wait_ge(S("dg_done"), 2 * q + s + 1)
                    act.activation(dgate[:, s, q * 512:(q + 1) * 512], bank[2 * q + s][:, :], ACT.Silu)\
                       .then_inc(S("dg_copied"), 1)
                act.sem_inc(slot_free[at_ring(OIN0, 6 + q)[0]], 1)
            act.wait_ge(S("sp_abs"), 1)
            ch.link(act.activation(sp_b, sp_b, ACT.Exp, scale=-1.0))
            act.activation(sp_b, sp_b, ACT.Ln, bias=1.0).then_inc(S("sp_ln"), 1)
            act.activation(beta.rearrange("p (s n) -> p s n", s=2), ab[:, :, 16:32], ACT.Exp, scale=-1.0)\
               .then_inc(S("beta_exp"), 1)
            act.activation(negA, p_("a_log"), ACT.Exp).then_inc(S("a_exp"), 1)
            act.wait_ge(S("qk_ss"), 1)
            ch.link(act.activation(qk_ss, qk_ss, ACT.Ln))
            act.activation(qk_ss, qk_ss, ACT.Exp, scale=-0.5).then_inc(S("qk_rs"), 1)
            act.wait_ge(S("gsum_done"), 1)
            gs = bank[7][:, 0:64].rearrange("p (i s h) -> p i s h", i=4, s=2)
            ev, kv = (x.rearrange("p (s d h) -> p s d h", s=2, d=2) for x in (egc, kdec))
            for i, (dst, d) in enumerate(((ev, 0), (ev, 1), (kv, 0), (kv, 1))):
                last = act.activation(dst[:, :, d, :], gs[:, i], ACT.Exp)
            last.then_inc(S("gsum_copied"), 1)
            act.wait_ge(S("gsum_copied"), 1)
            for n in range(8):
                w, s, hq = n // 4, (n // 2) % 2, n % 2
                act.wait_ge(S("qkt_done"), n + 1)
                act.activation(qk_t[:, w, s, 4 * hq:4 * hq + 4, :], bank[n % 4][:, :].rearrange("p (h n) -> p h n", h=4),
                               ACT.Copy).then_inc(S("qkt_copied"), 1)
            for b2 in range(4):
                for u in range(2):
                    b = 2 * b2 + u
                    w = sets[u]
                    act.wait_ge(S("diff_done"), b + 1)
                    act.activation(w["DT"], bank[3 * u][:, :].rearrange("p (h n) -> p h n", h=4), ACT.Exp)\
                       .then_inc(S("dt_ready"), 1)
                for u in range(2):
                    b = 2 * b2 + u
                    w = sets[u]
                    act.wait_ge(S("x0_done"), b + 1)
                    act.activation(w["X"], bank[3 * u][:, :].rearrange("p (h n) -> p h n", h=4), ACT.Copy)\
                       .then_inc(S("x0_copied"), 1)
                for lv in range(1, LEVELS):
                    if lv in (2, 4):
                        q = 2 * b2 + lv // 2 - 1
                        ada_copy(act, ADA_C, q, SLOTS_FIRST + SLOTS_EVEN + q, bank[6])
                    for u in range(2):
                        w = sets[u]
                        act.wait_ge(S("ly_done"), lev(b2, lv, u))
                        act.activation(w["Y"], bank[3 * u][:, :].rearrange("p (h n) -> p h n", h=4), ACT.Copy)\
                           .then_inc(S("ly_copied"), 1)
                for u in range(2):
                    b = 2 * b2 + u
                    s, d, hq = BATCHES[b]
                    if s == 0:
                        act.wait_ge(S("st_done"), b + 1)
                        if b >= 2:
                            act.wait_ge(S(f"state_out{u}"), 16)
                        act.activation(st_stage[:, u], bank[3 * u + 1][:, :].rearrange("p (h n) -> p h n", h=4), ACT.Copy)\
                           .then_inc(S("st_ready"), 1)
            act.wait_ge(S("o_ss"), 1)
            ch.link(act.activation(o_ss, o_ss, ACT.Ln))
            act.activation(o_ss, o_ss, ACT.Exp, scale=-0.5).then_inc(S("o_rs"), 1)
            for s in range(2):
                for q in range(2):
                    act.wait_ge(S("dot_done"), 2 * s + q + 1)
                    act.activation(act_t[:, 4 * q:4 * q + 4, s * P:(s + 1) * P],
                                   bank[2 * s + q][:, :].rearrange("p (h n) -> p h n", h=4), ACT.Copy,
                                   scale=p_("onorm")).then_inc(S("dot_copied"), 1)
            act.wait_ge(S("dot_copied"), 4)
            act.sem_inc(S("dot_banks_free"), 1)

        def delta_pool(pool, ch):
            pool.memset(zpad, 0.0).then_inc(S("pad_zero"), 1)
            pool.wait_ge(S("ab_done"), 1)
            pool.dma_start(s0, state0).then_inc(S("s0_in"), 16)
            pool.wait_ge(S("qkt_done"), 8)
            lvl = c_("level").rearrange("p (d l n) -> p d l n", d=2, l=LEVELS)

            def mask4(ap):
                return ap.unsqueeze(1).to_broadcast([P, 4, P])

            def gcol(x, s, d, hq):
                i = (s * 2 + d) * 8 + 4 * hq
                return bcast(x[:, i:i + 4], P)

            def st_out_dma(b):
                s, d, hq = BATCHES[b]
                pool.wait_ge(S("st_ready"), b + 1)
                pool.dma_start(st_out[d, :, 4 * hq:4 * hq + 4, :], st_stage[:, b % 2]).then_inc(S(f"state_out{b % 2}"), 16)

            for b2 in range(4):
                for u in range(2):
                    b = 2 * b2 + u
                    s, d, hq = BATCHES[b]
                    w = sets[u]
                    if b >= 2:
                        pool.wait_ge(S("batch_end"), b - 1)
                    pool.tensor_tensor(w["LM"], mask4(c_("le") if d == 0 else c_("ge")), gcol(g_tok, s, d, hq), ALU.mult)\
                        .then_inc(S("gm_ready"), 1)
                for u in range(2):
                    b = 2 * b2 + u
                    s, d, hq = BATCHES[b]
                    w = sets[u]
                    pool.wait_ge(S("dt_ready"), b + 1)
                    pool.tensor_tensor(w["LT"], w["DT"], gcol(nbeta, s, d, hq), ALU.mult).then_inc(S("dtb_ready"), 1)
                    pool.tensor_tensor(w["DT"], w["DT"], mask4(c_("le") if d == 0 else c_("ge")), ALU.mult)\
                        .then_inc(S("dtm_ready"), 1)
                for lv in range(LEVELS):
                    for u in range(2):
                        b = 2 * b2 + u
                        s, d, hq = BATCHES[b]
                        w = sets[u]
                        if lv == 0:
                            pool.wait_ge(S("lt_ready"), b + 1)
                            ch.link(pool.tensor_tensor(w["XT"], w["LT"], mask4(lvl[:, d, 0]), ALU.mult))
                            pool.tensor_tensor(w["XT"], w["XT"], mask4(ident), ALU.add).then_inc(S("xt0_ready"), 1)
                        else:
                            if lv >= 2:
                                pool.wait_ge(S("ly_done"), lev(b2, lv - 1, u))
                            pool.tensor_tensor(w["LM"], w["LT"], mask4(lvl[:, d, lv]), ALU.mult).then_inc(S("lm_ready"), 1)
                for u in range(2):
                    b = 2 * b2 + u
                    s, d, hq = BATCHES[b]
                    w = sets[u]
                    if s == 0:
                        pool.wait_ge(S("vn_ready"), b + 1)
                        pool.tensor_tensor(w["LM"], w["X"], gcol(kdec, s, d, hq), ALU.mult).then_inc(S("kd_ready"), 1)
                if b2 < 2:
                    for u in range(2):
                        st_out_dma(2 * b2 + u)
            pool.wait_ge(S("state_out0"), 32)
            pool.wait_ge(S("state_out1"), 32)


        def delta_dve(dve, ch):
            ab = ab_raw.rearrange("p (s n) -> p s n", s=2)
            cw = p_("conv").rearrange("p (i j) -> p i j", j=3)

            def to_tok(i):
                dve.wait_ge(S("tok_done"), i + 1)
                dve.tensor_copy(dqkv[:, :, i * P:(i + 1) * P], bank[4 + i % 2][:, 0:T].rearrange("p (s n) -> p s n", s=2))\
                   .then_inc(S("tok_copied"), 1)

            for i in range(24):
                dve.wait_ge(S("z_copied"), i + 1)
                if i >= 3:
                    dve.wait_ge(S("tok_done"), i - 2)
                z, y = zpad[:, i % 3], conv_o[:, i % 3]
                ch.link(dve.tensor_scalar(y, z[:, :, 0:128], cw[:, i, 0:1], None, ALU.mult))
                ch.link(dve.scalar_tensor_tensor(y, z[:, :, 1:129], cw[:, i, 1:2], y, ALU.mult, ALU.add))
                dve.scalar_tensor_tensor(y, z[:, :, 2:130], cw[:, i, 2:3], y, ALU.mult, ALU.add).then_inc(S("conv_sum"), 1)
                if i >= 3:
                    to_tok(i - 3)
            for i in range(21, 24):
                to_tok(i)
            dve.wait_ge(S("ab_done"), 1)
            ch.link(dve.tensor_copy(ab, bank[6][:, 0:64].rearrange("p (s n) -> p s n", s=2)))
            xv = sp_x.rearrange("p (s n) -> p s n", s=2)
            ch.link(dve.tensor_tensor(xv, ab[:, :, 0:16], p_("dt_bias").unsqueeze(1).to_broadcast([P, 2, 16]), ALU.add))
            ch.link(dve.tensor_scalar(sp_a, sp_x, -1.0, None, ALU.mult))
            dve.tensor_tensor(sp_b, sp_a, sp_x, ALU.max).then_inc(S("sp_abs"), 1)
            dve.wait_ge(S("sp_ln"), 1)
            ch.link(dve.scalar_tensor_tensor(sp_a, sp_x, 0.0, sp_b, ALU.max, ALU.add))
            dve.wait_ge(S("a_exp"), 1)
            dve.wait_ge(S("beta_exp"), 1)
            ch.link(dve.tensor_scalar(sp_a, sp_a, -1.0, None, ALU.mult))
            dve.tensor_tensor(g_tok.rearrange("p (s n) -> p s n", s=2), sp_a.rearrange("p (s n) -> p s n", s=2),
                              negA.unsqueeze(1).to_broadcast([P, 2, 16]), ALU.mult).then_inc(S("g_ready"), 1)
            ch.link(dve.tensor_scalar(beta, beta, 1.0, None, ALU.add))
            ch.link(dve.reciprocal(beta, beta))
            ch.link(dve.tensor_scalar(nbeta, beta, -1.0, None, ALU.mult))
            dve.wait_ge(S("tok_copied"), 24)
            for s in range(2):
                qk = dqkv[:, s, 0:2048]
                ch.link(dve.tensor_tensor(dsq, qk, qk, ALU.mult))
                ch.link(dve.tensor_reduce(qk_ss[:, s * 16:s * 16 + 16], dsq.rearrange("p (h n) -> p h n", h=16), AX, ALU.add))
            dve.tensor_scalar(qk_ss, qk_ss, 1e-6, None, ALU.add).then_inc(S("qk_ss"), 1)
            dve.wait_ge(S("qk_rs"), 1)
            rv = qk_ss.rearrange("p (s w h) -> p s w h", s=2, w=2)
            ch.link(dve.tensor_scalar(rv[:, :, 0, :], rv[:, :, 0, :], float(P) ** -0.5, None, ALU.mult))
            for s in range(2):
                qk = dqkv[:, s, 0:2048].rearrange("p (h n) -> p h n", h=16)
                last = dve.tensor_tensor(qk, qk, bcast(qk_ss[:, s * 16:s * 16 + 16], P), ALU.mult)
            last.then_inc(S("qk_ready"), 1)

            def b4(x, s, d, hq):
                i = (s * 2 + d) * 8 + 4 * hq
                return bcast(x[:, i:i + 4], P)

            def ps(i):
                return bank[i][:, :].rearrange("p (h n) -> p h n", h=4)

            for b2 in range(4):
                for u in range(2):
                    b = 2 * b2 + u
                    w = sets[u]
                    dve.wait_ge(S("kk_done"), b + 1)
                    dve.wait_ge(S("dtb_ready"), b + 1)
                    dve.tensor_tensor(w["LT"], w["LT"], ps(3 * u + 1), ALU.mult).then_inc(S("lt_ready"), 1)
                    dve.wait_ge(S("dtm_ready"), b + 1)
                    dve.tensor_tensor(w["AT"], w["DT"], ps(3 * u + 2), ALU.mult).then_inc(S("at_ready"), 1)
                for u in range(2):
                    dve.wait_ge(S("x0_copied"), 2 * b2 + u + 1)
                for lv in range(1, LEVELS):
                    if lv in (3, 5):
                        ada_store(dve, SLOTS_FIRST + SLOTS_EVEN + 2 * b2 + (lv - 1) // 2 - 1, bank[7])
                    for u in range(2):
                        w = sets[u]
                        dve.wait_ge(S("dx_done"), lev(b2, lv, u))
                        if lv < LEVELS - 1:
                            ch.link(dve.tensor_tensor(w["X"], w["X"], ps(3 * u + 2), ALU.add))
                        dve.tensor_tensor(w["XT"], w["XT"], ps(3 * u + 1), ALU.add).then_inc(S("x_summed"), 1)
                        dve.wait_ge(S("x_summed"), lev(b2, lv, u))
                for u in range(2):
                    b = 2 * b2 + u
                    s, d, hq = BATCHES[b]
                    w = sets[u]
                    if s == 1:
                        dve.wait_ge(S("ks_done"), b - 3)
                        ch.link(dve.tensor_tensor(w["Y"], ps(3 * u), b4(egc, s, d, hq), ALU.mult))
                        vv = dqkv[:, s, 2048 + 512 * hq:2048 + 512 * hq + 512].rearrange("p (h n) -> p h n", h=4)
                        ch.link(dve.tensor_tensor(w["Y"], vv, w["Y"], ALU.subtract))
                        oo = o_d[:, s, 512 * hq:512 * hq + 512].rearrange("p (h n) -> p h n", h=4)
                        ch.link(dve.tensor_tensor(w["LT"], ps(3 * u + 2), b4(egc, s, d, hq), ALU.mult))
                        if d == 0:
                            ch.link(dve.tensor_copy(oo, w["LT"]))
                        else:
                            ch.link(dve.tensor_tensor(oo, oo, w["LT"], ALU.add))
                    dve.sem_inc(S("xt_final"), 1)
                for u in range(2):
                    b = 2 * b2 + u
                    s, d, hq = BATCHES[b]
                    w = sets[u]
                    dve.wait_ge(S("vn_done"), b + 1)
                    dve.tensor_tensor(w["X"], ps(3 * u + 1), b4(beta, s, d, hq), ALU.mult).then_inc(S("vn_ready"), 1)
                for u in range(2):
                    b = 2 * b2 + u
                    s, d, hq = BATCHES[b]
                    w = sets[u]
                    dve.wait_ge(S("o_done"), b + 1)
                    oo = o_d[:, s, 512 * hq:512 * hq + 512].rearrange("p (h n) -> p h n", h=4)
                    if s == 0 and d == 0:
                        ch.link(dve.tensor_copy(oo, ps(3 * u)))
                    else:
                        ch.link(dve.tensor_tensor(oo, oo, ps(3 * u), ALU.add))
                    if s == 0:
                        dve.wait_ge(S("st_ready"), b + 1)
                    dve.sem_inc(S("batch_end"), 1)
            dve.wait_ge(S("ada_stored"), SLOTS_FIRST + SLOTS_EVEN + SLOTS_ODD)
            fold_norm(dve, ch, 2, 1, 3)
            for s in range(2):
                ch.link(dve.tensor_tensor(dsq[:, s * 1024:(s + 1) * 1024], o_d[:, s, :], o_d[:, s, :], ALU.mult))
            ch.link(dve.tensor_reduce(o_ss, dsq.rearrange("p (h n) -> p h n", h=16), AX, ALU.add))
            dve.tensor_scalar(o_ss, o_ss, 1.0 / P, EPS, ALU.mult, ALU.add).then_inc(S("o_ss"), 1)
            dve.wait_ge(S("o_rs"), 1)
            for s in range(2):
                oo = o_d[:, s, :].rearrange("p (h n) -> p h n", h=8)
                ch.link(dve.tensor_tensor(oo, oo, bcast(o_ss[:, s * 8:s * 8 + 8], P), ALU.mult))
                dve.tensor_tensor(o_d[:, s, :], o_d[:, s, :], dgate[:, s, :], ALU.mult).then_inc(S("do_ready"), 1)
            out_dve(dve, ch, 1, OOUT0)

        PAIRS = [(kind, s, c) for kind in range(2) for s in range(2) for c in range(4)]

        @block.tensor
        def _(pe):
            pe.wait_ge(S("params_in"), 16)
            pe.wait_ge(S("consts_in"), 16)
            pe.wait_ge(S("cond_ready"), 1)
            for q in range(SLOTS_FIRST):
                ada_rows(pe, ADA_A, q, q, bank[q % 2])
                ada_columns(pe, q, bank[2 + q % 2])
            meet(pe, "pe")
            for n in range(12):
                q, s = n // 2, n % 2
                k = wait_slot(pe, EIN0, q)
                w = ring[:, k, :].rearrange("p (c n) -> p c n", c=KC)
                if n >= 4:
                    pe.wait_ge(S("proj_copied"), n - 3)
                for c in range(KC):
                    last = pe.matmul(bank[n % 4][:, :], act_t[:, c, s * P:(s + 1) * P], w[:, c, :],
                                     start=(c == 0), stop=(c == KC - 1))
                last.then_inc(S("proj_done"), 1)
            pe.wait_ge(S("proj_copied"), 12)
            for n in range(8):
                wi, s = n // 2, n % 2
                col = (0, 512, 1536, 2048)[wi]
                if n >= 2:
                    pe.wait_ge(S("ht_copied"), n - 1)
                for j in range(4):
                    last = pe.transpose(bank[4 + n % 2][:, j * P:(j + 1) * P], qkv[:, s, col + j * P:col + (j + 1) * P], ident)
                last.then_inc(S("ht_done"), 1)
            pe.wait_ge(S("ht_copied"), 8)
            pe.wait_ge(S("even_in"), 112)

            def sc(p):
                kind, s, c = PAIRS[p]
                if p >= 2:
                    pe.wait_ge(S("exp_done"), 2 * (p - 1))
                for j in range(2):
                    bk = bank[p % 2 + 6 * j]
                    r = slice(64 * j, 64 * j + 64)
                    q = heads_t[r, 2 * kind, s, c, :]
                    biased_ = kind == 0 and s == 1
                    last = pe.matmul(bk[:, 0:P], q, heads_t[r, 2 * kind + 1, s, c, :], start=True, stop=not biased_)
                    if biased_:
                        last = pe.matmul(bk[:, 0:P], ident, bias[:, 2 * c + j, :], start=False, stop=True)
                    if s == 1:
                        cache = nkc if kind == 0 else dkc
                        last = pe.matmul(bk[:, P:2 * P], q, cache[r, c, :], start=True, stop=True)
                last.then_inc(S("score_done"), 1)

            def pt(p):
                kind, s, c = PAIRS[p]
                pe.wait_ge(S("p_ready"), p + 1)
                if p >= 2:
                    pe.wait_ge(S("pt_copied"), p - 1)
                nk2 = 1 if s == 0 else 2
                for j in range(2 if kind == 0 else 1):
                    for t in range(nk2):
                        i = j * nk2 + t
                        last = pe.transpose(bank[2 + p % 2][:, i * P:(i + 1) * P], probs[:, p % 2, j, t * P:(t + 1) * P], ident)
                last.then_inc(S("pt_done"), 1)

            def pv(p):
                kind, s, c = PAIRS[p]
                g = p // 4
                pe.wait_ge(S("pt_copied"), p + 1)
                if p % 4 == 0 and g >= 1:
                    pe.wait_ge(S("o_copied"), g)
                nk2 = 1 if s == 0 else 2
                pflat = probs_t[:, p % 2].rearrange("p j n -> p (j n)")
                for j in range(2 if kind == 0 else 1):
                    if kind == 0:
                        h = 2 * c + j
                        vs = [qkv[:, s, 1024 + h * 64:1024 + h * 64 + 64], nvc[:, h * 64:h * 64 + 64]]
                        out = bank[4][:, h * 64:h * 64 + 64]
                    else:
                        vs = [qkv[:, s, 2560 + c * P:2560 + (c + 1) * P], dvc[:, c * P:(c + 1) * P]]
                        out = bank[4][:, c * P:(c + 1) * P]
                    for t in range(nk2):
                        i = j * nk2 + t
                        last = pe.matmul(out, pflat[:, i * P:(i + 1) * P], vs[t], start=(t == 0), stop=(t == nk2 - 1))
                last.then_inc(S("pv_done"), 1)

            for p in range(18):
                if p < 16:
                    sc(p)
                if p < SLOTS_EVEN:
                    ada_rows(pe, ADA_B, p, SLOTS_FIRST + p, bank[5])
                if 1 <= p < 17:
                    pt(p - 1)
                if p >= 2:
                    pv(p - 2)
                if p < SLOTS_EVEN:
                    ada_columns(pe, SLOTS_FIRST + p, bank[5])
            for g in range(4):
                kind, s = g // 2, g % 2
                pe.wait_ge(S("o_copied"), 4)
                if kind == 1:
                    pe.wait_ge(S("o_normed"), 1)
                for j in range(4):
                    last = pe.transpose(bank[g][:, j * P:(j + 1) * P], o_tok[:, s, kind * 512 + j * P:kind * 512 + (j + 1) * P], ident)
                last.then_inc(S("ot_done"), 1)
            pe.wait_ge(S("ot_copied"), 4)
            out_pe(pe, 0, EOUT0)
            meet(pe, "pe")
            ln_pe(pe, 0)
            meet(pe, "pe")
            moe_pe(pe, 0, MOE0)
            meet(pe, "pe")
            ln_pe(pe, 1)
            meet(pe, "pe")
            delta_pe(pe)
            meet(pe, "pe")
            ln_pe(pe, 2)
            meet(pe, "pe")
            moe_pe(pe, 1, MOE1)
            meet(pe, "pe")
            ln_pe(pe, 3)
            meet(pe, "pe")
            for s in range(2):
                for q in range(2):
                    for j in range(4):
                        last = pe.transpose(bank[2 * s + q][:, j * P:(j + 1) * P], res[:, 4 * q + j, s * P:(s + 1) * P], ident)
                    last.then_inc(S("yt_done"), 1)

        @block.scalar
        def _(act):
            ch = Chain(act, "act_step")
            act.wait_ge(S("params_in"), 16)
            act.activation(cond_t, p_("cond"), ACT.Silu).then_inc(S("cond_ready"), 1)
            for q in range(SLOTS_FIRST):
                ada_copy(act, ADA_A, q, q, bank[q % 2])
            meet(act, "act")
            act.activation(lam_w[:, 0:2], lam_w[:, 0:2], ACT.Exp).then_inc(S("lam_exp"), 1)
            for n in range(12):
                q, s = n // 2, n % 2
                if q in (3, 4) and s == 1:
                    continue
                act.wait_ge(S("proj_done"), n + 1)
                dst = qkv[:, s, q * 512:(q + 1) * 512]
                act.activation(dst, bank[n % 4][:, :], ACT.Copy, scale=(0.125 if q in (0, 3) else 1.0))\
                   .then_inc(S("proj_act"), 1)
                act.wait_ge(S("proj_act"), 1 + len([m for m in range(n) if not (m // 2 in (3, 4) and m % 2 == 1)]))
                act.wait_ge(S("proj_copied"), n) if n else None
                act.sem_inc(S("proj_copied"), 1)
                if s == 1:
                    act.sem_inc(slot_free[at_ring(EIN0, q)[0]], 1)
                if s == 0 and q in (1, 2, 4, 5):
                    act.sem_inc(S("kv_out_ready"), 1)
            for n in range(8):
                wi, s = n // 2, n % 2
                act.wait_ge(S("ht_done"), n + 1)
                act.activation(heads_t[:, wi, s], bank[4 + n % 2][:, :].rearrange("p (c n) -> p c n", c=4), ACT.Copy)\
                   .then_inc(S("ht_copied"), 1)
            def ptc(p):
                kind, s, c = PAIRS[p]
                n = (1 if s == 0 else 2) * (2 if kind == 0 else 1) * P
                act.wait_ge(S("pt_done"), p + 1)
                if p >= 2:
                    act.wait_ge(S("pv_done"), p - 1)
                act.activation(probs_t[:, p % 2].rearrange("p j n -> p (j n)")[:, 0:n], bank[2 + p % 2][:, 0:n], ACT.Copy)\
                   .then_inc(S("pt_copied"), 1)

            def oc(g):
                kind, s = g // 2, g % 2
                act.wait_ge(S("pv_done"), 4 * g + 4)
                act.activation(o_tok[:, s, kind * 512:(kind + 1) * 512], bank[4][:, :], ACT.Copy)\
                   .then_inc(S("o_copied"), 1)

            for p in range(18):
                if p < 16:
                    kind, s, c = PAIRS[p]
                    nk = 128 if s == 0 else 256
                    if p >= 2:
                        act.wait_ge(S("pt_done"), p - 1)
                    for j in range(2):
                        act.wait_ge(S("max_done"), 2 * p + j + 1)
                        act.activation(probs[:, p % 2, j, 0:nk], bank[p % 2 + 6 * j][:, 0:nk], ACT.Exp,
                                       bias=mx[:, 2 * p + j:2 * p + j + 1],
                                       accum_out=sums[:, 2 * p + j:2 * p + j + 1]).then_inc(S("exp_done"), 1)
                if p < SLOTS_EVEN:
                    ada_copy(act, ADA_B, p, SLOTS_FIRST + p, bank[5])
                if 1 <= p < 17:
                    ptc(p - 1)
                if p >= 2 and (p - 2) % 4 == 3:
                    oc((p - 2) // 4)
            act.wait_ge(S("o_ms"), 1)
            ch.link(act.activation(rms[:, 0:8], rms[:, 0:8], ACT.Ln))
            act.activation(rms[:, 0:8], rms[:, 0:8], ACT.Exp, scale=-0.5).then_inc(S("o_rms"), 1)
            for g in range(2):
                act.wait_ge(S("ot_done"), g + 1)
                act.activation(act_t[:, 0:4, g * P:(g + 1) * P], bank[g][:, :].rearrange("p (c n) -> p c n", c=4), ACT.Copy)\
                   .then_inc(S("ot_copied"), 1)
            for g in range(2):
                act.wait_ge(S("ot_done"), g + 3)
                act.activation(act_t[:, 4:8, g * P:(g + 1) * P], bank[2 + g][:, :].rearrange("p (c n) -> p c n", c=4),
                               ACT.Copy, scale=sub_g).then_inc(S("ot_copied"), 1)
            meet(act, "act")
            ln_act(act, ch, 0)
            meet(act, "act")
            moe_act(act, ch, 0, MOE0)
            meet(act, "act")
            ln_act(act, ch, 1)
            meet(act, "act")
            delta_act(act, ch)
            meet(act, "act")
            ln_act(act, ch, 2)
            meet(act, "act")
            moe_act(act, ch, 1, MOE1)
            meet(act, "act")
            ln_act(act, ch, 3)
            meet(act, "act")
            for g in range(4):
                s, q = g // 2, g % 2
                act.wait_ge(S("yt_done"), g + 1)
                act.activation(y_tok[:, s, q * 512:(q + 1) * 512], bank[g][:, :], ACT.Copy).then_inc(S("y_ready"), 1)

        @block.vector
        def _(dve):
            ch = Chain(dve, "dve_step")
            dve.wait_ge(S("params_in"), 16)
            for q in range(SLOTS_FIRST):
                ada_store(dve, q, bank[2 + q % 2])
            dve.wait_ge(S("ada_stored"), SLOTS_FIRST)
            ch.link(dve.tensor_scalar(mod_v[:, 0, 1], mod_v[:, 0, 1], 1.0, None, ALU.add))
            for i, name in enumerate(("ln_g", "ln_b")):
                ch.link(dve.tensor_scalar(ln_scaled[:, 64 * i:64 * i + 48], p_(name)[:, 0:48], ALPHA, None, ALU.mult))
                ch.link(dve.tensor_copy(ln_scaled[:, 64 * i + 48:64 * i + 64], p_(name)[:, 48:64]))
            ch.link(dve.tensor_scalar(sub_g, p_("subln"), 1.0 - (0.8 - 0.6 * math.exp(0.0)), None, ALU.mult))
            dve.wait_ge(S("even_in"), 112)
            lamp = lam_p.rearrange("p (a b n) -> p a b n", a=2, b=2)
            ch.link(dve.tensor_tensor(rope_1[:, 0:128].rearrange("p (a n) -> p a n", a=2), lamp[:, :, 0], lamp[:, :, 1], ALU.mult))
            ch.link(dve.tensor_reduce(lam_w[:, 0:2], rope_1[:, 0:128].rearrange("p (a n) -> p a n", a=2), AX, ALU.add))
            dve.wait_ge(S("x_in"), 16)
            dve.wait_ge(S("pool_step"), 1)
            av = act_t[:, :, :].rearrange("p c (s n) -> p (c s) n", s=2)
            ch.link(dve.tensor_tensor(av, av, bcast(mod_v[:, 0, 1].rearrange("p c s -> p (c s)"), P), ALU.mult))
            ch.link(dve.tensor_tensor(av, av, bcast(mod_v[:, 0, 0].rearrange("p c s -> p (c s)"), P), ALU.add))
            meet(dve, "dve")
            for q in (3, 4):
                n = 2 * q + 1
                dve.wait_ge(S("proj_done"), n + 1)
                src = bank[n % 4][:, :].rearrange("p (h a b n) -> p h a b n", h=8, a=2, b=2)
                t1 = rope_1.rearrange("p (h n) -> p h n", h=8)
                t2 = rope_2.rearrange("p (h a b n) -> p h a b n", h=8, a=2, b=2)
                sn = ec_("rope_s").rearrange("p (a b n) -> p a b n", a=2, b=2)
                ch.link(dve.tensor_tensor(t1, bank[n % 4][:, :].rearrange("p (h n) -> p h n", h=8),
                                          ec_("rope_c").unsqueeze(1).to_broadcast([P, 8, 64]), ALU.mult))
                for b in range(2):
                    for a in range(2):
                        ch.link(dve.tensor_tensor(t2[:, :, a, b, :], src[:, :, a, 1 - b, :],
                                                  sn[:, a, b, :].unsqueeze(1).to_broadcast([P, 8, 16]), ALU.mult))
                dst = qkv[:, 1, q * 512:(q + 1) * 512]
                ch.link(dve.tensor_tensor(dst, rope_1, rope_2, ALU.add))
                if q == 3:
                    ch.link(dve.tensor_scalar(dst, dst, 0.125, None, ALU.mult))
                dve.wait_ge(S("proj_copied"), n)
                dve.sem_inc(S("proj_copied"), 1)
                dve.sem_inc(slot_free[at_ring(EIN0, q)[0]], 1)
            dve.wait_ge(S("lam_exp"), 1)
            ch.link(dve.tensor_tensor(lam_w[:, 2:3], lam_w[:, 1:2], lam_w[:, 0:1], ALU.subtract))
            ch.link(dve.tensor_scalar(lam_w[:, 3:4], lam_w[:, 2:3], -(0.8 - 0.6 * math.exp(0.0)), None, ALU.add))

            def mxp(p):
                kind, s, c = PAIRS[p]
                nk = 128 if s == 0 else 256
                dve.wait_ge(S("score_done"), p + 1)
                for j in range(2):
                    dve.tensor_reduce(mx[:, 2 * p + j:2 * p + j + 1], bank[p % 2 + 6 * j][:, 0:nk],
                                      AX, ALU.max, negate=True).then_inc(S("max_done"), 1)

            for p in range(17):
                if p < 16:
                    mxp(p)
                if 1 <= p <= SLOTS_EVEN:
                    ada_store(dve, SLOTS_FIRST + p - 1, bank[5])
                if p < 1:
                    continue
                q = p - 1
                kind, s, c = PAIRS[q]
                nk = 128 if s == 0 else 256
                dve.wait_ge(S("exp_done"), 2 * (q + 1))
                rs = rsum[:, 2 * q:2 * q + 2]
                ch.link(dve.reciprocal(rs, sums[:, 2 * q:2 * q + 2]))
                pb = probs[:, q % 2]
                if kind == 0:
                    dve.tensor_tensor(pb[:, :, 0:nk], pb[:, :, 0:nk], bcast(rs, nk), ALU.mult).then_inc(S("p_ready"), 1)
                else:
                    ch.link(dve.tensor_tensor(nlr[:, 0:1], rs[:, 1:2], lam_w[:, 3:4], ALU.mult))
                    ch.link(dve.tensor_scalar(pb[:, 0, 0:nk], pb[:, 0, 0:nk], rs[:, 0:1], None, ALU.mult))
                    dve.scalar_tensor_tensor(pb[:, 0, 0:nk], pb[:, 1, 0:nk], nlr[:, 0:1], pb[:, 0, 0:nk],
                                             ALU.mult, ALU.add).then_inc(S("p_ready"), 1)
            dve.wait_ge(S("o_copied"), 4)
            ov = o_tok[:, :, 512:1024]
            dve.wait_ge(S("pv_done"), 16)
            dve.wait_ge(S("out_done"), 64)
            ch.link(dve.tensor_tensor(o_sq.rearrange("p (s n) -> p s n", s=2), ov, ov, ALU.mult))
            ch.link(dve.tensor_reduce(rms[:, 0:8], o_sq.rearrange("p (h n) -> p h n", h=8), AX, ALU.add))
            dve.tensor_scalar(rms[:, 0:8], rms[:, 0:8], 1.0 / P, EPS, ALU.mult, ALU.add).then_inc(S("o_ms"), 1)
            dve.wait_ge(S("o_rms"), 1)
            for s in range(2):
                oh = o_tok[:, s, 512:1024].rearrange("p (h n) -> p h n", h=4)
                ch.link(dve.tensor_tensor(oh, oh, bcast(rms[:, 4 * s:4 * s + 4], P), ALU.mult))
            dve.sem_inc(S("o_normed"), 1)
            dve.wait_ge(S("ada_stored"), SLOTS_FIRST + SLOTS_EVEN)
            fold_norm(dve, ch, 0, 0, 3)
            fold_norm(dve, ch, 1, 1, 0)
            out_dve(dve, ch, 0, EOUT0)
            meet(dve, "dve")
            ln_dve(dve, ch, 0)
            meet(dve, "dve")
            moe_dve(dve, ch, 0, MOE0)
            meet(dve, "dve")
            ln_dve(dve, ch, 1)
            meet(dve, "dve")
            delta_dve(dve, ch)
            meet(dve, "dve")
            ln_dve(dve, ch, 2)
            meet(dve, "dve")
            moe_dve(dve, ch, 1, MOE1)
            meet(dve, "dve")
            ln_dve(dve, ch, 3)
            meet(dve, "dve")

        @block.sync
        def _(sp):
            sp.dma_start(par[:, :], params).then_inc(S("params_in"), 16)
            sp.dma_start(cst[:, :], consts).then_inc(S("consts_in"), 16)
            for k in range(RING):
                sp.dma_start(ring[:, k, :], slots[k]).then_inc(slot_full[k], 16)
            with sp.Fori(0, N_SLOTS // RING - 1) as turn:
                for k in range(RING):
                    sp.wait_ge(slot_free[k], turn + 1)
                    sp.dma_start(ring[:, k, :], slots[bass.ds(turn * RING + (RING + k), 1)].rearrange("a p n -> (a p) n")).then_inc(slot_full[k], 16)

        @block.gpsimd
        def _(pool):
            ch = Chain(pool, "pool_step")
            pool.dma_start(act_t[:, :, :], x_t).then_inc(S("x_in"), 16)
            for dst, src in ((nkc, nat_kc), (nvc, nat_vc), (dkc, diff_kc), (dvc, diff_vc), (bias, nat_bias), (lam_p, lam_in), (even_c, even_consts)):
                pool.dma_start(dst, src).then_inc(S("even_in"), 16)
            pool.wait_ge(S("x_in"), 16)
            ch.link(pool.tensor_scalar(res[:, :, :], act_t[:, :, :], ALPHA, None, ALU.mult))
            pool.wait_ge(S("even_in"), 112)
            pool.wait_ge(S("consts_in"), 16)
            ch.link(pool.tensor_tensor(bias, bias, ec_("window").unsqueeze(1).to_broadcast([P, 8, P]), ALU.add))
            meet(pool, "pool")
            pool.wait_ge(S("kv_out_ready"), 4)
            for w, out in ((1, nk_out), (2, nv_out), (4, dk_out), (5, dv_out)):
                pool.dma_start(out, qkv[:, 0, w * 512:(w + 1) * 512]).then_inc(S("out_done"), 16)
            pool.wait_ge(S("out_done"), 64)
            meet(pool, "pool")
            ln_pool(pool, ch, 0)
            meet(pool, "pool")
            meet(pool, "pool")
            ln_pool(pool, ch, 1)
            meet(pool, "pool")
            delta_pool(pool, ch)
            meet(pool, "pool")
            ln_pool(pool, ch, 2)
            meet(pool, "pool")
            meet(pool, "pool")
            ln_pool(pool, ch, 3)
            meet(pool, "pool")
            pool.wait_ge(S("y_ready"), 4)
            for s in range(2):
                pool.dma_start(y_out[s], y_tok[:, s, :]).then_inc(S("out_done"), 16)
            pool.wait_ge(S("out_done"), 64 + 32)


def shape_constants():
    import numpy as np
    f = np.float32
    i = np.arange(P)
    r, c = i[:, None], i[None, :]
    out = {"ident": r == c, "mean": np.full((P, P), 1.0 / D), "le": r <= c, "gt": r > c, "ge": r >= c, "lt": r < c}
    lv = []
    for d in range(2):
        for k in range(LEVELS):
            same = (r >> (k + 1)) == (c >> (k + 1))
            hi_r, hi_c = ((r >> k) & 1) == 1, ((c >> k) & 1) == 1
            lv.append(same & ((~hi_r & hi_c) if d == 0 else (hi_r & ~hi_c)))
    out["level"] = np.concatenate(lv, 1)
    inv = (f(10000.0) ** (-np.arange(16, dtype=f) / f(16))).astype(f)
    ar = (i // 64).astype(f)[:, None] * inv
    ac = (i % 64).astype(f)[:, None] * inv
    out["rope_c"] = np.concatenate([np.cos(ar), np.cos(ar), np.cos(ac), np.cos(ac)], 1)
    out["rope_s"] = np.concatenate([-np.sin(ar), np.sin(ar), -np.sin(ac), np.sin(ac)], 1)
    start = np.clip(i % 64 - 8, 0, 48)[:, None]
    ok = ((c % 64) >= start) & ((c % 64) < start + 16)
    out["window"] = np.where(ok, 0.0, -BIG)
    out["iota"] = np.broadcast_to(i.astype(f), (P, P))
    out["rank4"] = np.broadcast_to(4.0 - np.arange(4), (P, 4))
    out["rank16"] = np.broadcast_to(16.0 - np.arange(16), (P, 16))
    return [np.ascontiguousarray(np.concatenate([np.asarray(out[n], f) for n in names], 1)) for names in (CONST_W, EVEN_W)]


def kernel(**inputs):
    import numpy as np
    import concourse.bacc as bacc
    from concourse.bass_utils import run_bass_kernel_spmd as run

    a = {k: np.asarray(v) for k, v in inputs.items()}

    def rows(w, n):
        k, m = w.shape
        return w.reshape(k // P, P, m // n, n).transpose(2, 1, 0, 3).reshape(m // n, P, (k // P) * n)

    def feat(v):
        v = v.reshape(v.shape[:-1] + (-1, P))
        return np.moveaxis(v, -1, 0)

    def moe_slots(l):
        g = np.stack([np.stack([rows(a["moe_wg"][l, e], FF)[0], rows(a["moe_wu"][l, e], FF)[0],
                                rows(a["moe_wd"][l, e], D)[0]]) for e in range(N_EXP)])
        return g.reshape(3 * N_EXP, P, SLOT)

    w_odd = a["w_in_odd"][0]
    ada = np.concatenate([rows(a["ada_w"][l], 512) for l in range(DEPTH)], 0)
    slots = np.concatenate([ada[0:4], rows(a["w_in_even"][0], 512), ada[4:16], rows(a["w_out_even"][0], 512), moe_slots(0),
                            rows(np.concatenate([w_odd[:, :3072], w_odd[:, 3104:]], 1), 512), ada[16:24],
                            rows(a["w_out_odd"][0], 512), moe_slots(1)], 0)
    x = np.stack([a["x_prompt"][0], a["x_sample"][0]])
    x_t = np.ascontiguousarray(x.reshape(2, P, KC, P).transpose(3, 2, 0, 1).reshape(P, KC, T))

    def rep(v):
        return np.broadcast_to(v.reshape(1, -1), (P, v.size))

    par = {
        "cond": feat(np.stack([a["c_ctx"], a["c"][0]])).transpose(0, 2, 1).reshape(P, -1),
        "ada_b": np.repeat(feat(a["ada_b"]).reshape(P, 96), 2, axis=1),
        "ln_g": np.repeat(feat(a["ln_g"]).reshape(P, 32), 2, axis=1),
        "ln_b": np.repeat(feat(a["ln_b"]).reshape(P, 32), 2, axis=1),
        "router": rows(a["router_w"], 16)[0],
        "router_b": rep(a["router_b"]),
        "subln": a["diff_subln"][0].reshape(P, 1),
        "onorm": a["onorm_odd"][0].reshape(P, 1),
        "conv": a["conv_odd"][0].reshape(3, 24, P).transpose(2, 1, 0).reshape(P, 72),
        "a_log": rep(a["a_log_odd"][0]),
        "dt_bias": rep(a["dt_bias_odd"][0]),
        "w_ab": rows(np.ascontiguousarray(w_odd[:, 3072:3104]), 32)[0],
    }
    params = np.ascontiguousarray(np.concatenate([par[n] for n in PARAM_W], 1))
    i = np.arange(P)
    dr = i[None, :] // 64 - i[:, None] // 64 + 7
    dc = np.clip(i[None, :] % 64 - i[:, None] % 64, -15, 15) + 15
    nat_bias = np.ascontiguousarray(a["nat_bias"][0][:, dr, dc].transpose(1, 0, 2))
    consts, even_consts = shape_constants()
    arrays = {
        "slots": slots, "x_t": x_t, "consts": consts, "even_consts": even_consts, "params": params,
        "nat_kc": np.ascontiguousarray(a["cache_nat_k"][0, 0].reshape(P, 4, P).transpose(2, 1, 0)),
        "nat_vc": np.ascontiguousarray(a["cache_nat_v"][0, 0].reshape(P, 512)),
        "diff_kc": np.ascontiguousarray(a["cache_diff_k"][0, 0].reshape(P, 4, P).transpose(2, 1, 0)),
        "diff_vc": np.ascontiguousarray(a["cache_diff_v"][0, 0].reshape(P, 512)),
        "nat_bias": nat_bias, "lam": np.ascontiguousarray(rep(a["diff_lam"][0])),
        "state0": np.ascontiguousarray(a["state_delta"][0, 0].transpose(2, 0, 1, 3)),
    }
    nc = bacc.Bacc("TRN2", target_bir_lowering=False, num_devices=1)
    args = [nc.dram_tensor(n, v.shape, F32, kind="ExternalInput").ap() for n, v in arrays.items()]
    outs = {"y": (2, P, D), "nk": (P, 512), "nv": (P, 512), "dk": (P, 512), "dv": (P, 512), "st": (2, P, HEADS, P)}
    args += [nc.dram_tensor("out_" + n, s, F32, kind="ExternalOutput").ap() for n, s in outs.items()]
    build_program(nc, *args)
    r = run(nc, [arrays], core_ids=[0]).results[0]
    y = r["out_y"]
    return (y[0:1], y[1:2], r["out_nk"].reshape(1, 1, 128, 8, 64), r["out_nv"].reshape(1, 1, 128, 8, 64),
            r["out_dk"].reshape(1, 1, 128, 4, 2, 64), r["out_dv"].reshape(1, 1, 128, 4, 128),
            r["out_st"].transpose(0, 2, 1, 3).reshape(1, 1, 2, 8, 128, 128))
```

```python
from contextlib import ExitStack
import math

import concourse.bass as bass
from concourse import mybir

P = 128
D = 1024
KC = D // P
T = 256
SLOT = 4096
RING = 6
DEPTH = 2
N_EXP = 16
FF = 512
FC = FF // P
HEADS = 8
EIN0, EOUT0, MOE0, OIN0, OOUT0, MOE1, N_SLOTS = 4, 19, 24, 72, 86, 90, 138
ADA_SLOTS = (list(range(4)) + [EIN0 + 2 * q + 1 for q in range(6)] + [EIN0 + 12 + q for q in range(3)]
             + [EOUT0 + 2 + q for q in range(3)] + [OIN0 + 2 * q + 1 for q in range(6)] + [OOUT0 + 2, OOUT0 + 3])
POOL_JOBS = (8, 11, 12, 16, 18, 20)
PE_JOBS = (1, 3, 10, 13, 14, 15, 22, 23)
ADA_FIRST, ADA_PROJ, ADA_EVEN, ADA_MOE0, ADA_ODD, N_ADA = 4, 10, 13, 16, 22, 24
CAP = 128
ALPHA = (2 * DEPTH) ** 0.25
EPS = 1e-5
LEVELS = 7
BIG = 1e30

F32 = mybir.dt.float32
ALU = mybir.AluOpType
ACT = mybir.ActivationFunctionType
AX = mybir.AxisListType.X

CONST_W = {}
_at = 0
for _n, _w in (("ident", 128), ("mean", 128), ("le", 128), ("gt", 128), ("ge", 128), ("lt", 128),
               ("level", LEVELS * 128), ("half", LEVELS * 128), ("iota", 128), ("tile4", 4), ("rank4", 4), ("rank16", 16)):
    CONST_W[_n] = (_at, _at + _w)
    _at += _w
N_CONST = _at
EVEN_W = {"rope_c": (0, 64), "rope_s": (64, 128), "window": (128, 256)}
PARAM_W = {}
_at = 0
for _n, _w in (("cond", KC * 2), ("ada_b", 192), ("ln_g", 4 * 16), ("ln_b", 4 * 16), ("router", KC * 16),
               ("router_b", 16), ("subln", 1), ("onorm", 1), ("conv", 24 * 3), ("a_log", 16),
               ("dt_bias", 16), ("w_ab", KC * 32)):
    PARAM_W[_n] = (_at, _at + _w)
    _at += _w
N_PARAM = _at


def build_program(nc, slots, x_t, consts, even_consts, params, nat_kc, nat_vc, diff_kc, diff_vc, nat_bias, lam_in, state0,
                  y_out, nk_out, nv_out, dk_out, dv_out, st_out):
    ctx = ExitStack()
    with ctx:
        def sb(name, shape):
            return ctx.enter_context(nc.sbuf_tensor(name, shape, F32))

        ring = sb("ring", [P, RING, SLOT])
        res = sb("res", [P, KC, T])
        act_t = sb("act_t", [P, KC, T])
        cst = sb("cst", [P, N_CONST])
        par = sb("par", [P, N_PARAM])
        mod = sb("mod", [P, 192])
        small = sb("small", [P, 680])
        arena = sb("arena", [P, 17408])

        flags = ctx.enter_context(nc.sbuf_tensor("flags", [P, 2, N_EXP], mybir.dt.int32))
        ones = sb("ones", [P, 1])
        ada_prod = sb("ada_prod", [P, 512])
        bank = [ctx.enter_context(nc.psum_tensor(f"bank{i}", [P, 512], F32)) for i in range(8)]

        def c_(name):
            a, b = CONST_W[name]
            return cst[:, a:b]

        def ec_(name):
            a, b = EVEN_W[name]
            return even_c[:, a:b]

        def p_(name):
            a, b = PARAM_W[name]
            return par[:, a:b]

        ident = c_("ident")
        sems = {}

        def S(name):
            if name not in sems:
                sems[name] = ctx.enter_context(nc.semaphore(name))
            return sems[name]

        slot_full = [S(f"slot_full{k}") for k in range(RING)]
        slot_free = [S(f"slot_free{k}") for k in range(RING)]

        mod_v = mod[:, :].rearrange("p (l j c s) -> p l j c s", l=DEPTH, j=6, c=KC)

        def gate_col(l, j, c, s):
            i = ((l * 6 + j) * KC + c) * 2 + s
            return mod[:, i:i + 1]

        s_at = [0]

        def take(n):
            s_at[0] += n
            assert s_at[0] <= 680
            return small[:, s_at[0] - n:s_at[0]]

        cond_t = take(16)
        mod_g = take(48)
        mod_b = take(48)
        ln_scaled = take(128)
        lam_w = take(8)
        sub_g = take(1)
        phases_at = s_at[0]
        mx = take(32)
        sums = take(32)
        rsum = take(32)
        nlr = take(1)
        rms = take(8)
        s_at[0] = phases_at
        scores, biased, r_a, r_b = take(32), take(32), take(32), take(32)
        gate2, place2, place_t = take(4), take(4), take(16)
        masked, oh1, oh2, chosen, gates = (take(32) for _ in range(5))
        g8a, g8b, g8c = take(16), take(16), take(16)
        g2, w2 = take(8), take(8)
        s_at[0] = phases_at
        sp_x, sp_a, sp_b, g_tok, beta, nbeta, egc, kdec = (take(32) for _ in range(8))
        negA = take(16)
        qk_ss = take(32)
        o_ss = take(16)
        ab_raw = take(64)
        logit_t = ada_prod[:, T:2 * T]
        rstd = ada_prod[:, 0:T]
        o_d = sb("o_delta", [P, 2, 1024])
        ada_acc = o_d[:, :, :].rearrange("p b (s n) -> p b s n", s=2)

        a_at = [0]

        def ar(n, reset=False):
            if reset:
                a_at[0] = 0
            a_at[0] += n
            assert a_at[0] <= 17408, a_at[0]
            return arena[:, a_at[0] - n:a_at[0]]

        qkv = ar(6144, True).rearrange("p (s n) -> p s n", s=2)
        heads_t = ar(4096).rearrange("p (w s c n) -> p w s c n", w=4, s=2, c=4)
        nkc = ar(512).rearrange("p (c n) -> p c n", c=4)
        nvc = ar(512)
        dkc = ar(512).rearrange("p (c n) -> p c n", c=4)
        dvc = ar(512)
        bias = ar(1024).rearrange("p (h n) -> p h n", h=8)
        probs = ar(1024).rearrange("p (b j n) -> p b j n", b=2, j=2)
        probs_t = ar(1024).rearrange("p (b j n) -> p b j n", b=2, j=2)
        o_tok = ar(2048).rearrange("p (s n) -> p s n", s=2)
        lam_p = o_tok[:, 0, 0:256]
        even_c = o_tok[:, 0, 256:512]
        rope_1 = probs.rearrange("p b j n -> p (b j n)")[:, 0:512]
        rope_2 = probs.rearrange("p b j n -> p (b j n)")[:, 512:1024]
        o_sq = qkv[:, 0, 0:1024]

        xg = ar(5120, True).rearrange("p (c n) -> p c n", c=KC)
        ys = arena[:, 0:4096].rearrange("p (t n) -> p t n", t=4)
        yt = ar(5120).rearrange("p (c n) -> p c n", c=KC)
        yt_flat = arena[:, 5120:10240]
        h_tok = yt_flat[:, 0:2048].rearrange("p (s n) -> p s n", s=2)
        sel = yt_flat[:, 2048:3072].rearrange("p (s n) -> p s n", s=2)
        gsel = yt_flat[:, 3072:4096].rearrange("p (s n) -> p s n", s=2)
        eq = yt_flat[:, 4096:4608], yt_flat[:, 4608:5120]
        gate_t = ar(1024).rearrange("p (t n) -> p t n", t=4)
        sg = ar(1024).rearrange("p (b n) -> p b n", b=2)
        he = ar(1024).rearrange("p (b n) -> p b n", b=2)
        sg2, he2 = ar(512), ar(512)
        y_tok = arena[:, 0:2048].rearrange("p (s n) -> p s n", s=2)

        dqkv = ar(6144, True).rearrange("p (s n) -> p s n", s=2)
        dgate = ar(2048).rearrange("p (s n) -> p s n", s=2)
        qk_t = ar(4096).rearrange("p (w s h n) -> p w s h n", w=2, s=2, h=HEADS)
        work_at = a_at[0]
        zpad = ar(3 * 260).rearrange("p (b s n) -> p b s n", b=3, s=2)
        conv_o = ar(3 * 256).rearrange("p (b s n) -> p b s n", b=3, s=2)
        square = ar(256).rearrange("p (s n) -> p s n", s=2)
        a_at[0] = work_at
        sets = [{}, {}]
        for n in ("X", "XT", "LT", "LM", "Y"):
            for w in sets:
                w[n] = ar(512).rearrange("p (h n) -> p h n", h=4)
        for w, f in zip(sets, (dqkv[:, 0, 0:1024], dqkv[:, 1, 0:1024])):
            w["AT"] = f.rearrange("p (d h n) -> p d h n", d=2, h=4)
        st_stage = dqkv[:, 1, 1024:2048].rearrange("p (b h n) -> p b h n", b=2, h=4)
        st_buf = [[st_stage[:, 0], st_stage[:, 1]], [sets[0]["XT"], sets[1]["XT"]]]
        o_square = dqkv[:, 1, 1024:2048]
        act_flat = act_t[:, :, :].rearrange("p c n -> p (c n)")
        s0 = act_flat.rearrange("p (d h n) -> p d h n", d=2, h=HEADS)
        decay = [f.rearrange("p (u d h n) -> p u d h n", u=2, d=2, h=4) for f in (act_flat, dqkv[:, 0, 1024:3072])]

        def bcast(ap, n):
            return ap.unsqueeze(2).to_broadcast([ap.shape[0], ap.shape[1], n])

        block = ctx.enter_context(nc.Block())

        class Chain:

            def __init__(self, eng, name):
                self.eng, self.sem, self.n = eng, S(name), 0

            def link(self, ins):
                ins.then_inc(self.sem, 1)
                self.n += 1
                self.eng.wait_ge(self.sem, self.n)

            def post(self, ins):
                ins.then_inc(self.sem, 1)
                self.n += 1

        meet_n = {}

        def meet(eng, name):
            meet_n[name] = meet_n.get(name, 0) + 1
            eng.drain().then_inc(S("phase_done"), 1)
            eng.wait_ge(S("phase_done"), 4 * meet_n[name])

        def at_ring(n0, off=0):
            return (n0 + off) % RING, (n0 + off) // RING

        def wait_slot(eng, n0, off=0, turns=None):
            k, t = at_ring(n0, off)
            if turns is None:
                eng.wait_ge(slot_full[k], 16 * (t + 1))
            else:
                eng.wait_ge(slot_full[k], turns * 16 + 16 * (t + 1))
            return k

        def ada_wait(eng, job):
            eng.wait_ge(S("ada_by_dve"), job + 1 - len([j for j in PE_JOBS if j <= job]))
            if job in POOL_JOBS:
                eng.wait_ge(S("ada_by_pool"), POOL_JOBS.index(job) + 1)

        def ada_part(eng, ch, streams, job, chunks=range(KC)):
            k, t = at_ring(ADA_SLOTS[job])
            w = ring[:, k, :].rearrange("p (c n) -> p c n", c=KC)
            if chunks[0] == 0:
                eng.wait_ge(slot_full[k], 16 * (t + 1))
                if job >= 2:
                    eng.wait_ge(S("ada_sums"), job - 1)
            for c in chunks:
                for s in streams:
                    acc, col = ada_acc[:, job % 2, s, :], cond_t[:, 2 * c + s:2 * c + s + 1]
                    if c == 0:
                        ins = eng.tensor_scalar(acc, w[:, c, :], col, None, ALU.mult)
                    elif eng is nc.gpsimd:
                        ch.link(eng.tensor_scalar(ada_prod[:, :], w[:, c, :], col, None, ALU.mult))
                        ins = eng.tensor_tensor(acc, acc, ada_prod[:, :], ALU.add)
                    else:
                        ins = eng.scalar_tensor_tensor(acc, w[:, c, :], col, acc, ALU.mult, ALU.add)
                    if c == KC - 1 and s == streams[-1]:
                        ins.then_inc(S("ada_by_pool" if eng is nc.gpsimd else "ada_by_dve"), 1)
                    elif c < KC - 1 and s == streams[0] and len(streams) == 2:
                        ch.post(ins)
                    else:
                        ch.link(ins)
            if 1 in streams and chunks[-1] == KC - 1:
                ada_wait(eng, job)
                eng.sem_inc(slot_free[k], 1)

        def ada_dve(dve, ch, job, chunks=range(KC)):
            ada_part(dve, ch, (0,) if job in POOL_JOBS else (0, 1), job, chunks)

        def ada_pool(pool, ch, first, end):
            for job in range(first, end):
                if job in POOL_JOBS:
                    ada_part(pool, ch, (1,), job)

        def ada_sum(pe, job, bk):
            ada_wait(pe, job)
            if job >= 1:
                pe.wait_ge(S("ada_stored"), job)
            for m in range(4):
                for s in range(2):
                    last = pe.matmul(bk[:, 2 * m + s:2 * m + s + 1], ada_acc[:, job % 2, s, m * P:(m + 1) * P], ones[:, :],
                                     start=True, stop=True)
            last.then_inc(S("ada_sums"), 1)

        def ada_rows(pe, n, bk):
            job = PE_JOBS[n]
            k, t = at_ring(ADA_SLOTS[job])
            pe.wait_ge(slot_full[k], 16 * (t + 1))
            if job >= ADA_FIRST:
                pe.wait_ge(S("ada_stored"), job)
            w = ring[:, k, :].rearrange("p (c n) -> p c n", c=KC)
            for c in range(KC):
                last = pe.matmul(bk[0:2, :], cond_t[:, 2 * c:2 * c + 2], w[:, c, :], start=(c == 0), stop=(c == KC - 1))
            last.then_inc(S("ada_rows"), 1)

        def ada_copy(act, n, bk):
            act.wait_ge(S("ada_rows"), n + 1)
            act.activation(ada_acc[0:2, PE_JOBS[n] % 2, 0, :], bk[0:2, :], ACT.Copy).then_inc(S("ada_copied"), 1)
            act.sem_inc(slot_free[at_ring(ADA_SLOTS[PE_JOBS[n]])[0]], 1)

        def ada_columns(pe, n, bk):
            pe.wait_ge(S("ada_copied"), n + 1)
            for m in range(4):
                last = pe.transpose(bk[:, 2 * m:2 * m + 2], ada_acc[0:2, PE_JOBS[n] % 2, 0, m * P:(m + 1) * P],
                                    ident[0:2, 0:2])
            last.then_inc(S("ada_sums"), 1)

        def ada_store(dve, job, bk):
            dve.wait_ge(S("ada_sums"), job + 1)
            sl = slice(8 * job, 8 * job + 8)
            dve.tensor_tensor(mod[:, sl], bk[:, 0:8], p_("ada_b")[:, sl], ALU.add).then_inc(S("ada_stored"), 1)

        def fold_norm(dve, ch, site, l, j):
            sl = slice(site * 16, site * 16 + 16)
            shift, scale = (mod_v[:, l, j + i].rearrange("p c s -> p (c s)") for i in range(2))
            ch.link(dve.tensor_scalar(scale, scale, 1.0, None, ALU.add))
            ch.link(dve.tensor_tensor(mod_g[:, sl], p_("ln_g")[:, sl], scale, ALU.mult))
            ch.link(dve.tensor_tensor(mod_b[:, sl], p_("ln_b")[:, sl], scale, ALU.mult))
            ch.link(dve.tensor_tensor(mod_b[:, sl], mod_b[:, sl], shift, ALU.add))

        MOE_JOBS = ((3, 4, 5), (6, 7))
        LN_BANKS = ((6, 7), (0, 1), (6, 7), (0, 1))

        def ln_pe(pe, site):
            for half, (name, src) in enumerate((("ln_mean", res), ("ln_var", act_t))):
                for c in range(KC):
                    if half == 0 and c % 2 == 0:
                        pe.wait_ge(S("res_ready"), 4 * site + c // 2 + 1)
                    if half == 1 and c % 4 == 0:
                        pe.wait_ge(S("ln_sq"), 2 * site + c // 4 + 1)
                    last = pe.matmul(bank[LN_BANKS[site][half]][:, 0:T], c_("mean"), src[:, c, :], start=(c == 0), stop=(c == KC - 1))
                last.then_inc(S(name), 1)
            if site % 2 == 0:
                ada_rows(pe, MOE_JOBS[site // 2][0], bank[LN_BANKS[site][0]])

        def ln_act(act, ch, site):
            for h in range(2):
                act.wait_ge(S("ln_centred"), 2 * site + h + 1)
                act.activation(act_t[:, 4 * h:4 * h + 4, :], res[:, 4 * h:4 * h + 4, :], ACT.Square).then_inc(S("ln_sq"), 1)
            act.wait_ge(S("ln_eps"), site + 1)
            ch.link(act.activation(rstd, rstd, ACT.Ln))
            act.activation(rstd, rstd, ACT.Exp, scale=-0.5).then_inc(S("ln_rstd"), 1)
            if site < 3:
                act.wait_ge(S("ln_norm"), 2 * site + 2)
                for c in range(4, KC):
                    for s in range(2):
                        i = site * 16 + 2 * c + s
                        last = act.activation(act_t[:, c, s * P:(s + 1) * P], res[:, c, s * P:(s + 1) * P], ACT.Identity,
                                              scale=mod_g[:, i:i + 1], bias=mod_b[:, i:i + 1])
                last.then_inc(S("ln_h"), 1)
                if site % 2 == 0:
                    ada_copy(act, MOE_JOBS[site // 2][0], bank[LN_BANKS[site][0]])

        def ln_dve(dve, ch, site):
            dve.wait_ge(S("ln_mean"), site + 1)
            banks = [bank[b][:, 0:T] for b in LN_BANKS[site]]
            halves = [res[:, 4 * h:4 * h + 4, :] for h in range(2)]
            for h in range(2):
                dve.tensor_tensor(halves[h], halves[h], banks[0].unsqueeze(1).to_broadcast([P, 4, T]),
                                  ALU.subtract).then_inc(S("ln_centred"), 1)
            dve.wait_ge(S("ln_var"), site + 1)
            dve.tensor_scalar(rstd, banks[1], EPS, None, ALU.add).then_inc(S("ln_eps"), 1)
            dve.wait_ge(S("ln_rstd"), site + 1)
            dve.wait_ge(S("ln_centred"), 2 * site + 2)
            for h in (1, 0):
                dve.tensor_tensor(halves[h], halves[h], rstd.unsqueeze(1).to_broadcast([P, 4, T]),
                                  ALU.mult).then_inc(S("ln_norm"), 1)
            if site < 3:
                dve.wait_ge(S("ln_norm"), 2 * site + 2)
                rv = res[:, 0:4, :].rearrange("p c (s n) -> p (c s) n", s=2)
                av = act_t[:, 0:4, :].rearrange("p c (s n) -> p (c s) n", s=2)
                ch.link(dve.tensor_tensor(av, rv, bcast(mod_g[:, site * 16:site * 16 + 8], P), ALU.mult))
                dve.tensor_tensor(av, av, bcast(mod_b[:, site * 16:site * 16 + 8], P), ALU.add).then_inc(S("ln_h"), 1)

        def ln_pool(pool, site):
            pool.wait_ge(S("ln_norm"), 2 * site + 2)
            if site < 3:
                pool.wait_ge(S("ln_h"), 2 * site + 2)
            meet(pool, "pool")
            for c in range(KC):
                i = site * 16 + 2 * c
                pool.tensor_scalar(res[:, c, :], res[:, c, :], ln_scaled[:, 0 + i:i + 1],
                                   ln_scaled[:, 64 + i:65 + i], ALU.mult, ALU.add).then_inc(S("res_scaled"), 1)


        N_R2 = 6

        def nth(i, n):
            return n if i is None else 2 * i + n

        def one(i, n):
            return slice(n, n + 1) if i is None else bass.ds(2 * i + n, 1)

        def second_round(eng, i, n, layer, body, skipped=None):
            count = eng.value_load(flags[0:1, 0, one(i, n)], min_val=0, max_val=T)
            with eng.If(count > CAP):
                body(nth(i, n) * N_R2 + 16 * N_R2 * layer)
            if skipped is not None:
                with eng.Else():
                    skipped()

        def first_slot(eng, i, n, most=2 * T):
            return eng.value_load(flags[0:1, 1, one(i, n)], min_val=0, max_val=most)

        def transposes(pe, bk, srcs):
            for j, src in enumerate(srcs):
                last = pe.transpose(bk[:, j * P:(j + 1) * P], src, ident)
            return last

        def moe_pe(pe, layer, n0):
            L = layer
            for c in range(KC):
                last = pe.matmul(bank[1][0:16, 0:T], p_("router")[:, c * 16:c * 16 + 16], act_t[:, c, :],
                                 start=(c == 0), stop=(c == KC - 1))
            last.then_inc(S("logits_t"), 1)
            jobs = MOE_JOBS[L]
            ada_columns(pe, jobs[0], bank[6])
            for n in range(4):
                s, q = n // 2, n % 2
                transposes(pe, bank[2 + n], [act_t[:, 4 * q + j, s * P:(s + 1) * P] for j in range(4)])\
                    .then_inc(S("htok_done"), 1)
                if n == 0:
                    pe.wait_ge(S("logits_copied"), L + 1)
                    for s_ in range(2):
                        last = pe.transpose(bank[0][:, s_ * 16:s_ * 16 + 16], logit_t[0:16, s_ * P:(s_ + 1) * P],
                                            ident[0:16, 0:16])
                    last.then_inc(S("logits"), 1)
            ada_rows(pe, jobs[1], bank[6])
            pe.wait_ge(S("chosen_ready"), L + 1)
            pe.matmul(bank[1][:, 0:16], c_("lt"), chosen[:, 0:16], start=True, stop=True)
            pe.matmul(bank[1][:, 16:32], c_("lt"), chosen[:, 16:32], start=True, stop=False)
            for m in ("le", "gt"):
                pe.matmul(bank[1][:, 16:32], c_(m), chosen[:, 0:16], start=False, stop=(m == "gt"))
            for k, (m, s) in enumerate((("le", 0), ("gt", 0), ("le", 1), ("gt", 1))):
                last = pe.matmul(bank[1][:, 32:48], c_(m), chosen[:, s * 16:s * 16 + 16], start=(k == 0), stop=(k == 3))
            last.then_inc(S("rank_done"), 1)
            ada_columns(pe, jobs[1], bank[6])
            if len(jobs) == 3:
                ada_rows(pe, jobs[2], bank[6])
            pe.wait_ge(S("htok_copied"), 4 * (L + 1))
            pe.wait_ge(S("sel_ready"), 2 * (L + 1))
            for c in range(KC):
                if c >= 4:
                    pe.wait_ge(S("xg_copied"), c - 3 + 8 * L)
                for s in range(2):
                    last = pe.matmul(bank[2 + c % 4][:, :], h_tok[:, s, c * P:(c + 1) * P], sel[:, s, :],
                                     start=(s == 0), stop=(s == 1))
                last.then_inc(S("xg_done"), 1)
            if len(jobs) == 3:
                ada_columns(pe, jobs[2], bank[6])
            pe.wait_ge(S("ada_stored"), (ADA_MOE0, N_ADA)[L])
            pe.wait_ge(S("gsel_ready"), 2 * (L + 1))
            for b in range(2):
                transposes(pe, bank[6 + b], [gsel[:, s, t * P:(t + 1) * P] for t in (2 * b, 2 * b + 1) for s in range(2)])\
                    .then_inc(S("gate_done"), 1)
            pe.wait_ge(S("xg_copied"), 8 * (L + 1))
            pe.wait_ge(S("gate_copied"), 2 * (L + 1))
            pe.wait_ge(S("flags_ready"), L + 1)

            def gate_up_products(n, par, window, wait):
                for m in range(2):
                    k = (n0 + 3 * n + m) % RING
                    if wait:
                        wait_slot(pe, n0, 3 * n + m, wait[0])
                    w = ring[:, k, :].rearrange("p (c n) -> p c n", c=KC)
                    for f in range(FC):
                        for c in range(KC):
                            last = pe.matmul(bank[2 * m + par][:, f * P:(f + 1) * P], w[:, c, f * P:(f + 1) * P],
                                             xg[:, c, window], start=(c == 0), stop=(c == KC - 1))
                return last

            def down_products(n, h, par, src):
                w = ring[:, (n0 + 3 * n + 2) % RING, :].rearrange("p (f n) -> p f n", f=FC)
                for o in range(4):
                    for f in range(FC):
                        last = pe.matmul(bank[4 + 2 * par + h][:, o * P:(o + 1) * P],
                                         w[:, f, (4 * h + o) * P:(4 * h + o + 1) * P], src[:, f * P:(f + 1) * P],
                                         start=(f == 0), stop=(f == FC - 1))
                return last

            def gate_up(i, n):
                at = first_slot(pe, i, n)
                gate_up_products(n, n % 2, bass.ds(at, P), (i,)).then_inc(S("gu_done"), 1)
                second_round(pe, i, n, L, lambda base: round2(i, n, base))
                pe.wait_ge(S("round2"), nth(i, n) * N_R2 + (N_R2 + 16 * N_R2 * L))

            def round2(i, n, base):
                at = first_slot(pe, i, n, 2 * T - CAP)
                if not (i is None and n == 0):
                    pe.wait_ge(S("he_ready"), nth(i, n) + 16 * L)
                gate_up_products(n, 1 - n % 2, bass.ds(at + CAP, P), None).then_inc(S("round2"), 1)
                wait_slot(pe, n0, 3 * n + 2, i)
                pe.wait_ge(S("y_copied"), 2 * nth(i, n) + (2 + 36 * L))
                pe.wait_ge(S("round2"), base + 3)
                for h in range(2):
                    last = down_products(n, h, n % 2, he2)
                last.then_inc(S("round2"), 1)

            def down(i, n):
                wait_slot(pe, n0, 3 * n + 2, i)
                pe.wait_ge(S("he_ready"), nth(i, n) + (1 + 16 * L))
                pe.wait_ge(S("y_copied"), 2 * nth(i, n) + (2 + 36 * L))
                for h in range(2):
                    down_products(n, h, n % 2, he[:, n % 2, :]).then_inc(S("y_done"), 1)

            gate_up(None, 0)
            with pe.Fori(0, 7) as i:
                gate_up(i, 1)
                down(i, 0)
                gate_up(i, 2)
                down(i, 1)
            gate_up(None, 15)
            down(None, 14)
            down(None, 15)
            pe.wait_ge(S("y_copied"), 36 * (L + 1))
            for n in range(8):
                t, q = n // 2, n % 2
                if n >= 4:
                    pe.wait_ge(S(f"ys_copied{n % 2}"), (n - 4) // 2 + 1 + 4 * L)
                transposes(pe, bank[n % 4], [yt[:, 4 * q + j, t * P:(t + 1) * P] for j in range(4)])\
                    .then_inc(S("ys_done"), 1)
            for i in range(2):
                pe.wait_ge(S(f"ys_copied{i}"), 4 * (L + 1))
            for b in range(4):
                for o in range(2):
                    c = 2 * b + o
                    for t in range(4):
                        last = pe.matmul(bank[4 + b][:, o * T:(o + 1) * T], ys[:, t, c * P:(c + 1) * P],
                                         gate_t[:, t, :], start=(t == 0), stop=(t == 3))
                last.then_inc(S("moe_out"), 1)

        def moe_act(act, ch, layer, n0):
            L = layer
            act.wait_ge(S("logits_t"), L + 1)
            act.activation(logit_t[0:16, :], bank[1][0:16, 0:T], ACT.Copy).then_inc(S("logits_copied"), 1)
            act.wait_ge(S("logits"), L + 1)
            act.activation(scores, bank[0][:, 0:32], ACT.Exp, scale=-1.0).then_inc(S("sig_exp"), 1)
            for n in range(4):
                s, q = n // 2, n % 2
                act.wait_ge(S("htok_done"), 4 * L + n + 1)
                act.activation(h_tok[:, s, q * 512:(q + 1) * 512], bank[2 + n][:, :], ACT.Copy).then_inc(S("htok_copied"), 1)
            for n in MOE_JOBS[L][1:]:
                ada_copy(act, n, bank[6])
            for c in range(KC):
                act.wait_ge(S("xg_done"), c + 1 + 8 * L)
                act.activation(xg[:, c, 0:512], bank[2 + c % 4][:, :], ACT.Copy).then_inc(S("xg_copied"), 1)
            for b in range(2):
                act.wait_ge(S("gate_done"), b + 1 + 2 * L)
                act.activation(gate_t[:, 2 * b:2 * b + 2, :], bank[6 + b][:, :].rearrange("p (t n) -> p t n", t=2), ACT.Copy)\
                    .then_inc(S("gate_copied"), 1)
            act.wait_ge(S("flags_ready"), L + 1)
            act.sem_inc(S("y_copied"), 4)

            def silu(i, n):
                act.wait_ge(S("gu_done"), nth(i, n) + (1 + 16 * L))
                act.activation(sg[:, n % 2, :], bank[n % 2][:, :], ACT.Silu).then_inc(S("silu_done"), 1)

                def body(base):
                    act.wait_ge(S("round2"), base + 1)
                    act.activation(sg2, bank[1 - n % 2][:, :], ACT.Silu).then_inc(S("round2"), 1)
                    at = first_slot(act, i, n, 2 * T - CAP)
                    act.wait_ge(S("round2"), base + 4)
                    for h in range(2):
                        act.activation(yt[:, 4 * h:4 * h + 4, bass.ds(at + CAP, P)],
                                       bank[4 + 2 * (n % 2) + h][:, :].rearrange("p (o n) -> p o n", o=4), ACT.Copy)\
                            .then_inc(S("round2"), 1)
                second_round(act, i, n, L, body)
                for m in range(2):
                    act.sem_inc(slot_free[at_ring(n0, 3 * n + m)[0]], 1)

            def y_copy(i, n):
                at = first_slot(act, i, n)
                act.wait_ge(S("y_copied"), 2 * nth(i, n) + (4 + 36 * L))
                for h in range(2):
                    act.wait_ge(S("y_done"), 2 * nth(i, n) + (h + 1 + 32 * L))
                    act.activation(yt[:, 4 * h:4 * h + 4, bass.ds(at, P)],
                                   bank[4 + 2 * (n % 2) + h][:, :].rearrange("p (o n) -> p o n", o=4), ACT.Copy)\
                        .then_inc(S("y_copied"), 1)
                act.sem_inc(slot_free[at_ring(n0, 3 * n + 2)[0]], 1)

            silu(None, 0)
            with act.Fori(0, 7) as i:
                silu(i, 1)
                y_copy(i, 0)
                silu(i, 2)
                y_copy(i, 1)
            silu(None, 15)
            y_copy(None, 14)
            y_copy(None, 15)
            for n in range(0, 8, 2):
                act.wait_ge(S("ys_done"), n + 1 + 8 * L)
                act.activation(ys[:, n // 2, 0:512], bank[n % 4][:, :], ACT.Copy).then_inc(S("ys_copied0"), 1)

        def moe_dve(dve, ch, layer, n0):
            L = layer
            jobs = [PE_JOBS[n] for n in MOE_JOBS[L]]
            ada_store(dve, jobs[0], bank[6])
            ch.link(dve.memset(xg[:, :, 2 * T:2 * T + P], 0.0))
            dve.wait_ge(S("sig_exp"), L + 1)
            ch.link(dve.tensor_scalar(scores, scores, 1.0, None, ALU.add))
            ch.link(dve.reciprocal(scores, scores))
            sv = scores.rearrange("p (s e) -> p s e", s=2)
            ch.link(dve.tensor_tensor(biased.rearrange("p (s e) -> p s e", s=2), sv,
                                      p_("router_b").unsqueeze(1).to_broadcast([P, 2, 16]), ALU.add))
            bv = biased.rearrange("p (g k) -> p g k", k=4)
            a8 = g8a.rearrange("p (g k) -> p g k", k=2)
            b8 = g8b.rearrange("p (g k) -> p g k", k=2)
            dve.tensor_tensor(a8, bv[:, :, 0:2], bv[:, :, 2:4], ALU.max).then_inc(S("dve_par"), 1)
            dve.tensor_tensor(b8, bv[:, :, 0:2], bv[:, :, 2:4], ALU.min).then_inc(S("dve_par"), 1)
            dve.wait_ge(S("dve_par"), 2 * L + 2)
            c8 = g8c.rearrange("p (g k) -> p g k", k=2)
            ch.link(dve.tensor_tensor(c8[:, :, 0], a8[:, :, 0], a8[:, :, 1], ALU.max))
            ch.link(dve.tensor_tensor(c8[:, :, 1], a8[:, :, 0], a8[:, :, 1], ALU.min))
            ch.link(dve.tensor_tensor(a8[:, :, 0], b8[:, :, 0], b8[:, :, 1], ALU.max))
            ch.link(dve.tensor_tensor(a8[:, :, 1], a8[:, :, 0], c8[:, :, 1], ALU.max))
            ch.link(dve.tensor_tensor(b8[:, :, 0], a8[:, :, 1], c8[:, :, 0], ALU.add))

            def first_best(dst, src, n, rank, top, tmp):
                sv_ = src.rearrange("p (s n) -> p s n", s=2)
                tv, dv_ = tmp.rearrange("p (s n) -> p s n", s=2), dst.rearrange("p (s n) -> p s n", s=2)
                ch.link(dve.tensor_reduce(top, sv_, AX, ALU.max))
                ch.link(dve.tensor_tensor(tv, sv_, bcast(top, n), ALU.is_equal))
                ch.link(dve.tensor_tensor(tv, tv, rank.unsqueeze(1).to_broadcast([P, 2, n]), ALU.mult))
                ch.link(dve.tensor_reduce(top, tv, AX, ALU.max))
                ch.link(dve.tensor_tensor(dv_, tv, bcast(top, n), ALU.is_equal))

            gsc = g8c[:, 8:16]
            ch.link(dve.tensor_copy(gsc, b8[:, :, 0]))
            first_best(g2, gsc, 4, c_("rank4"), w2[:, 0:2], g8a[:, 0:8])
            in_group = g2.unsqueeze(2).to_broadcast([P, 8, 4])
            rv = r_a.rearrange("p (g k) -> p g k", k=4)
            ch.link(dve.tensor_tensor(rv, bv, in_group, ALU.mult))
            ch.link(dve.tensor_scalar(g8b[:, 0:8], g2, BIG, -BIG, ALU.mult, ALU.add))
            ch.link(dve.tensor_tensor(masked.rearrange("p (g k) -> p g k", k=4), rv,
                                      bcast(g8b[:, 0:8], 4), ALU.add))
            first_best(oh1, masked, 16, c_("rank16"), w2[:, 0:2], r_b)
            ch.link(dve.scalar_tensor_tensor(masked, oh1, -3.0 * BIG, masked, ALU.mult, ALU.add))
            first_best(oh2, masked, 16, c_("rank16"), w2[:, 0:2], r_b)
            dve.tensor_tensor(chosen, oh1, oh2, ALU.add).then_inc(S("chosen_ready"), 1)
            dve.wait_ge(S("chosen_ready"), L + 1)
            ch.link(dve.tensor_tensor(r_a, chosen, scores, ALU.mult))
            ch.link(dve.tensor_reduce(w2[:, 2:4], r_a.rearrange("p (s e) -> p s e", s=2), AX, ALU.add))
            ch.link(dve.reciprocal(w2[:, 4:6], w2[:, 2:4]))
            ch.link(dve.tensor_tensor(gates.rearrange("p (s e) -> p s e", s=2), r_a.rearrange("p (s e) -> p s e", s=2),
                                      bcast(w2[:, 4:6], 16), ALU.mult))
            for k, oh in enumerate((oh1, oh2)):
                ch.link(dve.tensor_tensor(r_b, oh, gates, ALU.mult))
                ch.link(dve.tensor_reduce(gate2[:, 2 * k:2 * k + 2], r_b.rearrange("p (s e) -> p s e", s=2), AX, ALU.add))
            dve.wait_ge(S("rank_done"), L + 1)
            ada_store(dve, jobs[1], bank[6])
            ch.link(dve.tensor_copy(r_b[:, 0:16], bank[1][:, 32:48]))
            run_a, run_b = g8a, g8b
            ch.link(dve.memset(run_a[:, 0:1], 0.0))
            ch.link(dve.tensor_copy(run_a[:, 1:16], r_b[:, 0:15]))
            for k in (1, 2, 4, 8):
                ch.link(dve.tensor_copy(run_b[:, 0:k], run_a[:, 0:k]))
                ch.link(dve.tensor_tensor(run_b[:, k:16], run_a[:, k:16], run_a[:, 0:16 - k], ALU.add))
                run_a, run_b = run_b, run_a
            ch.link(dve.tensor_copy(flags[:, 0, :], r_b[:, 0:16]))
            dve.tensor_copy(flags[:, 1, :], run_a).then_inc(S("flags_ready"), 1)
            ch.link(dve.tensor_tensor(masked.rearrange("p (s e) -> p s e", s=2),
                                      bank[1][:, 0:32].rearrange("p (s e) -> p s e", s=2),
                                      run_a.unsqueeze(1).to_broadcast([P, 2, 16]), ALU.add))
            for k, oh in enumerate((oh1, oh2)):
                ch.link(dve.tensor_tensor(r_b, oh, masked, ALU.mult))
                ch.link(dve.tensor_reduce(place2[:, 2 * k:2 * k + 2], r_b.rearrange("p (s e) -> p s e", s=2), AX, ALU.add))
            ch.link(dve.tensor_tensor(place_t.rearrange("p (k t) -> p k t", t=4), bcast(place2, 4),
                                      c_("tile4").unsqueeze(1).to_broadcast([P, 4, 4]), ALU.subtract))
            for s in range(2):
                for k, dst in enumerate((gsel[:, s, :], eq[s])):
                    i4 = (2 * k + s) * 4
                    ch.post(dve.tensor_tensor(dst.rearrange("p (t n) -> p t n", t=4),
                                              c_("iota").unsqueeze(1).to_broadcast([P, 4, P]),
                                              bcast(place_t[:, i4:i4 + 4], P), ALU.is_equal))
                dve.wait_ge(ch.sem, ch.n)
                dve.tensor_tensor(sel[:, s, :], gsel[:, s, :], eq[s], ALU.add).then_inc(S("sel_ready"), 1)
            dve.wait_ge(S("sel_ready"), 2 * (L + 1))
            for s in range(2):
                ch.link(dve.tensor_scalar(gsel[:, s, :], gsel[:, s, :], gate2[:, s:s + 1], None, ALU.mult))
                dve.scalar_tensor_tensor(gsel[:, s, :], eq[s], gate2[:, 2 + s:3 + s], gsel[:, s, :], ALU.mult, ALU.add)\
                    .then_inc(S("gsel_ready"), 1)
            if L == 0:
                ada_store(dve, jobs[2], bank[6])
                dve.wait_ge(S("ada_stored"), ADA_MOE0)
                fold_norm(dve, ch, 1, 1, 0)

            def he_product(i, n):
                def body(base):
                    dve.wait_ge(S("round2"), base + 2)
                    dve.tensor_tensor(he2, sg2, bank[3 - n % 2][:, :], ALU.mult).then_inc(S("round2"), 1)

                if not (i is None and n == 0 and L == 0):
                    dve.wait_ge(S("round2"), nth(i, n) * N_R2 + 16 * N_R2 * L)
                second_round(dve, i, n, L, body, lambda: dve.sem_inc(S("round2"), N_R2))
                dve.wait_ge(S("silu_done"), nth(i, n) + (1 + 16 * L))
                dve.tensor_tensor(he[:, n % 2, :], sg[:, n % 2, :], bank[2 + n % 2][:, :], ALU.mult)\
                    .then_inc(S("he_ready"), 1)

            he_product(None, 0)
            with dve.Fori(0, 7) as i:
                he_product(i, 1)
                he_product(i, 2)
            he_product(None, 15)
            for n in range(1, 8, 2):
                dve.wait_ge(S("ys_done"), n + 1 + 8 * L)
                dve.tensor_copy(ys[:, n // 2, 512:1024], bank[n % 4][:, :]).then_inc(S("ys_copied1"), 1)
            for b in range(4):
                dve.wait_ge(S("moe_out"), b + 1 + 4 * L)
                dve.wait_ge(S("res_scaled"), 2 * KC * L + 2 * b + 2)
                for o in range(2):
                    for s in range(2):
                        c = 2 * b + o
                        r = res[:, c, s * P:(s + 1) * P]
                        last = dve.scalar_tensor_tensor(r, bank[4 + b][:, o * T + s * P:o * T + (s + 1) * P],
                                                        gate_col(layer, 5, c, s), r, ALU.mult, ALU.add)
                last.then_inc(S("res_ready"), 1)
            dve.wait_ge(S("res_ready"), 8 * L + 8)

        def out_pe(pe, layer, n0):
            for q in range(2):
                k = wait_slot(pe, n0, q)
                w = ring[:, k, :].rearrange("p (c n) -> p c n", c=KC)
                for b in range(2):
                    for o in range(2):
                        m = 2 * b + o
                        for c in range(KC):
                            last = pe.matmul(bank[2 * q + b][:, o * T:(o + 1) * T], w[:, c, m * P:(m + 1) * P],
                                             act_t[:, c, :], start=(c == 0), stop=(c == KC - 1))
                    last.then_inc(S("mix_done"), 1)

        def out_dve(dve, ch, layer, n0):
            for q in range(2):
                for b in range(2):
                    dve.wait_ge(S("mix_done"), 4 * layer + 2 * q + b + 1)
                    if layer == 1:
                        dve.wait_ge(S("res_scaled"), KC + 4 * q + 2 * b + 2)
                    for o in range(2):
                        for s in range(2):
                            c = 4 * q + 2 * b + o
                            r = res[:, c, s * P:(s + 1) * P]
                            last = dve.scalar_tensor_tensor(r, bank[2 * q + b][:, o * T + s * P:o * T + (s + 1) * P],
                                                            gate_col(layer, 2, c, s), r, ALU.mult, ALU.add)
                    last.then_inc(S("res_ready"), 1)
                dve.sem_inc(slot_free[at_ring(n0, q)[0]], 1)
            dve.wait_ge(S("res_ready"), 8 * layer + 4)

        DIRS = (("le", "gt"), ("ge", "lt"))

        def lev(s, lv, u):
            return s * 2 * (LEVELS - 1) + 2 * (lv - 1) + u + 1

        def heads4(ap):
            return ap.rearrange("p (h n) -> p h n", h=4)

        def mask4(ap):
            return ap.unsqueeze(1).to_broadcast([P, 4, P])

        def level_mask(name, lv):
            return mask4(c_(name)[:, lv * P:(lv + 1) * P])

        def per_head(x, s, d, u):
            i = (s * 2 + d) * 8 + 4 * u
            return bcast(x[:, i:i + 4], P)

        def delta_pe(pe):
            def tr(i):
                pe.wait_ge(S("conv_done"), i + 1)
                if i >= 2:
                    pe.wait_ge(S("tok_copied"), i - 1)
                for s in range(2):
                    last = pe.transpose(bank[4 + i % 2][:, s * P:(s + 1) * P], conv_o[:, i % 3, s, :], ident)
                last.then_inc(S("tok_done"), 1)

            for i in range(24):
                k = wait_slot(pe, OIN0, 2 * (i // 4))
                if i >= 3:
                    pe.wait_ge(S("z_copied"), i - 2)
                w = ring[:, k, :].rearrange("p (c n) -> p c n", c=KC)
                for c in range(KC):
                    last = pe.matmul(bank[i % 3][:, 0:T], w[:, c, (i % 4) * P:(i % 4 + 1) * P], act_t[:, c, :],
                                     start=(c == 0), stop=(c == KC - 1))
                last.then_inc(S("z_done"), 1)
                if i == 20:
                    for s in range(2):
                        for c in range(KC):
                            last = pe.matmul(bank[3][:, s * 32:s * 32 + 32], act_t[:, c, s * P:(s + 1) * P],
                                             p_("w_ab")[:, c * 32:c * 32 + 32], start=(c == 0), stop=(c == KC - 1))
                    last.then_inc(S("ab_done"), 1)
                if i >= 2:
                    tr(i - 2)
                if i % 4 == 3 and i >= 7:
                    ada_sum(pe, ADA_MOE0 + i // 4 - 1, bank[6])
            pe.wait_ge(S("z_copied"), 24)
            for q in range(2):
                k = wait_slot(pe, OIN0, 12 + q)
                w = ring[:, k, :].rearrange("p (c n) -> p c n", c=KC)
                for s in range(2):
                    if (q, s) == (0, 1):
                        tr(22)
                        tr(23)
                    if q == 1 and s == 1:
                        pe.wait_ge(S("ab_copied"), 1)
                    for c in range(KC):
                        last = pe.matmul(bank[2 * q + s][:, :], act_t[:, c, s * P:(s + 1) * P], w[:, c, :],
                                         start=(c == 0), stop=(c == KC - 1))
                    last.then_inc(S("dg_done"), 1)
                    if q == 0 and s == 1:
                        pe.wait_ge(S("g_ready"), 1)
                        gv = g_tok.rearrange("p (s d h) -> p s d h", s=2, d=2)
                        for i, (m, d) in enumerate((("le", 0), ("ge", 1), ("gt", 0), ("lt", 1))):
                            last = pe.matmul(bank[7][:, i * 16:i * 16 + 16], c_(m), gv[:, :, d, :], start=True, stop=True)
                        last.then_inc(S("gsum_done"), 1)
                    for n in ((), range(0, 3), range(3, 6), range(6, 8))[2 * q + s]:
                        w_, s_, hq = n // 4, (n // 2) % 2, n % 2
                        pe.wait_ge(S("qk_ready"), n + 1)
                        if n < 2:
                            pe.wait_ge(S("tok_copied"), 23 + n)
                        else:
                            pe.wait_ge(S("qkt_copied"), n - 1)
                        col = w_ * 1024 + 4 * hq * P
                        transposes(pe, bank[4 + n % 2], [dqkv[:, s_, col + j * P:col + (j + 1) * P] for j in range(4)])\
                            .then_inc(S("qkt_done"), 1)
                if q == 0:
                    ada_sum(pe, ADA_ODD - 1, bank[6])
            pe.wait_ge(S("qkt_copied"), 8)
            pe.wait_ge(S("gsum_copied"), 1)
            pe.wait_ge(S("dg_copied"), 4)
            pe.wait_ge(S("ada_stored"), ADA_ODD)
            for s in range(2):
                for u in range(2):
                    i = 2 * s + u
                    w = sets[u]
                    if s == 1:
                        pe.wait_ge(S("st_ready"), 2 * u + 2)
                        pe.wait_ge(S("gm_backward"), 3 + u)
                    for d, name in enumerate(("LM", "Y")):
                        pe.wait_ge(S(("gm_forward", "gm_backward")[d]), i + 1)
                        pe.matmul(bank[4 * u + d][:, :], c_(DIRS[d][1]), w[name].rearrange("p h n -> p (h n)"),
                                  start=True, stop=True).then_inc(S("diff_done"), 1)
                    for j in range(4):
                        kt = qk_t[:, 1, s, 4 * u + j, :]
                        pe.matmul(bank[4 * u + 2][:, j * P:(j + 1) * P], kt, kt, start=True, stop=True)
                        last = pe.matmul(bank[4 * u + 3][:, j * P:(j + 1) * P], kt, qk_t[:, 0, s, 4 * u + j, :],
                                         start=True, stop=True)
                    last.then_inc(S("kk_done"), 1)
                for u in range(2):
                    pe.wait_ge(S("xt0_ready"), 2 * s + u + 1)
                    transposes(pe, bank[4 * u], [sets[u]["XT"][:, j, :] for j in range(4)]).then_inc(S("x0_done"), 1)
                for lv in range(1, LEVELS):
                    for u in range(2):
                        w = sets[u]
                        pe.wait_ge(S("lm_ready"), lev(s, lv, u))
                        pe.wait_ge(S("xm_ready"), lev(s, lv, u))
                        for j in range(4):
                            last = pe.matmul(bank[4 * u][:, j * P:(j + 1) * P], w["LM"][:, j, :], decay[s][:, u, 0, j, :],
                                             start=True, stop=True)
                        last.then_inc(S("ly_done"), 1)
                    for u in range(2):
                        w = sets[u]
                        pe.wait_ge(S("ly_copied"), lev(s, lv, u))
                        pe.wait_ge(S("xtm_ready"), lev(s, lv, u))
                        for j in range(4):
                            xtm = decay[s][:, u, 1, j, :]
                            if lv < LEVELS - 1:
                                pe.matmul(bank[4 * u + 2][:, j * P:(j + 1) * P], xtm, w["Y"][:, j, :], start=True, stop=True)
                            last = pe.matmul(bank[4 * u + 1][:, j * P:(j + 1) * P], w["Y"][:, j, :], xtm,
                                             start=True, stop=True)
                        last.then_inc(S("dx_done"), 1)
                if s == 1:
                    pe.wait_ge(S("s0_in"), 16)
                    for u in range(2):
                        pe.wait_ge(S("x_summed"), lev(s, LEVELS - 1, u))
                        for w_, bk in ((1, 0), (0, 2)):
                            for d in range(2):
                                for j in range(4):
                                    last = pe.matmul(bank[4 * u + bk + d][:, j * P:(j + 1) * P],
                                                     qk_t[:, w_, s, 4 * u + j, :], s0[:, d, 4 * u + j, :],
                                                     start=True, stop=True)
                            last.then_inc(S("ks_done"), 1)
                for u in range(2):
                    i = 2 * s + u
                    w = sets[u]
                    pe.wait_ge(S("xt_forward"), i + 1)
                    pe.wait_ge(S("xt_backward"), i + 1)
                    if s == 1:
                        pe.wait_ge(S("rhs_ready"), u + 1)
                    for d, name in enumerate(("LM", "LT")):
                        for j in range(4):
                            h = 4 * u + j
                            r = w[name][:, j, :] if s == 1 else dqkv[:, s, 2048 + h * P:2048 + (h + 1) * P]
                            last = pe.matmul(bank[4 * u + d][:, j * P:(j + 1) * P], decay[s][:, u, d, j, :], r,
                                             start=True, stop=True)
                    last.then_inc(S("vn_done"), 1)
                for u in range(2):
                    i = 2 * s + u
                    w = sets[u]
                    pe.wait_ge(S("vn_ready"), i + 1)
                    for j in range(4):
                        for d, name in enumerate(("X", "Y")):
                            last = pe.matmul(bank[4 * u + 2][:, j * P:(j + 1) * P], w["AT"][:, d, j, :], w[name][:, j, :],
                                             start=(d == 0), stop=(d == 1))
                    last.then_inc(S("o_done"), 1)
                    if s == 0:
                        pe.wait_ge(S("kd_ready"), u + 1)
                        for d, name in enumerate(("LM", "LT")):
                            for j in range(4):
                                h = 4 * u + j
                                last = pe.matmul(bank[4 * u + 3 * d][:, j * P:(j + 1) * P],
                                                 dqkv[:, s, 1024 + h * P:1024 + (h + 1) * P], w[name][:, j, :],
                                                 start=True, stop=True)
                        last.then_inc(S("st_done"), 1)
            for s in range(2):
                pe.wait_ge(S("do_ready"), s + 1)
                for q in range(2):
                    for j in range(4):
                        c = 4 * q + j
                        last = pe.transpose(bank[2 * s + q][:, j * P:(j + 1) * P],
                                            o_d[:, s, c * P:(c + 1) * P], ident)
                    last.then_inc(S("dot_done"), 1)
            pe.wait_ge(S("dot_copied"), 4)
            pe.wait_ge(S("dot_banks_free"), 1)
            out_pe(pe, 1, OOUT0)


        def delta_act(act, ch):
            ab = ab_raw.rearrange("p (s n) -> p s n", s=2)
            for i in range(24):
                act.wait_ge(S("z_done"), i + 1)
                if i == 0:
                    act.wait_ge(S("pad_zero"), 1)
                if i >= 3:
                    act.wait_ge(S("conv_sum"), i - 2)
                act.activation(zpad[:, i % 3, :, 1:129], bank[i % 3][:, 0:T].rearrange("p (s n) -> p s n", s=2),
                               ACT.Copy).then_inc(S("z_copied"), 1)
                if i % 4 == 3:
                    act.sem_inc(slot_free[at_ring(OIN0, 2 * (i // 4))[0]], 1)
                if i >= 1:
                    act.wait_ge(S("conv_sum"), i)
                    act.activation(conv_o[:, (i - 1) % 3], conv_o[:, (i - 1) % 3], ACT.Silu).then_inc(S("conv_done"), 1)
                if 4 <= i < 20:
                    act.wait_ge(S("tok_copied"), i - 3)
                    for s in range(2):
                        h = s * 16 + i - 4
                        act.activation(square[:, s, :], dqkv[:, s, (i - 4) * P:(i - 3) * P], ACT.Square,
                                       accum_out=qk_ss[:, h:h + 1]).then_inc(S("qk_squares"), 1)
                        act.wait_ge(S("qk_squares"), 2 * (i - 4) + s + 1)
                if i == 21:
                    act.wait_ge(S("qk_ss"), 1)
                    ch.link(act.activation(qk_ss, qk_ss, ACT.Ln))
                    act.activation(qk_ss, qk_ss, ACT.Exp, scale=-0.5).then_inc(S("qk_rs"), 1)
            act.wait_ge(S("conv_sum"), 24)
            act.activation(conv_o[:, 23 % 3], conv_o[:, 23 % 3], ACT.Silu).then_inc(S("conv_done"), 1)
            act.wait_ge(S("sp_abs"), 1)
            ch.link(act.activation(sp_b, sp_b, ACT.Exp, scale=-1.0))
            act.activation(sp_b, sp_b, ACT.Ln, bias=1.0).then_inc(S("sp_ln"), 1)
            act.activation(beta.rearrange("p (s n) -> p s n", s=2), ab[:, :, 16:32], ACT.Exp, scale=-1.0)\
               .then_inc(S("beta_exp"), 1)
            act.activation(negA, p_("a_log"), ACT.Exp).then_inc(S("a_exp"), 1)

            def qkt_copy(n):
                w, s, hq = n // 4, (n // 2) % 2, n % 2
                act.wait_ge(S("qkt_done"), n + 1)
                act.activation(qk_t[:, w, s, 4 * hq:4 * hq + 4, :], heads4(bank[4 + n % 2][:, :]), ACT.Copy)\
                   .then_inc(S("qkt_copied"), 1)

            for q in range(2):
                for s in range(2):
                    act.wait_ge(S("dg_done"), 2 * q + s + 1)
                    act.activation(dgate[:, s, q * 512:(q + 1) * 512], bank[2 * q + s][:, :], ACT.Silu)\
                       .then_inc(S("dg_copied"), 1)
                    if s == 1:
                        act.sem_inc(slot_free[at_ring(OIN0, 12 + q)[0]], 1)
                    for n in ((), range(0, 3), range(3, 6), range(6, 8))[2 * q + s]:
                        qkt_copy(n)
            act.wait_ge(S("gsum_done"), 1)
            gs = bank[7][:, 0:64].rearrange("p (i s h) -> p i s h", i=4, s=2)
            ev, kv = (x.rearrange("p (s d h) -> p s d h", s=2, d=2) for x in (egc, kdec))
            for i, (dst, d) in enumerate(((ev, 0), (ev, 1), (kv, 0), (kv, 1))):
                last = act.activation(dst[:, :, d, :], gs[:, i], ACT.Exp)
            last.then_inc(S("gsum_copied"), 1)
            def out_rms(s):
                act.wait_ge(S("o_ss"), s + 1)
                ss = o_ss[:, s * 8:s * 8 + 8]
                ch.link(act.activation(ss, ss, ACT.Ln))
                act.activation(ss, ss, ACT.Exp, scale=-0.5).then_inc(S("o_rs"), 1)

            for s in range(2):
                for u in range(2):
                    for d in range(2):
                        act.wait_ge(S("diff_done"), 4 * s + 2 * u + d + 1)
                        act.activation(decay[s][:, u, d], heads4(bank[4 * u + d][:, :]), ACT.Exp).then_inc(S("dt_ready"), 1)
                for u in range(2):
                    act.wait_ge(S("x0_done"), 2 * s + u + 1)
                    act.activation(sets[u]["X"], heads4(bank[4 * u][:, :]), ACT.Copy).then_inc(S("x0_copied"), 1)
                for lv in range(1, LEVELS):
                    for u in range(2):
                        act.wait_ge(S("ly_done"), lev(s, lv, u))
                        act.activation(sets[u]["Y"], heads4(bank[4 * u][:, :]), ACT.Copy).then_inc(S("ly_copied"), 1)
                    if s == 1 and lv == 4:
                        out_rms(0)
                if s == 0:
                    for u in range(2):
                        act.wait_ge(S("st_done"), u + 1)
                        for d in range(2):
                            act.activation(st_buf[u][d], heads4(bank[4 * u + 3 * d][:, :]), ACT.Copy)\
                               .then_inc(S("st_ready"), 1)
            out_rms(1)
            for s in range(2):
                for q in range(2):
                    act.wait_ge(S("dot_done"), 2 * s + q + 1)
                    act.activation(act_t[:, 4 * q:4 * q + 4, s * P:(s + 1) * P],
                                   bank[2 * s + q][:, :].rearrange("p (h n) -> p h n", h=4), ACT.Copy,
                                   scale=p_("onorm")).then_inc(S("dot_copied"), 1)
            act.wait_ge(S("dot_copied"), 4)
            act.sem_inc(S("dot_banks_free"), 1)

        def delta_pool(pool, ch):
            pool.memset(zpad, 0.0).then_inc(S("pad_zero"), 1)
            ada_pool(pool, ch, ADA_MOE0, ADA_ODD)
            def masked_forward(s, u):
                pool.tensor_tensor(sets[u]["LM"], mask4(c_(DIRS[0][0])), per_head(g_tok, s, 0, u), ALU.mult)\
                    .then_inc(S("gm_forward"), 1)

            pool.wait_ge(S("g_ready"), 1)
            for u in range(2):
                masked_forward(0, u)
            for s in range(2):
                for u in range(2):
                    pool.wait_ge(S("dt_ready"), 4 * s + 2 * u + 1)
                    pool.tensor_tensor(decay[s][:, u, 0], decay[s][:, u, 0], mask4(c_(DIRS[0][0])), ALU.mult)\
                        .then_inc(S("dtm_ready"), 1)
                for u in range(2):
                    w = sets[u]
                    pool.wait_ge(S("lt_masked"), 2 * s + u + 1)
                    pool.tensor_tensor(w["XT"], w["XT"], mask4(ident), ALU.add).then_inc(S("xt0_ready"), 1)
                for lv in range(1, LEVELS):
                    for u in range(2):
                        w = sets[u]
                        if lv >= 2:
                            pool.wait_ge(S("ly_done"), lev(s, lv - 1, u))
                        pool.tensor_tensor(w["LM"], w["LT"], level_mask("level", lv), ALU.mult).then_inc(S("lm_ready"), 1)
                    for u in range(2):
                        w = sets[u]
                        if lv == 1:
                            pool.wait_ge(S("xt0_ready"), 2 * s + u + 1)
                            pool.wait_ge(S("at_ready"), 2 * s + u + 1)
                        else:
                            pool.wait_ge(S("x_summed"), lev(s, lv - 1, u))
                        pool.tensor_tensor(decay[s][:, u, 1], w["XT"], level_mask("half", lv), ALU.mult)\
                            .then_inc(S("xtm_ready"), 1)
                for u in range(2):
                    pool.wait_ge(S("x_summed"), lev(s, LEVELS - 1, u))
                    pool.tensor_tensor(decay[s][:, u, 1], sets[u]["XT"], mask4(c_(DIRS[1][0])), ALU.mult)\
                        .then_inc(S("xt_backward"), 1)
                if s == 0:
                    pool.wait_ge(S("vn_done"), 2)
                    pool.dma_start(s0, state0).then_inc(S("s0_in"), 16)
                    for u in range(2):
                        w = sets[u]
                        pool.wait_ge(S("vn_ready"), u + 1)
                        ch.link(pool.tensor_tensor(w["LM"], w["X"], per_head(kdec, s, 0, u), ALU.mult))
                        pool.tensor_tensor(w["LT"], w["Y"], per_head(kdec, s, 1, u), ALU.mult).then_inc(S("kd_ready"), 1)
                    for u in range(2):
                        pool.wait_ge(S("st_done"), u + 1)
                        masked_forward(1, u)
                    for u in range(2):
                        for d in range(2):
                            pool.wait_ge(S("st_ready"), 2 * u + d + 1)
                            pool.dma_start(st_out[d, :, 4 * u:4 * u + 4, :], st_buf[u][d])\
                                .then_inc(S(f"state_out{2 * u + d}"), 16)
            for i in range(4):
                pool.wait_ge(S(f"state_out{i}"), 16)


        def delta_dve(dve, ch):
            ab = ab_raw.rearrange("p (s n) -> p s n", s=2)
            cw = p_("conv").rearrange("p (i j) -> p i j", j=3)

            def to_tok(i):
                dve.wait_ge(S("tok_done"), i + 1)
                dve.tensor_copy(dqkv[:, :, i * P:(i + 1) * P], bank[4 + i % 2][:, 0:T].rearrange("p (s n) -> p s n", s=2))\
                   .then_inc(S("tok_copied"), 1)

            def qk_norm(n):
                w, s, hq = n // 4, (n // 2) % 2, n % 2
                at = w * 1024 + 4 * hq * P
                h = s * 16 + w * 8 + 4 * hq
                qk = heads4(dqkv[:, s, at:at + 512])
                dve.tensor_tensor(qk, qk, bcast(qk_ss[:, h:h + 4], P), ALU.mult).then_inc(S("qk_ready"), 1)

            for i in range(24):
                dve.wait_ge(S("z_copied"), i + 1)
                if i >= 3:
                    dve.wait_ge(S("tok_done"), i - 2)
                z, y = zpad[:, i % 3], conv_o[:, i % 3]
                ch.link(dve.tensor_scalar(y, z[:, :, 0:128], cw[:, i, 0:1], None, ALU.mult))
                ch.link(dve.scalar_tensor_tensor(y, z[:, :, 1:129], cw[:, i, 1:2], y, ALU.mult, ALU.add))
                dve.scalar_tensor_tensor(y, z[:, :, 2:130], cw[:, i, 2:3], y, ALU.mult, ALU.add).then_inc(S("conv_sum"), 1)
                if i >= 3:
                    to_tok(i - 3)
                ada_dve(dve, ch, ADA_MOE0 + i // 4, range(2 * (i % 4), 2 * (i % 4) + 2))
                if i % 4 == 1 and i >= 9:
                    ada_store(dve, ADA_MOE0 + i // 4 - 2, bank[6])
                if i == 20:
                    dve.wait_ge(S("qk_squares"), 32)
                    dve.tensor_scalar(qk_ss, qk_ss, 1e-6, None, ALU.add).then_inc(S("qk_ss"), 1)
                if i == 22:
                    dve.wait_ge(S("qk_rs"), 1)
                    rv = qk_ss.rearrange("p (s w h) -> p s w h", s=2, w=2)
                    ch.link(dve.tensor_scalar(rv[:, :, 0, :], rv[:, :, 0, :], float(P) ** -0.5, None, ALU.mult))
                if i >= 22:
                    qk_norm(2 * (i - 22))
                    qk_norm(2 * (i - 22) + 1)
            for i in range(21, 24):
                to_tok(i)
            ada_store(dve, ADA_ODD - 2, bank[6])
            dve.wait_ge(S("ab_done"), 1)
            dve.tensor_copy(ab, bank[3][:, 0:64].rearrange("p (s n) -> p s n", s=2)).then_inc(S("ab_copied"), 1)
            dve.wait_ge(S("ab_copied"), 1)
            xv = sp_x.rearrange("p (s n) -> p s n", s=2)
            ch.link(dve.tensor_tensor(xv, ab[:, :, 0:16], p_("dt_bias").unsqueeze(1).to_broadcast([P, 2, 16]), ALU.add))
            ch.link(dve.tensor_scalar(sp_a, sp_x, -1.0, None, ALU.mult))
            dve.tensor_tensor(sp_b, sp_a, sp_x, ALU.max).then_inc(S("sp_abs"), 1)
            dve.wait_ge(S("sp_ln"), 1)
            ch.link(dve.scalar_tensor_tensor(sp_a, sp_x, 0.0, sp_b, ALU.max, ALU.add))
            dve.wait_ge(S("a_exp"), 1)
            dve.wait_ge(S("beta_exp"), 1)
            ch.link(dve.tensor_scalar(sp_a, sp_a, -1.0, None, ALU.mult))
            dve.tensor_tensor(g_tok.rearrange("p (s n) -> p s n", s=2), sp_a.rearrange("p (s n) -> p s n", s=2),
                              negA.unsqueeze(1).to_broadcast([P, 2, 16]), ALU.mult).then_inc(S("g_ready"), 1)
            ch.link(dve.tensor_scalar(beta, beta, 1.0, None, ALU.add))
            ch.link(dve.reciprocal(beta, beta))
            ch.link(dve.tensor_scalar(nbeta, beta, -1.0, None, ALU.mult))
            for n in range(4, 8):
                qk_norm(n)
            ada_store(dve, ADA_ODD - 1, bank[6])

            def ps(i):
                return heads4(bank[i][:, :])

            def gated_norm(s, step):
                ss, oo = o_ss[:, s * 8:s * 8 + 8], o_d[:, s, :].rearrange("p (h n) -> p h n", h=8)
                if step == 0:
                    ch.link(dve.tensor_tensor(o_square, o_d[:, s, :], o_d[:, s, :], ALU.mult))
                elif step == 1:
                    ch.link(dve.tensor_reduce(ss, o_square.rearrange("p (h n) -> p h n", h=8), AX, ALU.add))
                    dve.tensor_scalar(ss, ss, 1.0 / P, EPS, ALU.mult, ALU.add).then_inc(S("o_ss"), 1)
                elif step == 2:
                    ch.link(dve.tensor_tensor(o_d[:, s, :], o_d[:, s, :], dgate[:, s, :], ALU.mult))
                else:
                    dve.wait_ge(S("o_rs"), s + 1)
                    dve.tensor_tensor(oo, oo, bcast(ss, P), ALU.mult).then_inc(S("do_ready"), 1)

            def masked_backward(s, u):
                dve.tensor_tensor(sets[u]["Y"], mask4(c_(DIRS[1][0])), per_head(g_tok, s, 1, u), ALU.mult)\
                    .then_inc(S("gm_backward"), 1)

            for s in range(2):
                for u in range(2):
                    if s == 0:
                        masked_backward(s, u)
                for u in range(2):
                    i = 2 * s + u
                    w = sets[u]
                    if s == 1:
                        dve.wait_ge(S(f"state_out{2 + u}"), 16)
                    dve.wait_ge(S("kk_done"), i + 1)
                    dve.wait_ge(S("dt_ready"), 2 * i + 2)
                    ch.link(dve.tensor_tensor(decay[s][:, u, 1], decay[s][:, u, 1], mask4(c_(DIRS[1][0])), ALU.mult))
                    dve.wait_ge(S("dtm_ready"), i + 1)
                    ch.post(dve.tensor_tensor(w["X"], decay[s][:, u, 0], per_head(nbeta, s, 0, u), ALU.mult))
                    ch.link(dve.tensor_tensor(w["XT"], decay[s][:, u, 1], per_head(nbeta, s, 1, u), ALU.mult))
                    ch.link(dve.tensor_tensor(w["X"], w["X"], w["XT"], ALU.add))
                    ch.link(dve.tensor_tensor(w["LT"], w["X"], ps(4 * u + 2), ALU.mult))
                    dve.tensor_tensor(w["XT"], w["LT"], level_mask("level", 0), ALU.mult).then_inc(S("lt_masked"), 1)
                for u in range(2):
                    w = sets[u]
                    ch.link(dve.tensor_tensor(w["AT"][:, 0], decay[s][:, u, 0], ps(4 * u + 3), ALU.mult))
                    dve.tensor_tensor(w["AT"][:, 1], decay[s][:, u, 1], ps(4 * u + 3), ALU.mult).then_inc(S("at_ready"), 1)
                for u in range(2):
                    dve.wait_ge(S("x0_copied"), 2 * s + u + 1)
                    dve.tensor_tensor(decay[s][:, u, 0], sets[u]["X"], level_mask("half", 1), ALU.mult)\
                        .then_inc(S("xm_ready"), 1)
                for lv in range(1, LEVELS):
                    for u in range(2):
                        w = sets[u]
                        dve.wait_ge(S("dx_done"), lev(s, lv, u))
                        if lv < LEVELS - 1:
                            ch.link(dve.tensor_tensor(w["X"], w["X"], ps(4 * u + 2), ALU.add))
                            dve.tensor_tensor(decay[s][:, u, 0], w["X"], level_mask("half", lv + 1), ALU.mult)\
                                .then_inc(S("xm_ready"), 1)
                        dve.tensor_tensor(w["XT"], w["XT"], ps(4 * u + 1), ALU.add).then_inc(S("x_summed"), 1)
                    if s == 1 and 2 <= lv <= 5:
                        if lv == 2:
                            for d in range(2):
                                dve.wait_ge(S(f"state_out{d}"), 16)
                        gated_norm(0, lv - 2)
                for u in range(2):
                    dve.wait_ge(S("x_summed"), lev(s, LEVELS - 1, u))
                    dve.tensor_tensor(decay[s][:, u, 0], sets[u]["XT"], mask4(c_(DIRS[0][0])), ALU.mult)\
                        .then_inc(S("xt_forward"), 1)
                if s == 1:
                    for u in range(2):
                        w = sets[u]
                        v = heads4(dqkv[:, s, 2048 + 512 * u:2048 + 512 * u + 512])
                        dve.wait_ge(S("ks_done"), 2 * u + 1)
                        ch.post(dve.tensor_tensor(w["LM"], ps(4 * u), per_head(egc, s, 0, u), ALU.mult))
                        ch.link(dve.tensor_tensor(w["LT"], ps(4 * u + 1), per_head(egc, s, 1, u), ALU.mult))
                        ch.link(dve.tensor_tensor(w["LM"], v, w["LM"], ALU.subtract))
                        dve.tensor_tensor(w["LT"], v, w["LT"], ALU.subtract).then_inc(S("rhs_ready"), 1)
                    for u in range(2):
                        w = sets[u]
                        oo = heads4(o_d[:, s, 512 * u:512 * u + 512])
                        dve.wait_ge(S("ks_done"), 2 * u + 2)
                        ch.post(dve.tensor_tensor(oo, ps(4 * u + 2), per_head(egc, s, 0, u), ALU.mult))
                        ch.link(dve.tensor_tensor(w["Y"], ps(4 * u + 3), per_head(egc, s, 1, u), ALU.mult))
                        ch.link(dve.tensor_tensor(oo, oo, w["Y"], ALU.add))
                for u in range(2):
                    w = sets[u]
                    dve.wait_ge(S("vn_done"), 2 * s + u + 1)
                    ch.link(dve.tensor_tensor(w["X"], ps(4 * u), per_head(beta, s, 0, u), ALU.mult))
                    dve.tensor_tensor(w["Y"], ps(4 * u + 1), per_head(beta, s, 1, u), ALU.mult).then_inc(S("vn_ready"), 1)
                for u in range(2):
                    oo = heads4(o_d[:, s, 512 * u:512 * u + 512])
                    dve.wait_ge(S("o_done"), 2 * s + u + 1)
                    if s == 0:
                        ch.link(dve.tensor_copy(oo, ps(4 * u + 2)))
                        dve.wait_ge(S("kd_ready"), u + 1)
                        masked_backward(1, u)
                    else:
                        ch.link(dve.tensor_tensor(oo, oo, ps(4 * u + 2), ALU.add))
            dve.wait_ge(S("ada_stored"), ADA_ODD)
            fold_norm(dve, ch, 2, 1, 3)
            for step in range(4):
                gated_norm(1, step)
            out_dve(dve, ch, 1, OOUT0)

        PAIRS = [(kind, s, c) for kind in range(2) for s in range(2) for c in range(4)]

        @block.tensor
        def _(pe):
            pe.wait_ge(S("params_in"), 16)
            pe.wait_ge(S("ones_set"), 1)
            pe.wait_ge(S("ident_in"), 16)
            pe.wait_ge(S("cond_ready"), 1)
            ada_rows(pe, 0, bank[7])
            ada_sum(pe, 0, bank[6])
            ada_columns(pe, 0, bank[7])
            ada_rows(pe, 1, bank[5])
            ada_sum(pe, 2, bank[6])
            ada_columns(pe, 1, bank[5])
            meet(pe, "pe")
            for n in range(12):
                q, s = n // 2, n % 2
                k = wait_slot(pe, EIN0, 2 * q)
                w = ring[:, k, :].rearrange("p (c n) -> p c n", c=KC)
                if n >= 4:
                    pe.wait_ge(S("proj_copied"), n - 3)
                for c in range(KC):
                    last = pe.matmul(bank[n % 4][:, :], act_t[:, c, s * P:(s + 1) * P], w[:, c, :],
                                     start=(c == 0), stop=(c == KC - 1))
                last.then_inc(S("proj_done"), 1)
                if s == 1 and q >= 1:
                    ada_sum(pe, ADA_FIRST + q - 1, bank[6])
            ada_sum(pe, ADA_PROJ - 1, bank[6])
            pe.wait_ge(S("consts_in"), 16)
            pe.wait_ge(S("proj_copied"), 12)
            for n in range(8):
                wi, s = n // 2, n % 2
                col = (0, 512, 1536, 2048)[wi]
                if n >= 2:
                    pe.wait_ge(S("ht_copied"), n - 1)
                for j in range(4):
                    last = pe.transpose(bank[4 + n % 2][:, j * P:(j + 1) * P], qkv[:, s, col + j * P:col + (j + 1) * P], ident)
                last.then_inc(S("ht_done"), 1)
            pe.wait_ge(S("ht_copied"), 8)
            pe.wait_ge(S("even_in"), 112)
            pe.wait_ge(S("bias_ready"), 1)
            pe.wait_ge(S("ada_stored"), ADA_PROJ)

            def sc(p):
                kind, s, c = PAIRS[p]
                if p >= 2:
                    pe.wait_ge(S("exp_done"), 2 * (p - 1))
                for j in range(2):
                    bk = bank[p % 2 + 6 * j]
                    r = slice(64 * j, 64 * j + 64)
                    q = heads_t[r, 2 * kind, s, c, :]
                    biased_ = kind == 0 and s == 1
                    last = pe.matmul(bk[:, 0:P], q, heads_t[r, 2 * kind + 1, s, c, :], start=True, stop=not biased_)
                    if biased_:
                        last = pe.matmul(bk[:, 0:P], ident, bias[:, 2 * c + j, :], start=False, stop=True)
                    if s == 1:
                        cache = nkc if kind == 0 else dkc
                        last = pe.matmul(bk[:, P:2 * P], q, cache[r, c, :], start=True, stop=True)
                last.then_inc(S("score_done"), 1)

            def pt(p):
                kind, s, c = PAIRS[p]
                pe.wait_ge(S("p_ready"), p + 1)
                if p >= 2:
                    pe.wait_ge(S("pt_copied"), p - 1)
                nk2 = 1 if s == 0 else 2
                for j in range(2 if kind == 0 else 1):
                    for t in range(nk2):
                        i = j * nk2 + t
                        last = pe.transpose(bank[2 + p % 2][:, i * P:(i + 1) * P], probs[:, p % 2, j, t * P:(t + 1) * P], ident)
                last.then_inc(S("pt_done"), 1)

            def pv(p):
                kind, s, c = PAIRS[p]
                g = p // 4
                pe.wait_ge(S("pt_copied"), p + 1)
                if p % 4 == 0 and g >= 1:
                    pe.wait_ge(S("o_copied"), g)
                nk2 = 1 if s == 0 else 2
                pflat = probs_t[:, p % 2].rearrange("p j n -> p (j n)")
                for j in range(2 if kind == 0 else 1):
                    if kind == 0:
                        h = 2 * c + j
                        vs = [qkv[:, s, 1024 + h * 64:1024 + h * 64 + 64], nvc[:, h * 64:h * 64 + 64]]
                        out = bank[4][:, h * 64:h * 64 + 64]
                    else:
                        vs = [qkv[:, s, 2560 + c * P:2560 + (c + 1) * P], dvc[:, c * P:(c + 1) * P]]
                        out = bank[4][:, c * P:(c + 1) * P]
                    for t in range(nk2):
                        i = j * nk2 + t
                        last = pe.matmul(out, pflat[:, i * P:(i + 1) * P], vs[t], start=(t == 0), stop=(t == nk2 - 1))
                last.then_inc(S("pv_done"), 1)

            for p in range(19):
                if p < 16:
                    sc(p)
                if 2 <= p < 18:
                    pt(p - 2)
                if p >= 3:
                    pv(p - 3)
                if p == 0:
                    ada_rows(pe, 2, bank[5])
                if p == 1:
                    ada_columns(pe, 2, bank[5])
                if p in (6, 14):
                    ada_sum(pe, 11 if p == 6 else 12, bank[5])
            for g in range(4):
                kind, s = g // 2, g % 2
                pe.wait_ge(S("o_copied"), 4)
                if kind == 1:
                    pe.wait_ge(S("o_normed"), 1)
                for j in range(4):
                    last = pe.transpose(bank[g][:, j * P:(j + 1) * P], o_tok[:, s, kind * 512 + j * P:kind * 512 + (j + 1) * P], ident)
                last.then_inc(S("ot_done"), 1)
            pe.wait_ge(S("ot_copied"), 4)
            out_pe(pe, 0, EOUT0)
            ln_pe(pe, 0)
            meet(pe, "pe")
            moe_pe(pe, 0, MOE0)
            ln_pe(pe, 1)
            meet(pe, "pe")
            delta_pe(pe)
            ln_pe(pe, 2)
            meet(pe, "pe")
            moe_pe(pe, 1, MOE1)
            ln_pe(pe, 3)
            meet(pe, "pe")
            for s in range(2):
                for q in range(2):
                    pe.wait_ge(S("res_scaled"), 3 * KC + 4 * q + 4)
                    for j in range(4):
                        last = pe.transpose(bank[2 * s + q + 2][:, j * P:(j + 1) * P], res[:, 4 * q + j, s * P:(s + 1) * P], ident)
                    last.then_inc(S("yt_done"), 1)

        @block.scalar
        def _(act):
            ch = Chain(act, "act_step")
            act.wait_ge(S("params_in"), 16)
            act.activation(cond_t, p_("cond"), ACT.Silu).then_inc(S("cond_ready"), 1)
            ada_copy(act, 0, bank[7])
            act.wait_ge(S("x_in"), 16)
            act.activation(res[:, :, :], act_t[:, :, :], ACT.Copy, scale=ALPHA).then_inc(S("alpha_x"), 1)
            ada_copy(act, 1, bank[5])
            act.wait_ge(S("alpha_x"), 1)
            act.wait_ge(S("first_mod"), 1)
            for c in range(4, KC):
                for s in range(2):
                    a = act_t[:, c, s * P:(s + 1) * P]
                    act.activation(a, a, ACT.Identity, scale=mod_v[:, 0, 1, c, s:s + 1], bias=mod_v[:, 0, 0, c, s:s + 1])
            meet(act, "act")
            act.wait_ge(S("lam_dots"), 1)
            act.activation(lam_w[:, 0:2], lam_w[:, 0:2], ACT.Exp).then_inc(S("lam_exp"), 1)
            for n in range(12):
                q, s = n // 2, n % 2
                if q in (3, 4) and s == 1:
                    continue
                act.wait_ge(S("proj_done"), n + 1)
                dst = qkv[:, s, q * 512:(q + 1) * 512]
                act.activation(dst, bank[n % 4][:, :], ACT.Copy, scale=(0.125 if q in (0, 3) else 1.0))\
                   .then_inc(S("proj_act"), 1)
                act.wait_ge(S("proj_act"), 1 + len([m for m in range(n) if not (m // 2 in (3, 4) and m % 2 == 1)]))
                act.wait_ge(S("proj_copied"), n) if n else None
                act.sem_inc(S("proj_copied"), 1)
                if s == 1:
                    act.sem_inc(slot_free[at_ring(EIN0, 2 * q)[0]], 1)
                if s == 0 and q in (1, 2, 4, 5):
                    act.sem_inc(S("kv_out_ready"), 1)
            for n in range(8):
                wi, s = n // 2, n % 2
                act.wait_ge(S("ht_done"), n + 1)
                act.activation(heads_t[:, wi, s], bank[4 + n % 2][:, :].rearrange("p (c n) -> p c n", c=4), ACT.Copy)\
                   .then_inc(S("ht_copied"), 1)
            def ptc(p):
                kind, s, c = PAIRS[p]
                n = (1 if s == 0 else 2) * (2 if kind == 0 else 1) * P
                act.wait_ge(S("pt_done"), p + 1)
                if p >= 2:
                    act.wait_ge(S("pv_done"), p - 1)
                act.activation(probs_t[:, p % 2].rearrange("p j n -> p (j n)")[:, 0:n], bank[2 + p % 2][:, 0:n], ACT.Copy)\
                   .then_inc(S("pt_copied"), 1)

            def oc(g):
                kind, s = g // 2, g % 2
                act.wait_ge(S("pv_done"), 4 * g + 4)
                act.activation(o_tok[:, s, kind * 512:(kind + 1) * 512], bank[4][:, :], ACT.Copy)\
                   .then_inc(S("o_copied"), 1)

            for p in range(19):
                if p < 16:
                    kind, s, c = PAIRS[p]
                    nk = 128 if s == 0 else 256
                    if p >= 2:
                        act.wait_ge(S("pt_done"), p - 1)
                    for j in range(2):
                        act.wait_ge(S("max_done"), 2 * p + j + 1)
                        act.activation(probs[:, p % 2, j, 0:nk], bank[p % 2 + 6 * j][:, 0:nk], ACT.Exp,
                                       bias=mx[:, 2 * p + j:2 * p + j + 1],
                                       accum_out=sums[:, 2 * p + j:2 * p + j + 1]).then_inc(S("exp_done"), 1)
                if 2 <= p < 18:
                    ptc(p - 2)
                if p == 0:
                    ada_copy(act, 2, bank[5])
                if p >= 3 and (p - 3) % 4 == 3:
                    oc((p - 3) // 4)
            act.wait_ge(S("o_ms"), 1)
            ch.link(act.activation(rms[:, 0:8], rms[:, 0:8], ACT.Ln))
            act.activation(rms[:, 0:8], rms[:, 0:8], ACT.Exp, scale=-0.5).then_inc(S("o_rms"), 1)
            for g in range(2):
                act.wait_ge(S("ot_done"), g + 1)
                act.activation(act_t[:, 0:4, g * P:(g + 1) * P], bank[g][:, :].rearrange("p (c n) -> p c n", c=4), ACT.Copy)\
                   .then_inc(S("ot_copied"), 1)
            for g in range(2):
                act.wait_ge(S("ot_done"), g + 3)
                act.activation(act_t[:, 4:8, g * P:(g + 1) * P], bank[2 + g][:, :].rearrange("p (c n) -> p c n", c=4),
                               ACT.Copy, scale=sub_g).then_inc(S("ot_copied"), 1)
            ln_act(act, ch, 0)
            meet(act, "act")
            moe_act(act, ch, 0, MOE0)
            ln_act(act, ch, 1)
            meet(act, "act")
            delta_act(act, ch)
            ln_act(act, ch, 2)
            meet(act, "act")
            moe_act(act, ch, 1, MOE1)
            ln_act(act, ch, 3)
            meet(act, "act")
            for g in range(4):
                s, q = g // 2, g % 2
                act.wait_ge(S("yt_done"), g + 1)
                act.activation(y_tok[:, s, q * 512:(q + 1) * 512], bank[g + 2][:, :], ACT.Copy).then_inc(S("y_ready"), 1)

        @block.vector
        def _(dve):
            ch = Chain(dve, "dve_step")
            dve.wait_ge(S("params_in"), 16)
            dve.memset(ones[:, :], 1.0).then_inc(S("ones_set"), 1)
            for i, name in enumerate(("ln_g", "ln_b")):
                ch.link(dve.tensor_scalar(ln_scaled[:, 64 * i:64 * i + 48], p_(name)[:, 0:48], ALPHA, None, ALU.mult))
                ch.link(dve.tensor_copy(ln_scaled[:, 64 * i + 48:64 * i + 64], p_(name)[:, 48:64]))
            ch.link(dve.tensor_scalar(sub_g, p_("subln"), 1.0 - (0.8 - 0.6 * math.exp(0.0)), None, ALU.mult))
            dve.wait_ge(S("cond_ready"), 1)
            ada_dve(dve, ch, 0)
            ada_dve(dve, ch, 2)
            for q, bk in enumerate((6, 7, 6, 5)):
                ada_store(dve, q, bank[bk])
            dve.wait_ge(S("ada_stored"), ADA_FIRST)
            ch.link(dve.tensor_scalar(mod_v[:, 0, 1], mod_v[:, 0, 1], 1.0, None, ALU.add))
            dve.wait_ge(S("x_in"), 16)
            dve.wait_ge(S("alpha_x"), 1)
            dve.sem_inc(S("first_mod"), 1)
            av = act_t[:, 0:4, :].rearrange("p c (s n) -> p (c s) n", s=2)
            ch.link(dve.tensor_tensor(av, av, bcast(mod_v[:, 0, 1, 0:4].rearrange("p c s -> p (c s)"), P), ALU.mult))
            ch.link(dve.tensor_tensor(av, av, bcast(mod_v[:, 0, 0, 0:4].rearrange("p c s -> p (c s)"), P), ALU.add))
            meet(dve, "dve")
            dve.wait_ge(S("even_in"), 112)
            lamp = lam_p.rearrange("p (a b n) -> p a b n", a=2, b=2)
            ch.link(dve.tensor_tensor(rope_1[:, 0:128].rearrange("p (a n) -> p a n", a=2), lamp[:, :, 0], lamp[:, :, 1], ALU.mult))
            dve.tensor_reduce(lam_w[:, 0:2], rope_1[:, 0:128].rearrange("p (a n) -> p a n", a=2), AX, ALU.add).then_inc(S("lam_dots"), 1)
            for q in range(6):
                ada_dve(dve, ch, ADA_FIRST + q)
                if q >= 1:
                    ada_store(dve, ADA_FIRST + q - 1, bank[6])
                if q not in (3, 4):
                    continue
                n = 2 * q + 1
                dve.wait_ge(S("proj_done"), n + 1)
                src = bank[n % 4][:, :].rearrange("p (h a b n) -> p h a b n", h=8, a=2, b=2)
                t1 = rope_1.rearrange("p (h n) -> p h n", h=8)
                t2 = rope_2.rearrange("p (h a b n) -> p h a b n", h=8, a=2, b=2)
                sn = ec_("rope_s").rearrange("p (a b n) -> p a b n", a=2, b=2)
                ch.link(dve.tensor_tensor(t1, bank[n % 4][:, :].rearrange("p (h n) -> p h n", h=8),
                                          ec_("rope_c").unsqueeze(1).to_broadcast([P, 8, 64]), ALU.mult))
                for b in range(2):
                    for a in range(2):
                        ch.link(dve.tensor_tensor(t2[:, :, a, b, :], src[:, :, a, 1 - b, :],
                                                  sn[:, a, b, :].unsqueeze(1).to_broadcast([P, 8, 16]), ALU.mult))
                dst = qkv[:, 1, q * 512:(q + 1) * 512]
                ch.link(dve.tensor_tensor(dst, rope_1, rope_2, ALU.add))
                if q == 3:
                    ch.link(dve.tensor_scalar(dst, dst, 0.125, None, ALU.mult))
                dve.wait_ge(S("proj_copied"), n)
                dve.sem_inc(S("proj_copied"), 1)
                dve.sem_inc(slot_free[at_ring(EIN0, 2 * q)[0]], 1)
            ada_store(dve, ADA_PROJ - 1, bank[6])
            dve.wait_ge(S("lam_exp"), 1)
            ch.link(dve.tensor_tensor(lam_w[:, 2:3], lam_w[:, 1:2], lam_w[:, 0:1], ALU.subtract))
            ch.link(dve.tensor_scalar(lam_w[:, 3:4], lam_w[:, 2:3], -(0.8 - 0.6 * math.exp(0.0)), None, ALU.add))

            def mxp(p):
                kind, s, c = PAIRS[p]
                nk = 128 if s == 0 else 256
                dve.wait_ge(S("score_done"), p + 1)
                for j in range(2):
                    dve.tensor_reduce(mx[:, 2 * p + j:2 * p + j + 1], bank[p % 2 + 6 * j][:, 0:nk],
                                      AX, ALU.max, negate=True).then_inc(S("max_done"), 1)

            for p in range(17):
                if p < 16:
                    mxp(p)
                if p % 6 < 4 and p < 10:
                    ada_dve(dve, ch, 11 if p < 6 else 12, range(2 * (p % 6), 2 * (p % 6) + 2))
                if p in (2, 7, 15):
                    ada_store(dve, ADA_PROJ + (2, 7, 15).index(p), bank[5])
                if p < 1:
                    continue
                q = p - 1
                kind, s, c = PAIRS[q]
                nk = 128 if s == 0 else 256
                dve.wait_ge(S("exp_done"), 2 * (q + 1))
                rs = rsum[:, 2 * q:2 * q + 2]
                ch.link(dve.reciprocal(rs, sums[:, 2 * q:2 * q + 2]))
                pb = probs[:, q % 2]
                if kind == 0:
                    dve.tensor_tensor(pb[:, :, 0:nk], pb[:, :, 0:nk], bcast(rs, nk), ALU.mult).then_inc(S("p_ready"), 1)
                else:
                    ch.link(dve.tensor_tensor(nlr[:, 0:1], rs[:, 1:2], lam_w[:, 3:4], ALU.mult))
                    ch.link(dve.tensor_scalar(pb[:, 0, 0:nk], pb[:, 0, 0:nk], rs[:, 0:1], None, ALU.mult))
                    dve.scalar_tensor_tensor(pb[:, 0, 0:nk], pb[:, 1, 0:nk], nlr[:, 0:1], pb[:, 0, 0:nk],
                                             ALU.mult, ALU.add).then_inc(S("p_ready"), 1)
            dve.wait_ge(S("o_copied"), 4)
            ov = o_tok[:, :, 512:1024]
            dve.wait_ge(S("pv_done"), 16)
            dve.wait_ge(S("out_done"), 64)
            ch.link(dve.tensor_tensor(o_sq.rearrange("p (s n) -> p s n", s=2), ov, ov, ALU.mult))
            ch.link(dve.tensor_reduce(rms[:, 0:8], o_sq.rearrange("p (h n) -> p h n", h=8), AX, ALU.add))
            dve.tensor_scalar(rms[:, 0:8], rms[:, 0:8], 1.0 / P, EPS, ALU.mult, ALU.add).then_inc(S("o_ms"), 1)
            dve.wait_ge(S("o_rms"), 1)
            for s in range(2):
                oh = o_tok[:, s, 512:1024].rearrange("p (h n) -> p h n", h=4)
                ch.link(dve.tensor_tensor(oh, oh, bcast(rms[:, 4 * s:4 * s + 4], P), ALU.mult))
            dve.sem_inc(S("o_normed"), 1)
            dve.wait_ge(S("ada_stored"), ADA_EVEN)
            fold_norm(dve, ch, 0, 0, 3)
            out_dve(dve, ch, 0, EOUT0)
            ln_dve(dve, ch, 0)
            meet(dve, "dve")
            moe_dve(dve, ch, 0, MOE0)
            ln_dve(dve, ch, 1)
            meet(dve, "dve")
            delta_dve(dve, ch)
            ln_dve(dve, ch, 2)
            meet(dve, "dve")
            moe_dve(dve, ch, 1, MOE1)
            ln_dve(dve, ch, 3)
            meet(dve, "dve")

        @block.sync
        def _(sp):
            sp.dma_start(par[:, :], params).then_inc(S("params_in"), 16)
            sp.dma_start(ident, consts[:, 0:P]).then_inc(S("ident_in"), 16)
            for k in range(RING):
                sp.dma_start(ring[:, k, :], slots[k]).then_inc(slot_full[k], 16)
                if k == ADA_FIRST - 1:
                    sp.dma_start(cst[:, P:N_CONST], consts[:, P:N_CONST]).then_inc(S("consts_in"), 16)
            with sp.Fori(0, N_SLOTS // RING - 1) as turn:
                for k in range(RING):
                    sp.wait_ge(slot_free[k], turn + 1)
                    sp.dma_start(ring[:, k, :], slots[bass.ds(turn * RING + (RING + k), 1)].rearrange("a p n -> (a p) n")).then_inc(slot_full[k], 16)

        @block.gpsimd
        def _(pool):
            ch = Chain(pool, "pool_step")
            pool.dma_start(act_t[:, :, :], x_t).then_inc(S("x_in"), 16)
            pool.wait_ge(slot_full[0], 16)
            for dst, src in ((nkc, nat_kc), (nvc, nat_vc), (dkc, diff_kc), (dvc, diff_vc), (bias, nat_bias), (lam_p, lam_in), (even_c, even_consts)):
                pool.dma_start(dst, src).then_inc(S("even_in"), 16)
            pool.wait_ge(S("cond_ready"), 1)
            meet(pool, "pool")
            pool.wait_ge(S("even_in"), 112)
            pool.wait_ge(S("consts_in"), 16)
            pool.tensor_tensor(bias, bias, ec_("window").unsqueeze(1).to_broadcast([P, 8, P]), ALU.add).then_inc(S("bias_ready"), 1)
            ada_pool(pool, ch, ADA_FIRST, ADA_PROJ)
            pool.wait_ge(S("kv_out_ready"), 4)
            for w, out in ((1, nk_out), (2, nv_out), (4, dk_out), (5, dv_out)):
                pool.dma_start(out, qkv[:, 0, w * 512:(w + 1) * 512]).then_inc(S("out_done"), 16)
            ada_pool(pool, ch, ADA_PROJ, ADA_EVEN)
            pool.wait_ge(S("out_done"), 64)
            ln_pool(pool, 0)
            ln_pool(pool, 1)
            delta_pool(pool, ch)
            ln_pool(pool, 2)
            ln_pool(pool, 3)
            pool.wait_ge(S("y_ready"), 4)
            for s in range(2):
                pool.dma_start(y_out[s], y_tok[:, s, :]).then_inc(S("out_done"), 16)
            pool.wait_ge(S("out_done"), 64 + 32)


def shape_constants():
    import numpy as np
    f = np.float32
    i = np.arange(P)
    r, c = i[:, None], i[None, :]
    out = {"ident": r == c, "mean": np.full((P, P), 1.0 / D), "le": r <= c, "gt": r > c, "ge": r >= c, "lt": r < c}
    out["level"] = np.concatenate([((r >> (k + 1)) == (c >> (k + 1))) & ((r >> k) % 2 != (c >> k) % 2)
                                   for k in range(LEVELS)], 1)
    out["half"] = np.concatenate([np.where((r >> k) % 2 == 0, r >= c, r <= c) for k in range(LEVELS)], 1)
    inv = (f(10000.0) ** (-np.arange(16, dtype=f) / f(16))).astype(f)
    ar = (i // 64).astype(f)[:, None] * inv
    ac = (i % 64).astype(f)[:, None] * inv
    out["rope_c"] = np.concatenate([np.cos(ar), np.cos(ar), np.cos(ac), np.cos(ac)], 1)
    out["rope_s"] = np.concatenate([-np.sin(ar), np.sin(ar), -np.sin(ac), np.sin(ac)], 1)
    start = np.clip(i % 64 - 8, 0, 48)[:, None]
    ok = ((c % 64) >= start) & ((c % 64) < start + 16)
    out["window"] = np.where(ok, 0.0, -BIG)
    out["iota"] = np.broadcast_to(i.astype(f), (P, P))
    out["tile4"] = np.broadcast_to(128.0 * np.arange(4), (P, 4))
    out["rank4"] = np.broadcast_to(4.0 - np.arange(4), (P, 4))
    out["rank16"] = np.broadcast_to(16.0 - np.arange(16), (P, 16))
    return [np.ascontiguousarray(np.concatenate([np.asarray(out[n], f) for n in names], 1)) for names in (CONST_W, EVEN_W)]


def kernel(**inputs):
    import numpy as np
    import concourse.bacc as bacc
    from concourse.bass_utils import run_bass_kernel_spmd as run

    a = {k: np.asarray(v) for k, v in inputs.items()}

    def rows(w, n):
        k, m = w.shape
        return w.reshape(k // P, P, m // n, n).transpose(2, 1, 0, 3).reshape(m // n, P, (k // P) * n)

    def feat(v):
        v = v.reshape(v.shape[:-1] + (-1, P))
        return np.moveaxis(v, -1, 0)

    def moe_slots(l):
        g = np.stack([np.stack([rows(a["moe_wg"][l, e], FF)[0], rows(a["moe_wu"][l, e], FF)[0],
                                rows(a["moe_wd"][l, e], D)[0]]) for e in range(N_EXP)])
        return g.reshape(3 * N_EXP, P, SLOT)

    w_odd = a["w_in_odd"][0]
    ada = np.concatenate([rows(a["ada_w"][l], 512) for l in range(DEPTH)], 0)
    order = {}
    for at, block in ((MOE0, moe_slots(0)), (MOE1, moe_slots(1)), (EOUT0, rows(a["w_out_even"][0], 512)),
                      (OOUT0, rows(a["w_out_odd"][0], 512))):
        order.update({at + i: w for i, w in enumerate(block)})
    for at, block in ((EIN0, rows(a["w_in_even"][0], 512)),
                      (OIN0, rows(np.concatenate([w_odd[:, :3072], w_odd[:, 3104:]], 1), 512))):
        order.update({at + i + min(i, 6): w for i, w in enumerate(block)})
    order.update(dict(zip(ADA_SLOTS, ada)))
    slots = np.stack([order[i] for i in range(N_SLOTS)])
    x = np.stack([a["x_prompt"][0], a["x_sample"][0]])
    x_t = np.ascontiguousarray(x.reshape(2, P, KC, P).transpose(3, 2, 0, 1).reshape(P, KC, T))

    def rep(v):
        return np.broadcast_to(v.reshape(1, -1), (P, v.size))

    par = {
        "cond": feat(np.stack([a["c_ctx"], a["c"][0]])).transpose(0, 2, 1).reshape(P, -1),
        "ada_b": np.repeat(feat(a["ada_b"]).reshape(P, 96), 2, axis=1),
        "ln_g": np.repeat(feat(a["ln_g"]).reshape(P, 32), 2, axis=1),
        "ln_b": np.repeat(feat(a["ln_b"]).reshape(P, 32), 2, axis=1),
        "router": rows(a["router_w"], 16)[0],
        "router_b": rep(a["router_b"]),
        "subln": a["diff_subln"][0].reshape(P, 1),
        "onorm": a["onorm_odd"][0].reshape(P, 1),
        "conv": a["conv_odd"][0].reshape(3, 24, P).transpose(2, 1, 0).reshape(P, 72),
        "a_log": rep(a["a_log_odd"][0]),
        "dt_bias": rep(a["dt_bias_odd"][0]),
        "w_ab": rows(np.ascontiguousarray(w_odd[:, 3072:3104]), 32)[0],
    }
    params = np.ascontiguousarray(np.concatenate([par[n] for n in PARAM_W], 1))
    i = np.arange(P)
    dr = i[None, :] // 64 - i[:, None] // 64 + 7
    dc = np.clip(i[None, :] % 64 - i[:, None] % 64, -15, 15) + 15
    nat_bias = np.ascontiguousarray(a["nat_bias"][0][:, dr, dc].transpose(1, 0, 2))
    consts, even_consts = shape_constants()
    arrays = {
        "slots": slots, "x_t": x_t, "consts": consts, "even_consts": even_consts, "params": params,
        "nat_kc": np.ascontiguousarray(a["cache_nat_k"][0, 0].reshape(P, 4, P).transpose(2, 1, 0)),
        "nat_vc": np.ascontiguousarray(a["cache_nat_v"][0, 0].reshape(P, 512)),
        "diff_kc": np.ascontiguousarray(a["cache_diff_k"][0, 0].reshape(P, 4, P).transpose(2, 1, 0)),
        "diff_vc": np.ascontiguousarray(a["cache_diff_v"][0, 0].reshape(P, 512)),
        "nat_bias": nat_bias, "lam": np.ascontiguousarray(rep(a["diff_lam"][0])),
        "state0": np.ascontiguousarray(a["state_delta"][0, 0].transpose(2, 0, 1, 3)),
    }
    nc = bacc.Bacc("TRN2", target_bir_lowering=False, num_devices=1)
    args = [nc.dram_tensor(n, v.shape, F32, kind="ExternalInput").ap() for n, v in arrays.items()]
    outs = {"y": (2, P, D), "nk": (P, 512), "nv": (P, 512), "dk": (P, 512), "dv": (P, 512), "st": (2, P, HEADS, P)}
    args += [nc.dram_tensor("out_" + n, s, F32, kind="ExternalOutput").ap() for n, s in outs.items()]
    build_program(nc, *args)
    r = run(nc, [arrays], core_ids=[0]).results[0]
    y = r["out_y"]
    return (y[0:1], y[1:2], r["out_nk"].reshape(1, 1, 128, 8, 64), r["out_nv"].reshape(1, 1, 128, 8, 64),
            r["out_dk"].reshape(1, 1, 128, 4, 2, 64), r["out_dv"].reshape(1, 1, 128, 4, 128),
            r["out_st"].transpose(0, 2, 1, 3).reshape(1, 1, 2, 8, 128, 128))
```
